# Optimizing a Trainium2 kernel written in Bass

```python
import math
import jax, jax.numpy as jnp
from jax import lax
import numpy as np

D_MODEL = 1024
BATCH = 1
SEQ = 512
DEPTH = 1

CHUNK = 64
EPS = 1e-6

SSM_WIDTH = 512
SSM_GROUP = 16
SSM_GROUPS = SSM_WIDTH // SSM_GROUP
SSM_STATE = 64
DT_MIN = 1e-3
DT_MAX = 1e-1

ATT_HEADS = 8
HEAD_DIM = 128
ATT_WIDTH = ATT_HEADS * HEAD_DIM
Q_BLOCK = 128

N_BRANCHES = 2
IN_SPLITS = (
    SSM_WIDTH,
    SSM_WIDTH + ATT_WIDTH,
    SSM_WIDTH + 2 * ATT_WIDTH,
    SSM_WIDTH + 3 * ATT_WIDTH,
    SSM_WIDTH + 3 * ATT_WIDTH + ATT_HEADS,
    SSM_WIDTH + 3 * ATT_WIDTH + ATT_HEADS + D_MODEL,
)
IN_COLS = SSM_WIDTH + 3 * ATT_WIDTH + ATT_HEADS + N_BRANCHES * D_MODEL

PEER_HEADS = 8
PEER_KEYS = 128
PEER_EXPERTS = PEER_KEYS * PEER_KEYS
PEER_QUERY = 256
PEER_HALF = PEER_QUERY // 2
PEER_TOPK = 16
TOKEN_BLOCK = 128


def rms_norm(x, g):
    x32 = x.astype(jnp.float32)
    y = x32 * lax.rsqrt(jnp.mean(x32 * x32, axis=-1, keepdims=True) + EPS)
    return (y * g.astype(jnp.float32)).astype(x.dtype)

def _complex_affine_combine(earlier, later):
    ar1, ai1, br1, bi1 = earlier
    ar2, ai2, br2, bi2 = later
    return (ar2 * ar1 - ai2 * ai1,
            ar2 * ai1 + ai2 * ar1,
            ar2 * br1 - ai2 * bi1 + br2,
            ar2 * bi1 + ai2 * br1 + bi2)

def s5_branch(u, a_re, a_im, log_step, b_re, b_im, c_re, c_im, d_skip, w_glu):
    bsz, seq = u.shape[0], u.shape[1]
    f32 = jnp.float32
    u32 = u.astype(f32)
    ug = u32.reshape(bsz, seq, SSM_GROUPS, SSM_GROUP)
    step = jnp.exp(log_step.astype(f32))[:, None]
    ar = a_re.astype(f32)
    ai = a_im.astype(f32)
    mag = jnp.exp(ar * step)
    lam_re = mag * jnp.cos(ai * step)
    lam_im = mag * jnp.sin(ai * step)
    nr = lam_re - 1.0
    ni = lam_im
    den = ar * ar + ai * ai
    coef_re = (nr * ar + ni * ai) / den
    coef_im = (ni * ar - nr * ai) / den
    br = coef_re[..., None] * b_re.astype(f32) - coef_im[..., None] * b_im.astype(f32)
    bi = coef_re[..., None] * b_im.astype(f32) + coef_im[..., None] * b_re.astype(f32)
    xr = jnp.einsum('blgh,gph->blgp', ug, br)
    xi = jnp.einsum('blgh,gph->blgp', ug, bi)
    lr = jnp.broadcast_to(lam_re[None, None], (1, seq, SSM_GROUPS, SSM_STATE))
    li = jnp.broadcast_to(lam_im[None, None], (1, seq, SSM_GROUPS, SSM_STATE))
    _, _, sr, si = lax.associative_scan(_complex_affine_combine, (lr, li, xr, xi), axis=1)
    y = (jnp.einsum('blgp,ghp->blgh', sr, c_re.astype(f32))
         - jnp.einsum('blgp,ghp->blgh', si, c_im.astype(f32)))
    y = y.reshape(bsz, seq, SSM_WIDTH) + d_skip.astype(f32) * u32
    y = jax.nn.gelu(y).astype(u.dtype)
    z = y @ w_glu
    val, gate = jnp.split(z, 2, axis=-1)
    return val * jax.nn.sigmoid(gate)

def head_rms_norm(x, g):
    x32 = x.astype(jnp.float32)
    y = x32 * lax.rsqrt(jnp.mean(x32 * x32, axis=-1, keepdims=True) + EPS)
    return (y * g.astype(jnp.float32)).astype(x.dtype)

def forgetting_attention(q, k, v, f_logit, f_bias, q_g, k_g):
    bsz, seq = q.shape[0], q.shape[1]
    q = head_rms_norm(q.reshape(bsz, seq, ATT_HEADS, HEAD_DIM), q_g).transpose(0, 2, 1, 3)
    k = head_rms_norm(k.reshape(bsz, seq, ATT_HEADS, HEAD_DIM), k_g).transpose(0, 2, 1, 3)
    v = v.reshape(bsz, seq, ATT_HEADS, HEAD_DIM).transpose(0, 2, 1, 3)
    log_f = jax.nn.log_sigmoid((f_logit + f_bias).astype(jnp.float32)).transpose(0, 2, 1)
    cum = jnp.cumsum(log_f, axis=-1)
    n_blk = seq // Q_BLOCK
    q_blocks = q.reshape(bsz, ATT_HEADS, n_blk, Q_BLOCK, HEAD_DIM).transpose(2, 0, 1, 3, 4)
    c_blocks = cum.reshape(bsz, ATT_HEADS, n_blk, Q_BLOCK).transpose(2, 0, 1, 3)
    key_pos = jnp.arange(seq)
    scale = HEAD_DIM ** -0.5

    def one_block(args):
        blk, q_blk, c_blk = args
        s = jnp.einsum('bhqd,bhkd->bhqk', q_blk, k).astype(jnp.float32) * scale
        s = s + c_blk[..., None] - cum[:, :, None, :]
        q_pos = blk * Q_BLOCK + jnp.arange(Q_BLOCK)
        s = jnp.where(key_pos[None, :] <= q_pos[:, None], s, -jnp.inf)
        p = jax.nn.softmax(s, axis=-1)
        return jnp.einsum('bhqk,bhkd->bhqd', p.astype(v.dtype), v)

    o = lax.map(one_block, (jnp.arange(n_blk), q_blocks, c_blocks))
    return o.transpose(1, 0, 3, 2, 4).reshape(bsz, seq, ATT_WIDTH)

def peer_ffn(h, w_query, sub_keys, u_tab, v_tab):
    bsz, seq, d = h.shape
    q = (h @ w_query).reshape(bsz, seq, PEER_HEADS, 2, PEER_HALF).astype(jnp.float32)
    scores = jnp.einsum('blhcd,hckd->blhck', q, sub_keys.astype(jnp.float32))
    s_top, i_top = lax.top_k(scores, PEER_TOPK)
    cand_s = (s_top[..., 0, :, None] + s_top[..., 1, None, :]).reshape(bsz, seq, PEER_HEADS, PEER_TOPK * PEER_TOPK)
    cand_i = (i_top[..., 0, :, None] * PEER_KEYS + i_top[..., 1, None, :]).reshape(bsz, seq, PEER_HEADS, PEER_TOPK * PEER_TOPK)
    best_s, pos = lax.top_k(cand_s, PEER_TOPK)
    expert_idx = jnp.take_along_axis(cand_i, pos, axis=-1)
    gates = jax.nn.softmax(best_s, axis=-1)
    n_tok = bsz * seq
    n_tb = n_tok // TOKEN_BLOCK
    h_blocks = h.reshape(n_tb, TOKEN_BLOCK, d)
    i_blocks = expert_idx.reshape(n_tb, TOKEN_BLOCK, PEER_HEADS, PEER_TOPK)
    g_blocks = gates.reshape(n_tb, TOKEN_BLOCK, PEER_HEADS, PEER_TOPK)

    def one_block(args):
        h_blk, i_blk, g_blk = args
        u_sel = u_tab[i_blk]
        act = jax.nn.gelu(jnp.einsum('td,thkd->thk', h_blk, u_sel).astype(jnp.float32))
        w = (g_blk * act).astype(h.dtype)
        return jnp.einsum('thk,thkd->td', w, v_tab[i_blk])

    out = lax.map(one_block, (h_blocks, i_blocks, g_blocks))
    return out.reshape(bsz, seq, d)

def first_inputs(seed: int = 0) -> dict:
    key = jax.random.key(seed)
    ks = jax.random.split(key, 21)
    f32 = jnp.float32
    nrm = lambda k, shape: jax.random.normal(k, shape, dtype=f32)
    x = nrm(ks[0], (BATCH, SEQ, D_MODEL))
    mix_norm_g = 1.0 + 0.02 * nrm(ks[1], (DEPTH, D_MODEL))
    w_in = nrm(ks[2], (DEPTH, D_MODEL, IN_COLS)) * D_MODEL ** -0.5
    ssm_a_re = -0.5 + 0.01 * nrm(ks[3], (DEPTH, SSM_GROUPS, SSM_STATE))
    ssm_a_im = math.pi * jnp.arange(SSM_STATE, dtype=f32) + 0.01 * nrm(ks[4], (DEPTH, SSM_GROUPS, SSM_STATE))
    ssm_log_step = jax.random.uniform(ks[5], (DEPTH, SSM_GROUPS), dtype=f32, minval=math.log(DT_MIN), maxval=math.log(DT_MAX))
    ssm_b_re = nrm(ks[6], (DEPTH, SSM_GROUPS, SSM_STATE, SSM_GROUP)) * (2.0 * SSM_GROUP) ** -0.5
    ssm_b_im = nrm(ks[7], (DEPTH, SSM_GROUPS, SSM_STATE, SSM_GROUP)) * (2.0 * SSM_GROUP) ** -0.5
    ssm_c_re = nrm(ks[8], (DEPTH, SSM_GROUPS, SSM_GROUP, SSM_STATE)) * (2.0 * SSM_STATE) ** -0.5
    ssm_c_im = nrm(ks[9], (DEPTH, SSM_GROUPS, SSM_GROUP, SSM_STATE)) * (2.0 * SSM_STATE) ** -0.5
    ssm_d = nrm(ks[10], (DEPTH, SSM_WIDTH))
    ssm_w_glu = nrm(ks[11], (DEPTH, SSM_WIDTH, 2 * D_MODEL)) * SSM_WIDTH ** -0.5
    fox_forget_bias = 2.0 + 0.5 * nrm(ks[12], (DEPTH, ATT_HEADS))
    q_norm_g = 1.0 + 0.02 * nrm(ks[13], (DEPTH, HEAD_DIM))
    k_norm_g = 1.0 + 0.02 * nrm(ks[14], (DEPTH, HEAD_DIM))
    w_out = nrm(ks[15], (DEPTH, D_MODEL, D_MODEL)) * D_MODEL ** -0.5
    ffn_norm_g = 1.0 + 0.02 * nrm(ks[16], (DEPTH, D_MODEL))
    peer_w_query = nrm(ks[17], (DEPTH, D_MODEL, PEER_HEADS * PEER_QUERY)) * D_MODEL ** -0.5
    peer_sub_keys = nrm(ks[18], (DEPTH, PEER_HEADS, 2, PEER_KEYS, PEER_HALF)) * PEER_HALF ** -0.5
    peer_u = nrm(ks[19], (DEPTH, PEER_EXPERTS, D_MODEL)) * D_MODEL ** -0.5
    peer_v = nrm(ks[20], (DEPTH, PEER_EXPERTS, D_MODEL)) * 0.1
    return {"x": x, "mix_norm_g": mix_norm_g, "w_in": w_in,
            "ssm_a_re": ssm_a_re, "ssm_a_im": ssm_a_im, "ssm_log_step": ssm_log_step,
            "ssm_b_re": ssm_b_re, "ssm_b_im": ssm_b_im, "ssm_c_re": ssm_c_re, "ssm_c_im": ssm_c_im,
            "ssm_d": ssm_d, "ssm_w_glu": ssm_w_glu, "fox_forget_bias": fox_forget_bias,
            "q_norm_g": q_norm_g, "k_norm_g": k_norm_g, "w_out": w_out, "ffn_norm_g": ffn_norm_g,
            "peer_w_query": peer_w_query, "peer_sub_keys": peer_sub_keys,
            "peer_u": peer_u, "peer_v": peer_v}

def first_block(x, mix_norm_g, w_in, ssm_a_re, ssm_a_im, ssm_log_step, ssm_b_re, ssm_b_im,
              ssm_c_re, ssm_c_im, ssm_d, ssm_w_glu, fox_forget_bias, q_norm_g, k_norm_g,
              w_out, ffn_norm_g, peer_w_query, peer_sub_keys, peer_u, peer_v):
    for layer in range(DEPTH):
        h = rms_norm(x, mix_norm_g[layer])
        proj = h @ w_in[layer]
        u, q, k, v, f_logit, g_ssm, g_att = jnp.split(proj, IN_SPLITS, axis=-1)
        y_ssm = s5_branch(u, ssm_a_re[layer], ssm_a_im[layer], ssm_log_step[layer],
                          ssm_b_re[layer], ssm_b_im[layer], ssm_c_re[layer], ssm_c_im[layer],
                          ssm_d[layer], ssm_w_glu[layer])
        y_att = forgetting_attention(q, k, v, f_logit, fox_forget_bias[layer],
                                     q_norm_g[layer], k_norm_g[layer])
        merged = jax.nn.sigmoid(g_ssm) * y_ssm + jax.nn.sigmoid(g_att) * y_att
        x = x + (merged @ w_out[layer]).astype(x.dtype)
        h2 = rms_norm(x, ffn_norm_g[layer])
        x = x + peer_ffn(h2, peer_w_query[layer], peer_sub_keys[layer],
                         peer_u[layer], peer_v[layer]).astype(x.dtype)
    return x


DEPTH_2 = 2

ROPE_THETA = 10000.0
NORM_EPS = 1e-6

A_HEADS = 8
A_NOPE = 64
A_ROPE = 32
A_KV_RANK = 128
A_V_DIM = 64
A_SCALE = (A_NOPE + A_ROPE) ** -0.5
IDX_HEADS = 8
IDX_DIM = 64
TOPK_MAX = 256

B_HEADS = 4
B_QK_DIM = 64
B_V_DIM = 2 * B_QK_DIM

C_HEADS = 16
C_GROUPS = 4
C_HPG = C_HEADS // C_GROUPS
C_DIM = 64
CMP_LEN = 32
CMP_STRIDE = 16
CMP_HIDDEN = 128
SEL_BLOCK = 64
SEL_TOPN = 16
WINDOW = 512
C_Q_BLOCK = 16

D_FF = -(-8 * D_MODEL // (3 * 256)) * 256

EVEN_SPLITS = [A_HEADS * A_NOPE, A_HEADS * A_ROPE, A_KV_RANK, A_ROPE, IDX_HEADS * IDX_DIM, IDX_DIM, IDX_HEADS,
               B_HEADS * 2 * B_QK_DIM, B_HEADS * 2 * B_QK_DIM, B_HEADS * B_V_DIM]
EVEN_IN = sum(EVEN_SPLITS)
ODD_SPLITS = [C_HEADS * C_DIM] + [C_GROUPS * C_DIM] * 6 + [C_HEADS * 3]
ODD_IN = sum(ODD_SPLITS)


def rmsnorm(x, g):
    xf = x.astype(jnp.float32)
    y = xf * lax.rsqrt(jnp.mean(xf * xf, axis=-1, keepdims=True) + NORM_EPS)
    return (y * g.astype(jnp.float32)).astype(x.dtype)

def rope(x, pos):
    d = x.shape[-1]
    inv = ROPE_THETA ** (-jnp.arange(0, d, 2, dtype=jnp.float32) / d)
    ang = pos.astype(jnp.float32)[:, None] * inv[None, :]
    shape = (x.shape[1],) + (1,) * (x.ndim - 3) + (d // 2,)
    cos = jnp.cos(ang).reshape(shape)
    sin = jnp.sin(ang).reshape(shape)
    xf = x.astype(jnp.float32)
    x1, x2 = xf[..., :d // 2], xf[..., d // 2:]
    return jnp.concatenate([x1 * cos - x2 * sin, x2 * cos + x1 * sin], axis=-1).astype(x.dtype)

def safe_softmax(s, mask):
    s = jnp.where(mask, s, -jnp.inf)
    m = jnp.max(s, axis=-1, keepdims=True)
    m = jnp.where(jnp.isfinite(m), m, 0.0)
    e = jnp.exp(s - m)
    den = jnp.sum(e, axis=-1, keepdims=True)
    return e / jnp.where(den > 0, den, 1.0)

def split_cols(y, sizes):
    return jnp.split(y, np.cumsum(sizes)[:-1].tolist(), axis=-1)

def qslice(a, i, qb):
    return lax.dynamic_slice_in_dim(a, i * qb, qb, axis=1)

def map_blocks(fn, n_blocks):
    out = lax.map(fn, jnp.arange(n_blocks, dtype=jnp.int32))
    nb, b, qb = out.shape[:3]
    return jnp.moveaxis(out, 0, 1).reshape((b, nb * qb) + out.shape[3:])

def dsa_mixer(q_nope, q_rope, c_kv, k_rope, iq, ik, iw, kv_gain, w_uk, w_uv, pos):
    B, T = c_kv.shape[:2]
    q_nope = q_nope.reshape(B, T, A_HEADS, A_NOPE)
    q_rope = rope(q_rope.reshape(B, T, A_HEADS, A_ROPE), pos)
    c_kv = rmsnorm(c_kv, kv_gain)
    k_rope = rope(k_rope, pos)
    q_lat = jnp.einsum('bthd,hdc->bthc', q_nope, w_uk)
    qc = jnp.concatenate([q_lat, q_rope], axis=-1)
    kc = jnp.concatenate([c_kv, k_rope], axis=-1)
    iq = rope(iq.reshape(B, T, IDX_HEADS, IDX_DIM), pos)
    ik = rope(ik, pos)
    iw = iw * IDX_HEADS ** -0.5
    k_sel = min(TOPK_MAX, T // 4)

    def block(i):
        t = i * Q_BLOCK + jnp.arange(Q_BLOCK, dtype=jnp.int32)
        rel = jax.nn.relu(jnp.einsum('bqhd,bsd->bqhs', qslice(iq, i, Q_BLOCK), ik).astype(jnp.float32) * IDX_DIM ** -0.5)
        score = jnp.einsum('bqhs,bqh->bqs', rel, qslice(iw, i, Q_BLOCK).astype(jnp.float32))
        causal = pos[None, :] <= t[:, None]
        score = jnp.where(causal[None], score, -jnp.inf)
        _, idx = lax.top_k(score, k_sel)
        kg = jax.vmap(lambda k, j: k[j])(kc, idx)
        s = jnp.einsum('bqhc,bqkc->bqhk', qslice(qc, i, Q_BLOCK), kg).astype(jnp.float32) * A_SCALE
        valid = (idx <= t[None, :, None])[:, :, None, :]
        p = safe_softmax(s, valid)
        return jnp.einsum('bqhk,bqkc->bqhc', p.astype(kg.dtype), kg[..., :A_KV_RANK])

    o_lat = map_blocks(block, T // Q_BLOCK)
    o = jnp.einsum('bthc,hcd->bthd', o_lat, w_uv)
    return o.reshape(B, T, A_HEADS * A_V_DIM)

def diff_mixer(q, k, v, lam, subln_gain, lam_init, pos):
    B, T = q.shape[:2]
    q = rope(q.reshape(B, T, B_HEADS * 2, B_QK_DIM), pos).reshape(B, T, B_HEADS, 2, B_QK_DIM)
    k = rope(k.reshape(B, T, B_HEADS * 2, B_QK_DIM), pos).reshape(B, T, B_HEADS, 2, B_QK_DIM)
    v = v.reshape(B, T, B_HEADS, B_V_DIM)
    lf = lam.astype(jnp.float32)
    lam_full = jnp.exp(jnp.sum(lf[0] * lf[1])) - jnp.exp(jnp.sum(lf[2] * lf[3])) + lam_init

    def block(i):
        t = i * Q_BLOCK + jnp.arange(Q_BLOCK, dtype=jnp.int32)
        s = jnp.einsum('bqhmd,bshmd->bhmqs', qslice(q, i, Q_BLOCK), k).astype(jnp.float32) * B_QK_DIM ** -0.5
        causal = pos[None, :] <= t[:, None]
        p = safe_softmax(s, causal)
        a = p[:, :, 0] - lam_full * p[:, :, 1]
        return jnp.einsum('bhqs,bshe->bqhe', a.astype(v.dtype), v)

    o = map_blocks(block, T // Q_BLOCK)
    o = rmsnorm(o, subln_gain) * (1.0 - lam_init)
    return o.reshape(B, T, B_HEADS * B_V_DIM)

def compress(x, pe, w1, w2):
    B, T, G, d = x.shape
    chunks = x.reshape(B, T // CMP_STRIDE, CMP_STRIDE, G, d)
    blocks = jnp.concatenate([chunks[:, :-1], chunks[:, 1:]], axis=2) + pe[None, None, :, None, :]
    flat = blocks.transpose(0, 1, 3, 2, 4).reshape(B, -1, G, CMP_LEN * d)
    return jnp.einsum('bngf,fe->bnge', jax.nn.gelu(flat @ w1), w2)

def nsa_mixer(q, kc_raw, vc_raw, ks, vs, kw, vw, gates, pe, w1, w2, pos):
    B, T = q.shape[:2]
    kv = lambda a: a.reshape(B, T, C_GROUPS, C_DIM)
    q = rope(q.reshape(B, T, C_HEADS, C_DIM), pos).reshape(B, T, C_GROUPS, C_HPG, C_DIM)
    k_cmp = compress(rope(kv(kc_raw), pos), pe[0], w1[0], w2[0])
    v_cmp = compress(kv(vc_raw), pe[1], w1[1], w2[1])
    k_slc, v_slc = rope(kv(ks), pos), kv(vs)
    k_win, v_win = rope(kv(kw), pos), kv(vw)
    gates = jax.nn.sigmoid(gates.astype(jnp.float32)).reshape(B, T, C_GROUPS, C_HPG, 3).astype(q.dtype)
    n_cmp = T // CMP_STRIDE - 1
    n_blk = T // SEL_BLOCK
    top_n = min(SEL_TOPN, n_blk)
    cmp_end = jnp.arange(n_cmp, dtype=jnp.int32) * CMP_STRIDE + CMP_LEN - 1
    cs = np.arange(n_cmp) * CMP_STRIDE
    ss = np.arange(n_blk) * SEL_BLOCK
    overlap = jnp.asarray(((cs[:, None] < ss[None, :] + SEL_BLOCK) & (cs[:, None] + CMP_LEN > ss[None, :])).astype(np.float32))
    k_blocks = k_slc.reshape(B, n_blk, SEL_BLOCK, C_GROUPS, C_DIM).transpose(0, 3, 1, 2, 4)
    v_blocks = v_slc.reshape(B, n_blk, SEL_BLOCK, C_GROUPS, C_DIM).transpose(0, 3, 1, 2, 4)
    k_pad = jnp.pad(k_win, ((0, 0), (WINDOW, 0), (0, 0), (0, 0)))
    v_pad = jnp.pad(v_win, ((0, 0), (WINDOW, 0), (0, 0), (0, 0)))
    blk_ids = jnp.arange(n_blk, dtype=jnp.int32)
    scale = C_DIM ** -0.5
    gather = jax.vmap(jax.vmap(lambda a, j: a[j]))

    def block(i):
        t = i * C_Q_BLOCK + jnp.arange(C_Q_BLOCK, dtype=jnp.int32)
        qb = qslice(q, i, C_Q_BLOCK)
        s = jnp.einsum('bqghd,bngd->bqghn', qb, k_cmp).astype(jnp.float32) * scale
        p_cmp = safe_softmax(s, (cmp_end[None, :] <= t[:, None])[:, None, None, :])
        o_cmp = jnp.einsum('bqghn,bngd->bqghd', p_cmp.astype(v_cmp.dtype), v_cmp)
        imp = jnp.einsum('bqghn,nj->bqgj', p_cmp, overlap)
        cur = t // SEL_BLOCK
        forced = (blk_ids[None, :] == 0) | (blk_ids[None, :] == cur[:, None]) | (blk_ids[None, :] == cur[:, None] - 1)
        admissible = blk_ids[None, :] * SEL_BLOCK <= t[:, None]
        imp = jnp.where(forced[:, None, :], jnp.inf, imp)
        imp = jnp.where(admissible[:, None, :], imp, -jnp.inf)
        _, sel = lax.top_k(imp, top_n)
        sel = sel.transpose(0, 2, 1, 3)
        kg = gather(k_blocks, sel)
        vg = gather(v_blocks, sel)
        s = jnp.einsum('bqghd,bgqnld->bqghnl', qb, kg).astype(jnp.float32) * scale
        tok = sel[..., None] * SEL_BLOCK + jnp.arange(SEL_BLOCK, dtype=jnp.int32)
        m_slc = (tok <= t[None, None, :, None, None]).transpose(0, 2, 1, 3, 4)
        m_slc = m_slc.reshape(B, C_Q_BLOCK, C_GROUPS, 1, top_n * SEL_BLOCK)
        p = safe_softmax(s.reshape(B, C_Q_BLOCK, C_GROUPS, C_HPG, top_n * SEL_BLOCK), m_slc)
        p = p.reshape(B, C_Q_BLOCK, C_GROUPS, C_HPG, top_n, SEL_BLOCK)
        o_slc = jnp.einsum('bqghnl,bgqnld->bqghd', p.astype(vg.dtype), vg)
        kwb = lax.dynamic_slice_in_dim(k_pad, i * C_Q_BLOCK, WINDOW + C_Q_BLOCK, axis=1)
        vwb = lax.dynamic_slice_in_dim(v_pad, i * C_Q_BLOCK, WINDOW + C_Q_BLOCK, axis=1)
        kpos = i * C_Q_BLOCK - WINDOW + jnp.arange(WINDOW + C_Q_BLOCK, dtype=jnp.int32)
        dist = t[:, None] - kpos[None, :]
        m_win = ((dist >= 0) & (dist < WINDOW) & (kpos[None, :] >= 0))[:, None, None, :]
        s = jnp.einsum('bqghd,bsgd->bqghs', qb, kwb).astype(jnp.float32) * scale
        p = safe_softmax(s, m_win)
        o_win = jnp.einsum('bqghs,bsgd->bqghd', p.astype(vwb.dtype), vwb)
        g = qslice(gates, i, C_Q_BLOCK)
        return g[..., 0:1] * o_cmp + g[..., 1:2] * o_slc + g[..., 2:3] * o_win

    o = map_blocks(block, T // C_Q_BLOCK)
    return o.reshape(B, T, C_HEADS * C_DIM)

def swiglu(h, w_gate, w_up, w_down):
    return (jax.nn.silu(h @ w_gate) * (h @ w_up)) @ w_down

def _w(key, shape, fan_in, gain=1.0):
    return jax.random.normal(key, shape, jnp.float32) * (gain * fan_in ** -0.5)

def _gain(key, shape):
    return 1.0 + 0.02 * jax.random.normal(key, shape, jnp.float32)

def second_inputs(seed: int = 0) -> dict:
    key = jax.random.key(seed)
    k = jax.random.split(key, 19)
    n_even = (DEPTH_2 + 1) // 2
    n_odd = DEPTH_2 // 2
    out_gain = (2 * DEPTH_2) ** -0.5
    return {
        'x': jax.random.normal(k[0], (BATCH, SEQ, D_MODEL), jnp.float32),
        'norm_mix': _gain(k[1], (DEPTH_2, D_MODEL)),
        'norm_ffn': _gain(k[2], (DEPTH_2, D_MODEL)),
        'norm_final': _gain(k[3], (D_MODEL,)),
        'ev_w_in': _w(k[4], (n_even, D_MODEL, EVEN_IN), D_MODEL),
        'ev_kv_gain': _gain(k[5], (n_even, A_KV_RANK)),
        'ev_w_uk': _w(k[6], (n_even, A_HEADS, A_NOPE, A_KV_RANK), A_KV_RANK),
        'ev_w_uv': _w(k[7], (n_even, A_HEADS, A_KV_RANK, A_V_DIM), A_KV_RANK),
        'ev_lambda': 0.1 * jax.random.normal(k[8], (n_even, 4, B_QK_DIM), jnp.float32),
        'ev_subln': _gain(k[9], (n_even, B_V_DIM)),
        'ev_w_out': _w(k[10], (n_even, D_MODEL, D_MODEL), D_MODEL, out_gain),
        'od_w_in': _w(k[11], (n_odd, D_MODEL, ODD_IN), D_MODEL),
        'od_cmp_pe': 0.1 * jax.random.normal(k[12], (n_odd, 2, CMP_LEN, C_DIM), jnp.float32),
        'od_cmp_w1': _w(k[13], (n_odd, 2, CMP_LEN * C_DIM, CMP_HIDDEN), CMP_LEN * C_DIM),
        'od_cmp_w2': _w(k[14], (n_odd, 2, CMP_HIDDEN, C_DIM), CMP_HIDDEN),
        'od_w_out': _w(k[15], (n_odd, D_MODEL, D_MODEL), D_MODEL, out_gain),
        'ffn_w_gate': _w(k[16], (DEPTH_2, D_MODEL, D_FF), D_MODEL),
        'ffn_w_up': _w(k[17], (DEPTH_2, D_MODEL, D_FF), D_MODEL),
        'ffn_w_down': _w(k[18], (DEPTH_2, D_FF, D_MODEL), D_FF, out_gain),
    }

def second_block(x, norm_mix, norm_ffn, norm_final,
              ev_w_in, ev_kv_gain, ev_w_uk, ev_w_uv, ev_lambda, ev_subln, ev_w_out,
              od_w_in, od_cmp_pe, od_cmp_w1, od_cmp_w2, od_w_out,
              ffn_w_gate, ffn_w_up, ffn_w_down):
    pos = jnp.arange(x.shape[1], dtype=jnp.int32)
    for layer in range(DEPTH_2):
        j = layer // 2
        h = rmsnorm(x, norm_mix[layer])
        if layer % 2 == 0:
            y = h @ ev_w_in[j]
            qa_nope, qa_rope, c_kv, ka_rope, iq, ik, iw, qb, kb, vb = split_cols(y, EVEN_SPLITS)
            o_a = dsa_mixer(qa_nope, qa_rope, c_kv, ka_rope, iq, ik, iw, ev_kv_gain[j], ev_w_uk[j], ev_w_uv[j], pos)
            lam_init = 0.8 - 0.6 * math.exp(-0.3 * layer)
            o_b = diff_mixer(qb, kb, vb, ev_lambda[j], ev_subln[j], lam_init, pos)
            mix = jnp.concatenate([o_a, o_b], axis=-1) @ ev_w_out[j]
        else:
            y = h @ od_w_in[j]
            qc, kc_raw, vc_raw, ks, vs, kw, vw, gc = split_cols(y, ODD_SPLITS)
            o_c = nsa_mixer(qc, kc_raw, vc_raw, ks, vs, kw, vw, gc, od_cmp_pe[j], od_cmp_w1[j], od_cmp_w2[j], pos)
            mix = o_c @ od_w_out[j]
        x = x + mix
        x = x + swiglu(rmsnorm(x, norm_ffn[layer]), ffn_w_gate[layer], ffn_w_up[layer], ffn_w_down[layer])
    return rmsnorm(x, norm_final)


def setup_inputs(seed=0):
    out = dict(first_inputs(seed))
    for name, value in second_inputs(seed + 1).items():
        if name != "x":
            out[name + "_2"] = value
    return out


def reference(
    x, mix_norm_g, w_in, ssm_a_re, ssm_a_im, ssm_log_step, ssm_b_re, ssm_b_im, ssm_c_re,
    ssm_c_im, ssm_d, ssm_w_glu, fox_forget_bias, q_norm_g, k_norm_g, w_out, ffn_norm_g,
    peer_w_query, peer_sub_keys, peer_u, peer_v, norm_mix_2, norm_ffn_2, norm_final_2,
    ev_w_in_2, ev_kv_gain_2, ev_w_uk_2, ev_w_uv_2, ev_lambda_2, ev_subln_2, ev_w_out_2,
    od_w_in_2, od_cmp_pe_2, od_cmp_w1_2, od_cmp_w2_2, od_w_out_2, ffn_w_gate_2, ffn_w_up_2,
    ffn_w_down_2,
):
    x = first_block(
        x, mix_norm_g, w_in, ssm_a_re, ssm_a_im, ssm_log_step, ssm_b_re, ssm_b_im, ssm_c_re,
        ssm_c_im, ssm_d, ssm_w_glu, fox_forget_bias, q_norm_g, k_norm_g, w_out, ffn_norm_g,
        peer_w_query, peer_sub_keys, peer_u, peer_v,
    )
    return second_block(
        x, norm_mix_2, norm_ffn_2, norm_final_2, ev_w_in_2, ev_kv_gain_2, ev_w_uk_2, ev_w_uv_2,
        ev_lambda_2, ev_subln_2, ev_w_out_2, od_w_in_2, od_cmp_pe_2, od_cmp_w1_2, od_cmp_w2_2,
        od_w_out_2, ffn_w_gate_2, ffn_w_up_2, ffn_w_down_2,
    )


_drawn_inputs = setup_inputs


def setup_inputs(seed=0):
    import zlib

    import numpy as np

    out = dict(_drawn_inputs(seed))
    spreads = {}
    factors = {'mix_norm_g': 4.815,
     'ssm_a_re': 64.0,
     'ssm_a_im': 3.64,
     'ssm_log_step': 3.778,
     'ssm_b_re': 4.8,
     'ssm_b_im': 4.864,
     'ssm_c_re': 4.852,
     'ssm_c_im': 4.911,
     'q_norm_g': 8.0,
     'k_norm_g': 8.0,
     'ffn_norm_g': 6.378,
     'norm_mix_2': 4.899,
     'norm_ffn_2': 5.333,
     'norm_final_2': 8.112,
     'ev_kv_gain_2': 8.0,
     'ev_lambda_2': 4.304,
     'ev_subln_2': 22.32,
     'od_cmp_pe_2': 12.622}
    for name, (base, spread) in spreads.items():
        noise = np.random.default_rng([zlib.crc32(name.encode()), seed]).standard_normal(out[name].shape)
        drawn = base * np.exp(spread * noise) if base else spread * noise
        out[name] = __import__('jax').numpy.asarray(drawn.astype(out[name].dtype))
    for name, factor in factors.items():
        out[name] = (out[name] * factor).astype(out[name].dtype)
    return out
```

```python
import math
from contextlib import ExitStack

import numpy as np
import concourse.bass as bass
from concourse import mybir

F32 = mybir.dt.float32
U32 = mybir.dt.uint32
ALU = mybir.AluOpType
ACT = mybir.ActivationFunctionType
AX = mybir.AxisListType

P = 128
T = 512
TT = T // P
D = 1024
KD = D // P
EPS = 1e-6
NEG = -1.0e30
LOWEST = -3.0e38

SSM_W, SSM_H, SSM_G, SSM_S = 512, 16, 32, 64
PAIRS = SSM_G // 2
SSM_T = SSM_W // P
FOX_H = 8
PEER_H, PEER_K, TOPK = 8, 128, 16
SLOTS = PEER_H * TOPK

DSA_H, DSA_SEL = 8, T // 4
DIFF_H = 4
NSA_G, NSA_HPG, NSA_D = 4, 4, 64
NSA_H = NSA_G * NSA_HPG
CMP_LEN, CMP_STRIDE = 32, 16
CMP_N = T // CMP_STRIDE - 1
D_FF = 2816
KF = D_FF // P

W_SLOTS = 4
W_SLOT = KD * P


class Tally:

    def __init__(self, sem):
        self.sem = sem
        self.n = 0

    def inc(self, ins, by=1):
        ins.then_inc(self.sem, by)
        self.n += by
        return self.n


def hold(eng, sem, value, tick):
    eng.wait_ge(sem, value)
    eng.sem_inc(tick, 1)


class Chain:

    def __init__(self, eng, tally, turn=None, per=0, tick=None):
        self.eng, self.tally, self.turn, self.per, self.tick = eng, tally, turn, per, tick
        self.base = tally.n
        self.k = 0

    def __call__(self, ins):
        self.k += 1
        ins.then_inc(self.tally.sem, 1)
        if self.turn is None:
            self.tally.n += 1
        self.wait()

    def mark(self, ins):
        self.k += 1
        ins.then_inc(self.tally.sem, 1)
        if self.turn is None:
            self.tally.n += 1

    def wait(self):
        if self.turn is None:
            self.eng.wait_ge(self.tally.sem, self.tally.n)
        elif self.tick is None:
            self.eng.wait_ge(self.tally.sem, self.turn * self.per + (self.base + self.k))
        else:
            hold(self.eng, self.tally.sem, self.turn * self.per + (self.base + self.k), self.tick)

    def ends(self, turns):
        assert self.k == self.per, (self.k, self.per)
        self.tally.n += turns * self.per


class Core:

    def __init__(self, nc, ctx, ins):
        self.nc, self.ctx, self.ins = nc, ctx, ins
        self.names = 0
        self.xT = self.sbuf(ctx, "xT", [P, KD, T])
        self.hT = self.sbuf(ctx, "hT", [P, KD, T])
        self.w_ring = self.sbuf(ctx, "w_ring", [P, W_SLOTS, W_SLOT])
        self.ident = self.sbuf(ctx, "ident", [P, P])
        self.ones = self.sbuf(ctx, "ones", [P, P])
        self.causal = self.sbuf(ctx, "causal", [P, P])
        self.ps = ctx.enter_context(nc.psum_tensor("ps", [P, 8, T], F32))
        self.w_in = [Tally(self.sem(f"w_in{b}")) for b in range(W_SLOTS)]
        self.act_step = Tally(self.sem("act_step"))
        self.dve_step = Tally(self.sem("dve_step"))
        self.dve_tick, self.pool_tick = self.sem("dve_tick"), self.sem("pool_tick")

    def sbuf(self, ctx, name, shape, dt=F32):
        self.names += 1
        return ctx.enter_context(self.nc.sbuf_tensor(f"{name}_{self.names}", shape, dt))

    def sem(self, name):
        self.names += 1
        return self.nc.alloc_semaphore(f"{name}_{self.names}")

    def stage(self):
        return Stage(self)


class Stage:

    def __init__(self, core):
        self.core = core
        self.memory = ExitStack()
        self.sems = []

    def __enter__(self):
        return self

    def __exit__(self, *failed):
        if not any(failed) and self.sems:
            self.core.nc.clear_and_free_semaphores(self.sems)
            self.core.nc.all_engine_barrier(sem_only=True)
        self.memory.close()

    def sbuf(self, name, shape, dt=F32):
        return self.core.sbuf(self.memory, name, shape, dt)

    def sem(self, name):
        self.sems.append(self.core.sem(name))
        return self.sems[-1]


def load_consts(c):
    nc = c.nc
    with c.stage() as ctx:
        x_rows = ctx.sbuf("x_rows", [P, TT, D])
        consts_in, x_in = ctx.sem("consts_in"), ctx.sem("x_in")
        ones_set, transposed, copied = ctx.sem("ones_set"), ctx.sem("transposed"), ctx.sem("copied")
        with nc.Block() as block:

            @block.sync
            def _(sp):
                sp.dma_start(c.ident[:, :], c.ins["c_ident"]).then_inc(consts_in, 16)
                sp.dma_start(c.causal[:, :], c.ins["c_causal"]).then_inc(consts_in, 16)
                sp.dma_start(x_rows[:, :, :], c.ins["x"][0].rearrange("(t p) d -> p t d", p=P)).then_inc(x_in, 16)

            @block.gpsimd
            def _(pool):

                nc.gpsimd.memset(c.ones[:, :], 1.0).then_inc(ones_set, 1)
                pool.wait_ge(consts_in, 32)
                pool.wait_ge(ones_set, 1)

            @block.tensor
            def _(pe):
                pe.wait_ge(consts_in, 32)
                pe.wait_ge(x_in, 16)
                for k in range(KD):
                    for t in range(TT):
                        tr = nc.tensor.transpose(c.ps[:, k, t * P:(t + 1) * P], x_rows[:, t, k * P:(k + 1) * P], c.ident[:, :])
                    tr.then_inc(transposed, 1)

            @block.scalar
            def _(act):
                for k in range(KD):
                    act.wait_ge(transposed, k + 1)
                    nc.scalar.activation(c.xT[:, k, :], c.ps[:, k, :], ACT.Copy).then_inc(copied, 1)
                act.wait_ge(copied, KD)


def rms_norm(c, gain):
    nc = c.nc
    with c.stage() as ctx:
        gains = ctx.sbuf("gains", [P, KD])
        squares = ctx.sbuf("squares", [P, KD, T])
        rstd = ctx.sbuf("rstd", [P, T])
        gain_in, squared, summed = ctx.sem("gain_in"), ctx.sem("squared"), ctx.sem("summed")
        inverted, rooted, normed = ctx.sem("inverted"), ctx.sem("rooted"), ctx.sem("normed")
        with nc.Block() as block:

            @block.sync
            def _(sp):
                sp.dma_start(gains[:, :], gain.rearrange("(k p) -> p k", p=P), allow_slow_non_contiguous=True).then_inc(gain_in, 16)

            @block.scalar
            def _(act):
                for k in range(KD):
                    nc.scalar.activation(squares[:, k, :], c.xT[:, k, :], ACT.Square).then_inc(squared, 1)
                act.wait_ge(inverted, 1)
                nc.scalar.activation(rstd[:, :], rstd[:, :], ACT.Sqrt).then_inc(rooted, 1)

            @block.tensor
            def _(pe):
                for k in range(KD):
                    pe.wait_ge(squared, k + 1)
                    mm = nc.tensor.matmul(c.ps[:, 0, :], c.ones[:, :], squares[:, k, :], start=(k == 0), stop=(k == KD - 1))
                mm.then_inc(summed, 1)

            @block.vector
            def _(dve):
                step = Chain(dve, c.dve_step)
                dve.wait_ge(summed, 1)
                step(nc.vector.tensor_scalar(rstd[:, :], c.ps[:, 0, :], 1.0 / D, EPS, ALU.mult, ALU.add))
                nc.vector.reciprocal(rstd[:, :], rstd[:, :]).then_inc(inverted, 1)
                dve.wait_ge(gain_in, 16)
                dve.wait_ge(rooted, 1)
                for k in range(KD):
                    nc.vector.scalar_tensor_tensor(c.hT[:, k, :], c.xT[:, k, :], gains[:, k:k + 1], rstd[:, :], ALU.mult, ALU.mult).then_inc(normed, 1)
                dve.wait_ge(normed, KD)


def project(c, turns, per_turn, source, evacuate, kt=KD, rhs=None, ring=None):
    nc = c.nc
    rhs = c.hT if rhs is None else rhs
    ring = c.w_ring if ring is None else ring
    ctx = c.stage()
    mm_done, bank_free = ctx.sem("mm_done"), ctx.sem("bank_free")
    pieces = len(source(0, 0))
    w_base = [c.w_in[b].n for b in range(per_turn)]

    def w_slot(b):
        return ring[:, b, 0:kt * P].rearrange("p (k n) -> p k n", n=P)

    def ready(i, b):
        return i * per_turn + (per_turn + b + 1)

    def freed(i, b):
        return i * per_turn + (b + 1)

    def turn_loop(eng, body):
        if turns == 1:
            body(0)
        else:
            with eng.Fori(0, turns) as i:
                body(i)

    with nc.Block() as block:

        @block.sync
        def _(sp):
            def body(i):
                for b in range(per_turn):
                    sp.wait_ge(mm_done, freed(i, b))
                    for place, view in source(i, b):
                        sp.dma_start(w_slot(b)[place], view).then_inc(c.w_in[b].sem, 16)
            turn_loop(sp, body)

        @block.tensor
        def _(pe):
            pe.sem_inc(mm_done, per_turn)
            pe.sem_inc(bank_free, per_turn)

            def body(i):
                for b in range(per_turn):
                    pe.wait_ge(c.w_in[b].sem, i * (16 * pieces) + (w_base[b] + 16 * pieces))
                    pe.wait_ge(bank_free, freed(i, b))
                    for k in range(kt):
                        mm = nc.tensor.matmul(c.ps[:, b, :], w_slot(b)[:, k, :], rhs[:, k, :], start=(k == 0), stop=(k == kt - 1))
                    mm.then_inc(mm_done, 1)
                if "pe" in evacuate:
                    evacuate["pe"](pe, i)
            turn_loop(pe, body)

        for name, deco in (("act", block.scalar), ("dve", block.vector)):
            if name in evacuate:
                def program(eng, part=evacuate[name]):
                    turn_loop(eng, lambda i: part(eng, i, lambda b: eng.wait_ge(mm_done, ready(i, b)), bank_free))
                    eng.wait_ge(bank_free, per_turn * (turns + 1))
                deco(program)
    for b in range(per_turn):
        c.w_in[b].n += 16 * pieces * turns
    ctx.__exit__()


ALL = (slice(None), slice(None), slice(None))


def columns(w, col0, per_turn):
    view = w.rearrange("(k p) n -> p k n", p=P)

    def source(i, b):
        at = i * (per_turn * P) + (col0 + b * P)
        return [(ALL, view[:, :, bass.ds(at, P)])]
    return source


def tile_of(buf, i, per_turn, b):
    return buf[:, i * per_turn + b, :]


def project_copy(c, turns, per_turn, source, dest, kt=KD, rhs=None, scale=1.0):
    nc = c.nc

    def act(eng, i, wait_tile, bank_free):
        for b in range(per_turn):
            wait_tile(b)
            nc.scalar.activation(tile_of(dest, i, per_turn, b), c.ps[:, b, :], ACT.Copy, scale=scale).then_inc(bank_free, 1)
    project(c, turns, per_turn, source, {"act": act}, kt, rhs)


def project_add(c, turns, per_turn, source, dest, kt=KD, rhs=None, ring=None):
    nc = c.nc

    def dve(eng, i, wait_tile, bank_free):
        for b in range(per_turn):
            wait_tile(b)
            d = tile_of(dest, i, per_turn, b)
            nc.vector.tensor_tensor(d, d, c.ps[:, b, :], ALU.add).then_inc(bank_free, 1)
    project(c, turns, per_turn, source, {"dve": dve}, kt, rhs, ring)


def project_swiglu(c, turns, source, dest):
    nc = c.nc
    with c.stage() as ctx:
        gate = ctx.sbuf("gate", [P, 2, T])
        gated = ctx.sem("gated")

        def act(eng, i, wait_tile, bank_free):
            for j in range(2):
                wait_tile(2 * j)
                eng.wait_ge(bank_free, i * 4 + (2 * j + 2))
                nc.scalar.activation(gate[:, j, :], c.ps[:, 2 * j, :], ACT.Silu).then_inc(gated, 1)

        def dve(eng, i, wait_tile, bank_free):
            for j in range(2):
                wait_tile(2 * j + 1)
                eng.wait_ge(gated, i * 2 + (j + 1))
                nc.vector.tensor_tensor(tile_of(dest, i, 2, j), gate[:, j, :], c.ps[:, 2 * j + 1, :], ALU.mult).then_inc(bank_free, 2)
        project(c, turns, 4, source, {"act": act, "dve": dve})


def project_head_norm(c, turns, source, gains, dest):
    nc = c.nc
    with c.stage() as ctx:
        squares = ctx.sbuf("squares", [P, 4, T])
        rstd = ctx.sbuf("rstd", [P, 4, T])
        squared, summed, inverted, rooted = ctx.sem("squared"), ctx.sem("summed"), ctx.sem("inverted"), ctx.sem("rooted")

        def act(eng, i, wait_tile, bank_free):
            for b in range(4):
                wait_tile(b)
                nc.scalar.activation(squares[:, b, :], c.ps[:, b, :], ACT.Square).then_inc(squared, 1)
            for b in range(4):
                eng.wait_ge(inverted, i * 4 + (b + 1))
                nc.scalar.activation(rstd[:, b, :], rstd[:, b, :], ACT.Sqrt).then_inc(rooted, 1)

        def pe(eng, i):
            for b in range(4):
                eng.wait_ge(squared, i * 4 + (b + 1))
                nc.tensor.matmul(c.ps[:, 4 + b, :], c.ones[:, :], squares[:, b, :], start=True, stop=True).then_inc(summed, 1)

        def dve(eng, i, wait_tile, bank_free):
            step = Chain(eng, c.dve_step, i, 4)
            for b in range(4):
                eng.wait_ge(summed, i * 4 + (b + 1))
                step(nc.vector.tensor_scalar(rstd[:, b, :], c.ps[:, 4 + b, :], 1.0 / P, EPS, ALU.mult, ALU.add))
                nc.vector.reciprocal(rstd[:, b, :], rstd[:, b, :]).then_inc(inverted, 1)
            step.ends(turns)
            for b in range(4):
                eng.wait_ge(rooted, i * 4 + (b + 1))
                nc.vector.scalar_tensor_tensor(tile_of(dest, i, 4, b), c.ps[:, b, :], gains[:, bass.ds(i * 4 + b, 1)],
                                               rstd[:, b, :], ALU.mult, ALU.mult).then_inc(bank_free, 1)
        project(c, turns, 4, source, {"act": act, "pe": pe, "dve": dve})


def project_rope(c, turns, per_turn, source, tables, scale, dest):
    nc = c.nc
    swap, cos, sin = tables
    with c.stage() as ctx:
        raw = ctx.sbuf("raw", [P, per_turn, T])
        part = ctx.sbuf("part", [P, per_turn, 2, T])
        copied, swapped, scaled = ctx.sem("copied"), ctx.sem("swapped"), ctx.sem("scaled")

        def act(eng, i, wait_tile, bank_free):
            for b in range(per_turn):
                wait_tile(b)
                nc.scalar.activation(raw[:, b, :], c.ps[:, b, :], ACT.Copy).then_inc(copied, 1)

        def pe(eng, i):
            for b in range(per_turn):
                eng.wait_ge(copied, i * per_turn + (b + 1))
                nc.tensor.matmul(c.ps[:, 4 + b, :], swap[:, :], raw[:, b, :], start=True, stop=True).then_inc(swapped, 1)

        def dve(eng, i, wait_tile, bank_free):
            for b in range(per_turn):
                eng.wait_ge(swapped, i * per_turn + (b + 1))
                nc.vector.scalar_tensor_tensor(part[:, b, 0, :], c.ps[:, b, :], scale, cos[:, :], ALU.mult, ALU.mult).then_inc(scaled, 1)
                nc.vector.scalar_tensor_tensor(part[:, b, 1, :], c.ps[:, 4 + b, :], scale, sin[:, :], ALU.mult, ALU.mult).then_inc(scaled, 1)
                eng.wait_ge(scaled, i * (2 * per_turn) + (2 * b + 2))
                nc.vector.tensor_tensor(tile_of(dest, i, per_turn, b), part[:, b, 0, :], part[:, b, 1, :], ALU.add).then_inc(bank_free, 1)
        project(c, turns, per_turn, source, {"act": act, "pe": pe, "dve": dve})


def project_rows(c, w, chunks):
    nc = c.nc
    ctx = c.stage()
    w_in, mm_done, copied = ctx.sem("w_rows_in"), ctx.sem("rows_done"), ctx.sem("rows_copied")
    view = w.rearrange("(k p) n -> p k n", p=P)
    big = ctx.sbuf("w_rows", [P, min(2, len(chunks)), KD * max(n for _, n, _, _ in chunks)])
    with nc.Block() as block:

        @block.sync
        def _(sp):
            for j, (col, n, _, _) in enumerate(chunks):
                if j >= 1:
                    sp.wait_ge(w_in, 16 * j)
                if j >= 2:
                    sp.wait_ge(mm_done, TT * (j - 1))
                sp.dma_start(big[:, j % 2, 0:KD * n].rearrange("p (k n) -> p k n", n=n), view[:, :, col:col + n]).then_inc(w_in, 16)

        @block.tensor
        def _(pe):
            for j, (col, n, _, _) in enumerate(chunks):
                pe.wait_ge(w_in, 16 * (j + 1))
                for t in range(TT):
                    bank = 4 * (j % 2) + t
                    if j >= 2:
                        pe.wait_ge(copied, TT * (j - 2) + t + 1)
                    for k in range(KD):
                        mm = nc.tensor.matmul(c.ps[:, bank, 0:n], c.hT[:, k, t * P:(t + 1) * P],
                                              big[:, j % 2, k * n:(k + 1) * n], start=(k == 0), stop=(k == KD - 1))
                    mm.then_inc(mm_done, 1)

        @block.scalar
        def _(act):
            for j, (_, n, dest, func) in enumerate(chunks):
                for t in range(TT):
                    act.wait_ge(mm_done, TT * j + t + 1)
                    nc.scalar.activation(dest[:, t, :], c.ps[:, 4 * (j % 2) + t, 0:n], func).then_inc(copied, 1)
            act.wait_ge(copied, TT * len(chunks))
    ctx.__exit__()


def ffn(c, gain, w_gate, w_up, w_down):
    rms_norm(c, gain)
    gate, up = (w.rearrange("(k p) n -> p k n", p=P) for w in (w_gate, w_up))
    with c.stage() as ctx:
        aT = ctx.sbuf("aT", [P, KF, T])
        down_ring = ctx.sbuf("down_ring", [P, W_SLOTS, KF * P])

        def source(i, b):
            at = i * (2 * P) + (b // 2) * P
            return [(ALL, (gate, up)[b % 2][:, :, bass.ds(at, P)])]
        project_swiglu(c, KF // 2, source, aT)
        project_add(c, 2, 4, columns(w_down, 0, 4), c.xT, kt=KF, rhs=aT, ring=down_ring)


def store_normed(c, gain, out):
    nc = c.nc
    rms_norm(c, gain)
    with c.stage() as ctx:
        rows = ctx.sbuf("rows", [P, TT, D])
        transposed, copied, stored = ctx.sem("transposed"), ctx.sem("copied"), ctx.sem("stored")
        out_rows = out[0].rearrange("(t p) d -> p t d", p=P)
        with nc.Block() as block:

            @block.tensor
            def _(pe):
                for t in range(TT):
                    for h in range(2):
                        for k in range(4):
                            tr = nc.tensor.transpose(c.ps[:, 2 * t + h, k * P:(k + 1) * P], c.hT[:, 4 * h + k, t * P:(t + 1) * P], c.ident[:, :])
                        tr.then_inc(transposed, 1)

            @block.scalar
            def _(act):
                for t in range(TT):
                    for h in range(2):
                        act.wait_ge(transposed, 2 * t + h + 1)
                        nc.scalar.activation(rows[:, t, h * T:(h + 1) * T], c.ps[:, 2 * t + h, :], ACT.Copy).then_inc(copied, 1)

            @block.sync
            def _(sp):
                for t in range(TT):
                    sp.wait_ge(copied, 2 * t + 2)
                    sp.dma_start(out_rows[:, t, :], rows[:, t, :]).then_inc(stored, 16)
                sp.wait_ge(stored, 16 * TT)


def attention(c, turns, units, scale, staging, sinks, lag=2):
    nc = c.nc
    steps = [(u, t) for u in range(len(units)) for t in range(TT)]
    n_steps, n_units, n_sinks = len(steps), len(units), len(sinks)
    s_banks, p_bufs = (0, 1, 2), 4
    pt_bank, o_bank = 3, 7
    sink_no = {u: n for n, u in enumerate(sorted(sinks))}
    slots = sorted(staging)
    last_user = {s: max(u for u in range(n_units) if units[u]["slot"] == s) for s in slots}
    width = [P * (t + 1) for t in range(TT)]
    with c.stage() as ctx:
        probs = ctx.sbuf("probs", [P, p_bufs, T])
        probsT = ctx.sbuf("probsT", [P, 2, TT, T])
        stat = ctx.sbuf("stat", [P, 3, p_bufs])
        top, total, inverse = stat[:, 0, :], stat[:, 1, :], stat[:, 2, :]
        scored, topped, exped, summed, normed = (ctx.sem(x) for x in ("scored", "topped", "exped", "inverted", "normed"))
        p_used, turned, pt_act, pt_dve, pv_done, o_read = (ctx.sem(x) for x in ("p_used", "turned", "pt_act", "pt_dve", "pv_done", "o_read"))
        staged = {s: ctx.sem(f"staged{s}") for s in slots}
        scaled = ctx.sem("scaled")
        copies = {s: len(staging[s](0)) for s in slots}

        def loop(eng, body):
            if turns == 1:
                body(0)
            else:
                with eng.Fori(0, turns) as i:
                    body(i)

        with nc.Block() as block:

            @block.gpsimd
            def _(pool):
                pool.sem_inc(pv_done, n_units)

                def body(i):
                    for s in slots:
                        hold(pool, pv_done, i * n_units + (last_user[s] + 1), c.pool_tick)
                        for dest, source in staging[s](i):
                            nc.gpsimd.tensor_copy(dest, source).then_inc(staged[s], 1)
                loop(pool, body)

            @block.tensor
            def _(pe):
                def score(i, s):
                    u, t = steps[s]
                    unit = units[u]
                    if t == 0 and unit["slot"] is not None:
                        pe.wait_ge(staged[unit["slot"]], i * copies[unit["slot"]] + copies[unit["slot"]])
                    if s >= len(s_banks):
                        pe.wait_ge(exped, i * n_steps + (s - len(s_banks) + 1))
                    w, bank = width[t], s_banks[s % len(s_banks)]
                    out, q = c.ps[:, bank, 0:w], slice(t * P, (t + 1) * P)
                    masked = unit["mask"] is not None
                    nc.tensor.matmul(out, unit["q"][:, q], unit["k"][:, 0:w], start=True, stop=False)
                    if unit.get("q2") is not None:
                        nc.tensor.matmul(out, unit["q2"][:, q], unit["k2"][:, 0:w], start=False, stop=False)
                    if unit.get("bias") is not None:
                        ones, row = unit["bias"]
                        nc.tensor.matmul(out, ones, row[:, 0:w], start=False, stop=False)
                    if masked:
                        mm = nc.tensor.matmul(out, c.ident[:, :], unit["mask"](t), start=False, stop=True)
                    else:
                        mm = nc.tensor.matmul(c.ps[:, bank, w - P:w], c.ident[:, :], c.causal[:, :], start=False, stop=True)
                    mm.then_inc(scored, 1)

                def transposes(i, s):
                    u, t = steps[s]
                    pe.wait_ge(normed, i * n_steps + (s + 1))
                    if t == 0 and u >= 1:
                        weigh(i, u - 1)
                    for j in range(t + 1):
                        tr = nc.tensor.transpose(c.ps[:, pt_bank + j, t * P:(t + 1) * P], probs[:, s % p_bufs, j * P:(j + 1) * P], c.ident[:, :])
                    tr.then_inc(p_used, 1)

                def weigh(i, u):
                    unit = units[u]
                    pe.wait_ge(pt_act, i * (2 * n_units) + (2 * u + 2))
                    pe.wait_ge(pt_dve, i * (2 * n_units) + (2 * u + 2))
                    if unit["first"]:
                        done = sum(1 for x in sinks if x < u)
                        pe.wait_ge(o_read, i * n_sinks + (done + n_sinks))
                    for j in range(TT):
                        mm = nc.tensor.matmul(unit["out"][:, j * P:T], unit["v"](j), probsT[:, u % 2, j, j * P:T],
                                              start=unit["first"] and j == 0, stop=unit["last"] and j == TT - 1 and "add" not in unit,
                                              skip_group_check=True)
                    if "add" in unit:
                        mm = nc.tensor.matmul(unit["out"], *unit["add"], start=False, stop=unit["last"], skip_group_check=True)
                    mm.then_inc(pv_done, 1)

                pe.sem_inc(o_read, n_sinks)

                def body(i):
                    for s in range(n_steps + lag):
                        if s < n_steps:
                            score(i, s)
                        if s >= lag:
                            transposes(i, s - lag)
                    weigh(i, n_units - 1)
                loop(pe, body)

            def turned_tiles(eng, i, u, tiles, sem, copy):
                eng.wait_ge(p_used, i * n_steps + (TT * (u + 1)))
                eng.wait_ge(pv_done, i * n_units + (n_units + u - 1))
                for j in tiles:
                    copy(probsT[:, u % 2, j, j * P:T], c.ps[:, pt_bank + j, j * P:T]).then_inc(sem, 1)

            def sink_unit(s):
                u = (s - lag - TT) // TT
                return u if (s - lag) % TT == 1 and u in sinks else None

            @block.scalar
            def _(act):
                def body(i):
                    for s in range(n_steps + lag):
                        if s < n_steps:
                            u, t = steps[s]
                            act.wait_ge(topped, i * n_steps + (s + 1))
                            if s >= p_bufs:
                                act.wait_ge(p_used, i * n_steps + (s - p_bufs + 1))
                            nc.scalar.activation(probs[:, s % p_bufs, 0:width[t]], c.ps[:, s_banks[s % len(s_banks)], 0:width[t]], ACT.Exp,
                                                 bias=top[:, s % p_bufs:s % p_bufs + 1], scale=scale,
                                                 accum_out=total[:, s % p_bufs:s % p_bufs + 1]).then_inc(exped, 1)
                        if s >= lag and (s - lag) % TT == TT - 1:
                            turned_tiles(act, i, (s - lag) // TT, (0, 3), pt_act,
                                         lambda d, x: nc.scalar.activation(d, x, ACT.Copy))
                        u = sink_unit(s)
                        if u is not None:
                            read_out(i, u)
                    read_out(i, n_units - 1)

                def read_out(i, u):
                    act.wait_ge(pv_done, i * n_units + (n_units + u + 1))
                    nc.scalar.activation(sinks[u](i), units[u]["sum"], ACT.Copy).then_inc(o_read, 1)
                loop(act, body)
                act.wait_ge(o_read, n_sinks * (turns + 1))

            @block.vector
            def _(dve):
                def body(i):
                    def normalise(s):
                        u, t = steps[s]
                        dve.wait_ge(exped, i * n_steps + (s + 1))
                        one = slice(s % p_bufs, s % p_bufs + 1)
                        nc.vector.reciprocal(inverse[:, one], total[:, one]).then_inc(summed, 1)
                        dve.wait_ge(summed, i * n_steps + (s + 1))
                        p = probs[:, s % p_bufs, 0:width[t]]
                        gate = units[u]["gate"](i, t) if units[u].get("gate") else None
                        if gate is None:
                            op = nc.vector.tensor_scalar(p, p, inverse[:, one], None, ALU.mult)
                        else:
                            op = nc.vector.tensor_scalar(p, p, inverse[:, one], gate, ALU.mult, ALU.mult)
                        op.then_inc(normed, 1)

                    for s in range(n_steps + lag):
                        if s < n_steps:
                            u, t = steps[s]
                            dve.wait_ge(scored, i * n_steps + (s + 1))
                            one = top[:, s % p_bufs:s % p_bufs + 1]
                            top_op = nc.vector.tensor_reduce(one, c.ps[:, s_banks[s % len(s_banks)], 0:width[t]], AX.X, ALU.max, negate=True)
                            if scale == 1.0:
                                top_op.then_inc(topped, 1)
                            else:
                                top_op.then_inc(scaled, 1)
                                dve.wait_ge(scaled, i * n_steps + (s + 1))
                                nc.vector.tensor_scalar(one, one, scale, None, ALU.mult).then_inc(topped, 1)
                        if 1 <= s <= n_steps:
                            normalise(s - 1)
                        if s >= lag and (s - lag) % TT == TT - 1:
                            turned_tiles(dve, i, (s - lag) // TT, (1, 2), pt_dve, nc.vector.tensor_copy)
                loop(dve, body)


def whole(buf, i):
    return buf[:, i, :]


def fox_attention(c, w_in, f_bias, q_gain, k_gain, attT):
    nc = c.nc
    with c.stage() as ctx:
        qkT = ctx.sbuf("qkT", [P, 2 * FOX_H, T])
        v = ctx.sbuf("v", [P, TT, FOX_H * P])
        f = ctx.sbuf("f", [P, TT, FOX_H])
        gains = ctx.sbuf("gains", [P, 2 * FOX_H])
        pair = ctx.sbuf("pair", [P, 2])
        bias = ctx.sbuf("bias", [P, FOX_H])
        minus_tri = ctx.sbuf("minus_tri", [P, T])
        cum = ctx.sbuf("cum", [FOX_H, T])
        cum_rows = ctx.sbuf("cum_rows", [1, FOX_H, T])
        g_in, g_set = ctx.sem("gains_in"), ctx.sem("gains_set")
        with nc.Block() as block:

            @block.sync
            def _(sp):
                sp.dma_start(pair[:, 0:1], q_gain.rearrange("(p a) -> p a", a=1)).then_inc(g_in, 16)
                sp.dma_start(pair[:, 1:2], k_gain.rearrange("(p a) -> p a", a=1)).then_inc(g_in, 16)
                sp.dma_start(bias[:, :], f_bias.partition_broadcast(P)).then_inc(g_in, 16)
                sp.dma_start(minus_tri[:, :], c.ins["c_minus_tri"]).then_inc(g_in, 16)
                sp.wait_ge(g_in, 64)

            @block.vector
            def _(dve):
                dve.wait_ge(g_in, 64)
                nc.vector.tensor_scalar(gains[:, 0:FOX_H], pair[:, 0:1].to_broadcast([P, FOX_H]), float(P) ** -0.5, None, ALU.mult).then_inc(g_set, 1)
                nc.vector.tensor_copy(gains[:, FOX_H:], pair[:, 1:2].to_broadcast([P, FOX_H])).then_inc(g_set, 1)
                dve.wait_ge(g_set, 2)
        project_head_norm(c, 4, columns(w_in, SSM_W, 4), gains, qkT)
        at = SSM_W + 2 * FOX_H * P
        project_rows(c, w_in, [(at, T, v[:, :, 0:T], ACT.Copy), (at + T, T, v[:, :, T:2 * T], ACT.Copy),
                               (at + FOX_H * P, FOX_H, f, ACT.Copy)])
        forget_sums(c, f, bias, minus_tri, cum, cum_rows)
        slots = [[ctx.sbuf(f"{n}{s}", shape) for n, shape in (("q", [P, T]), ("k", [P, T]), ("v", [P, TT, P]), ("row", [1, T]))] for s in range(2)]

        def stage(s):
            def f(i):
                h = i * 2 + s
                q, k, vv, row = slots[s]
                return [(q[:, :], whole(qkT, h)), (k[:, :], whole(qkT, h + FOX_H)),
                        (vv[:, :, :], v[:, :, bass.ds(h * P, P)]), (row[:, :], whole(cum_rows, h))]
            return f
        units = [dict(q=slots[s][0], k=slots[s][1], v=lambda j, s=s: slots[s][2][:, j, :], mask=None, slot=s,
                      bias=(c.ones[0:1, :], slots[s][3]), out=c.ps[:, 7, :], sum=c.ps[:, 7, :], first=True, last=True) for s in range(2)]
        attention(c, FOX_H // 2, units, 1.0, {s: stage(s) for s in range(2)}, {s: (lambda i, s=s: whole(attT, i * 2 + s)) for s in range(2)})


def forget_sums(c, f, bias, minus_tri, cum, cum_rows):
    nc = c.nc
    with c.stage() as ctx:
        z, e, low = (ctx.sbuf(n, [P, TT, FOX_H]) for n in ("z", "e", "low"))
        zed, exped, logged, ready, summed, copied, moved = (ctx.sem(n) for n in ("zed", "exped", "logged", "ready", "summed", "copied", "moved"))
        with nc.Block() as block:

            @block.vector
            def _(dve):
                step = Chain(dve, c.dve_step)
                step(nc.vector.tensor_tensor(z[:, :, :], f[:, :, :], bias[:, :].unsqueeze(1).to_broadcast([P, TT, FOX_H]), ALU.add))
                nc.vector.tensor_scalar(low[:, :, :], z[:, :, :], 0.0, None, ALU.min).then_inc(zed, 1)
                dve.wait_ge(logged, 1)
                nc.vector.tensor_tensor(z[:, :, :], low[:, :, :], e[:, :, :], ALU.subtract).then_inc(ready, 1)
                dve.wait_ge(ready, 1)

            @block.scalar
            def _(act):
                act.wait_ge(zed, 1)
                nc.scalar.activation(e[:, :, :], z[:, :, :], ACT.Abs).then_inc(exped, 1)
                act.wait_ge(exped, 1)
                nc.scalar.activation(e[:, :, :], e[:, :, :], ACT.Exp, scale=-1.0).then_inc(exped, 1)
                act.wait_ge(exped, 2)
                nc.scalar.activation(e[:, :, :], e[:, :, :], ACT.Ln, bias=1.0).then_inc(logged, 1)
                act.wait_ge(summed, 1)
                nc.scalar.activation(cum[:, :], c.ps[0:FOX_H, 0, :], ACT.Copy).then_inc(copied, 1)

            @block.tensor
            def _(pe):
                pe.wait_ge(ready, 1)
                for t in range(TT):
                    mm = nc.tensor.matmul(c.ps[0:FOX_H, 0, t * P:T], z[:, t, :], minus_tri[:, 0:T - t * P],
                                          start=(t == 0), stop=(t == TT - 1), skip_group_check=True)
                mm.then_inc(summed, 1)

            @block.sync
            def _(sp):
                sp.wait_ge(copied, 1)
                sp.dma_start(cum_rows[0:1, :, :], cum[:, :]).then_inc(moved, 16)
                sp.wait_ge(moved, 16)


def ssm(c, A, w_in, ygT):
    nc = c.nc
    with c.stage() as ctx:
        uT = ctx.sbuf("uT", [P, SSM_T, T])
        project_copy(c, 1, SSM_T, columns(w_in, 0, SSM_T), uT)
        PM = [P, PAIRS]
        names = ("ar", "ai", "dt", "mag", "th", "turn", "cos", "sin", "lre", "lim", "nr", "den", "cre", "cim", "t0", "t1", "half_pi")
        m = {n: ctx.sbuf(n, PM) for n in names}
        powers = ctx.sbuf("powers", [P, 9, 3, PAIRS])
        b_in = [ctx.sbuf(n, [P, PAIRS, SSM_H]) for n in ("b_re", "b_im")]
        tmp = [ctx.sbuf(n, [P, PAIRS, SSM_H]) for n in ("tmp0", "tmp1")]
        wide = [c.w_ring[:, 2 * x:2 * x + 2, :].rearrange("p s (j n) -> p (s j) n", n=P) for x in range(2)]
        bT = [ctx.sbuf(n, [P, PAIRS, P]) for n in ("bT_re", "bT_im")]
        cT = [ctx.sbuf(n, [P, PAIRS, P]) for n in ("cT_re", "cT_im")]
        skip = ctx.sbuf("skip", [P, SSM_T])
        param_in, zeroed, c_in = ctx.sem("param_in"), ctx.sem("zeroed"), ctx.sem("c_in")
        mag_set, angle, trig, b_wide, b_turned, b_moved, c_turned, c_moved, b_free = (
            ctx.sem(n) for n in ("mag_set", "angle", "trig", "b_wide", "b_turned", "b_moved", "c_turned", "c_moved", "b_free"))
        by_state = lambda a: a.rearrange("(j two) s -> (two s) j", two=2)
        dt2 = A["ssm_log_step"][0].rearrange("(j two) -> two j", two=2)
        with nc.Block() as block:

            @block.sync
            def _(sp):
                sp.dma_start(m["ar"][:, :], by_state(A["ssm_a_re"][0]), allow_slow_non_contiguous=True).then_inc(param_in, 16)
                sp.dma_start(m["ai"][:, :], by_state(A["ssm_a_im"][0]), allow_slow_non_contiguous=True).then_inc(param_in, 16)
                for two in range(2):
                    sp.dma_start(m["dt"][two * SSM_S:(two + 1) * SSM_S, :], dt2[two].partition_broadcast(SSM_S), allow_slow_non_contiguous=True).then_inc(param_in, 16)
                sp.dma_start(skip[:, :], A["ssm_d"][0].rearrange("(t p) -> p t", p=P), allow_slow_non_contiguous=True).then_inc(param_in, 16)
                for x, name in enumerate(("ssm_b_re", "ssm_b_im")):
                    sp.dma_start(b_in[x][:, :, :], A[name][0].rearrange("(j two) s h -> (two s) j h", two=2)).then_inc(param_in, 16)
                sp.wait_ge(param_in, 16 * 7)
                sp.wait_ge(zeroed, 4)
                for x, name in enumerate(("ssm_c_re", "ssm_c_im")):
                    view = A[name][0].rearrange("(t g) h s -> g h t s", g=8)
                    dest = wide[x].rearrange("p (t q) n -> p t (q n)", t=SSM_T)
                    for g in range(8):
                        sp.dma_start(dest[g * SSM_H:(g + 1) * SSM_H, :, g * SSM_S:(g + 1) * SSM_S], view[g]).then_inc(c_in, 16)
                sp.wait_ge(c_in, 16 * 16)

            @block.gpsimd
            def _(pool):
                for x in range(2):
                    nc.gpsimd.memset(wide[x][:, :, :], 0.0).then_inc(zeroed, 1)
                nc.gpsimd.memset(m["half_pi"][:, :], math.pi / 2).then_inc(zeroed, 1)
                pool.wait_ge(b_moved, 8)
                for x in range(2):
                    nc.gpsimd.memset(wide[x][:, :, :], 0.0).then_inc(b_free, 1)
                pool.wait_ge(b_free, 2)
                pool.sem_inc(zeroed, 1)

            @block.scalar
            def _(act):
                act.wait_ge(param_in, 16 * 7)
                nc.scalar.activation(m["dt"][:, :], m["dt"][:, :], ACT.Exp).then_inc(mag_set, 1)
                act.wait_ge(angle, 1)
                nc.scalar.activation(m["mag"][:, :], m["mag"][:, :], ACT.Exp).then_inc(trig, 1)
                act.wait_ge(angle, 2)
                act.wait_ge(zeroed, 3)
                nc.scalar.activation(m["sin"][:, :], m["th"][:, :], ACT.Sin).then_inc(trig, 1)
                nc.scalar.activation(m["turn"][:, :], m["th"][:, :], ACT.Abs).then_inc(trig, 1)
                act.wait_ge(trig, 3)
                nc.scalar.activation(m["cos"][:, :], m["turn"][:, :], ACT.Sin, bias=m["half_pi"][:, 0:1], scale=-1.0).then_inc(trig, 1)
                act.wait_ge(trig, 4)
                for n in range(8):
                    x, q = n // 4, n % 4
                    act.wait_ge(b_turned, n + 1)
                    nc.scalar.activation(bT[x][:, 4 * q:4 * q + 4, :], c.ps[:, n, :], ACT.Copy).then_inc(b_moved, 1)
                for n in range(8):
                    x, q = n // 4, n % 4
                    act.wait_ge(c_turned, n + 1)
                    nc.scalar.activation(cT[x][:, 4 * q:4 * q + 4, :], c.ps[:, n, :], ACT.Copy, scale=(1.0, -1.0)[x]).then_inc(c_moved, 1)
                act.wait_ge(c_moved, 8)

            @block.vector
            def _(dve):
                v = nc.vector
                step = Chain(dve, c.dve_step)
                tt = lambda o, a, b, op: step(v.tensor_tensor(m[o][:, :], m[a][:, :], m[b][:, :], op))
                dve.wait_ge(param_in, 16 * 7)
                dve.wait_ge(mag_set, 1)
                step(v.tensor_tensor(m["th"][:, :], m["ai"][:, :], m["dt"][:, :], ALU.mult))
                v.tensor_tensor(m["mag"][:, :], m["ar"][:, :], m["dt"][:, :], ALU.mult).then_inc(angle, 1)
                step(v.tensor_scalar(m["turn"][:, :], m["th"][:, :], 1.0 / (2 * math.pi), 12582912.0, ALU.mult, ALU.add))
                step(v.tensor_scalar(m["turn"][:, :], m["turn"][:, :], 12582912.0, None, ALU.subtract))
                for part in (6.28125, 0.0019350051879882812, 3.019915981956753e-07):
                    step(v.scalar_tensor_tensor(m["th"][:, :], m["turn"][:, :], -part, m["th"][:, :], ALU.mult, ALU.add))
                v.tensor_scalar(m["th"][:, :], m["th"][:, :], 3.1415925, -3.1415925, ALU.min, ALU.max).then_inc(angle, 1)
                dve.wait_ge(trig, 4)
                tt("lre", "mag", "cos", ALU.mult)
                tt("lim", "mag", "sin", ALU.mult)
                step(v.tensor_scalar(m["nr"][:, :], m["lre"][:, :], 1.0, None, ALU.subtract))
                tt("den", "ar", "ar", ALU.mult)
                tt("t0", "ai", "ai", ALU.mult)
                tt("den", "den", "t0", ALU.add)
                step(v.reciprocal(m["den"][:, :], m["den"][:, :]))
                tt("t0", "nr", "ar", ALU.mult)
                tt("t1", "lim", "ai", ALU.mult)
                tt("t0", "t0", "t1", ALU.add)
                tt("cre", "t0", "den", ALU.mult)
                tt("t0", "lim", "ar", ALU.mult)
                tt("t1", "nr", "ai", ALU.mult)
                tt("t0", "t0", "t1", ALU.subtract)
                tt("cim", "t0", "den", ALU.mult)
                dve.wait_ge(zeroed, 3)
                spread = lambda n: m[n][:, :].unsqueeze(2).to_broadcast([P, PAIRS, SSM_H])
                for x, (first, second, op) in enumerate(((("cre", 0), ("cim", 1), ALU.subtract), (("cre", 1), ("cim", 0), ALU.add))):
                    step(v.tensor_tensor(tmp[0][:, :, :], spread(first[0]), b_in[first[1]][:, :, :], ALU.mult))
                    step(v.tensor_tensor(tmp[1][:, :, :], spread(second[0]), b_in[second[1]][:, :, :], ALU.mult))
                    for two in range(2):
                        rows = slice(two * SSM_S, (two + 1) * SSM_S)
                        for q in range(4):
                            at = (2 * q + two) * SSM_H
                            step(v.tensor_tensor(wide[x][rows, q::4, at:at + SSM_H], tmp[0][rows, q::4, :], tmp[1][rows, q::4, :], op))
                    dve.sem_inc(b_wide, 1)
                for lv in range(9):
                    re, im, neg = (powers[:, lv, z, :] for z in range(3))
                    if lv == 0:
                        step(v.tensor_copy(re, m["lre"][:, :]))
                        step(v.tensor_copy(im, m["lim"][:, :]))
                    else:
                        r0, i0, n0 = (powers[:, lv - 1, z, :] for z in range(3))
                        step(v.tensor_tensor(m["t0"][:, :], i0, i0, ALU.mult))
                        step(v.tensor_tensor(m["t1"][:, :], r0, r0, ALU.mult))
                        step(v.tensor_tensor(re, m["t1"][:, :], m["t0"][:, :], ALU.subtract))
                        step(v.tensor_tensor(m["t0"][:, :], r0, i0, ALU.mult))
                        step(v.tensor_scalar(im, m["t0"][:, :], 2.0, None, ALU.mult))
                    step(v.tensor_scalar(neg, im, -1.0, None, ALU.mult))

            @block.tensor
            def _(pe):
                for n in range(8):
                    x, q = n // 4, n % 4
                    pe.wait_ge(b_wide, x + 1)
                    for y in range(4):
                        tr = nc.tensor.transpose(c.ps[:, n, y * P:(y + 1) * P], wide[x][:, 4 * q + y, :], c.ident[:, :])
                    tr.then_inc(b_turned, 1)
                pe.wait_ge(c_in, 16 * 16)
                for n in range(8):
                    x, q = n // 4, n % 4
                    pe.wait_ge(b_moved, n + 1)
                    for y in range(4):
                        tr = nc.tensor.transpose(c.ps[:, n, y * P:(y + 1) * P], wide[x][:, 4 * q + y, :], c.ident[:, :])
                    tr.then_inc(c_turned, 1)
        scan(c, uT, bT, cT, powers, skip, ygT)


def scan(c, uT, bT, cT, powers, skip, ygT):
    nc = c.nc
    LEVELS = 9
    BIG = 3
    with c.stage() as ctx:
        S = [ctx.sbuf(n, [P, PAIRS, T]) for n in ("s_re", "s_im")]
        small = [ctx.sbuf(f"small{x}", [P, PAIRS, T >> (BIG + 1)]) for x in range(4)]
        filled, moved, swept, ready, y_done, y_sum, y_out = (
            ctx.sem(n) for n in ("filled", "moved", "swept", "ready", "y_done", "y_sum", "y_out"))
        with nc.Block() as block:

            @block.tensor
            def _(pe):
                for j in range(PAIRS):
                    for x in range(2):
                        n = 2 * j + x
                        if n >= 4:
                            pe.wait_ge(moved, n - 3)
                        nc.tensor.matmul(c.ps[:, n % 4, :], bT[x][:, j, :], uT[:, j // 4, :], start=True, stop=True).then_inc(filled, 1)
                for t in range(SSM_T):
                    for q in range(4):
                        j = 4 * t + q
                        pe.wait_ge(ready, j + 1)
                        for x in range(2):
                            mm = nc.tensor.matmul(c.ps[:, 4 + t, :], cT[x][:, j, :], S[x][:, j, :], start=(q == 0 and x == 0), stop=(q == 3 and x == 1))
                    mm.then_inc(y_done, 1)

            @block.scalar
            def _(act):
                for j in range(PAIRS):
                    for x in range(2):
                        act.wait_ge(filled, 2 * j + x + 1)
                        nc.scalar.activation(S[x][:, j, :], c.ps[:, (2 * j + x) % 4, :], ACT.Copy).then_inc(moved, 1)
                for t in range(SSM_T):
                    act.wait_ge(y_sum, t + 1)
                    nc.scalar.activation(ygT[:, t, :], ygT[:, t, :], ACT.Gelu_apprx_tanh).then_inc(y_out, 1)
                act.wait_ge(y_out, SSM_T)

            @block.vector
            def _(dve):
                v = nc.vector
                done = [0]

                def after(ins, n=1):
                    done[0] += 1
                    ins.then_inc(swept, 1)

                def views(level, down):
                    d = 1 << level
                    if down:
                        return slice(3 * d - 1, T, 2 * d), slice(2 * d - 1, T - d, 2 * d)
                    return slice(2 * d - 1, T, 2 * d), slice(d - 1, T, 2 * d)

                def pair_step(j, level, down):
                    to, of = views(level, down)
                    re, im, neg = (powers[:, level, z, j:j + 1] for z in range(3))
                    Sr, Si = S[0][:, j, :], S[1][:, j, :]
                    after(v.scalar_tensor_tensor(Sr[:, to], Sr[:, of], re, Sr[:, to], ALU.mult, ALU.add))
                    after(v.scalar_tensor_tensor(Si[:, to], Si[:, of], re, Si[:, to], ALU.mult, ALU.add))
                    dve.wait_ge(swept, done[0])
                    after(v.scalar_tensor_tensor(Sr[:, to], Si[:, of], neg, Sr[:, to], ALU.mult, ALU.add))
                    after(v.scalar_tensor_tensor(Si[:, to], Sr[:, of], im, Si[:, to], ALU.mult, ALU.add))
                    dve.wait_ge(swept, done[0])

                def all_step(level, down):
                    to, of = views(level, down)
                    n = len(range(*to.indices(T)))
                    a = [s[:, :, 0:n] for s in small]
                    lam = [powers[:, level, z, :].unsqueeze(2).to_broadcast([P, PAIRS, n]) for z in range(3)]
                    Sr, Si = S[0], S[1]
                    after(v.tensor_tensor(a[0], Sr[:, :, of], lam[0], ALU.mult))
                    after(v.tensor_tensor(a[1], Si[:, :, of], lam[2], ALU.mult))
                    after(v.tensor_tensor(a[2], Si[:, :, of], lam[0], ALU.mult))
                    after(v.tensor_tensor(a[3], Sr[:, :, of], lam[1], ALU.mult))
                    dve.wait_ge(swept, done[0])
                    after(v.tensor_tensor(a[0], a[0], a[1], ALU.add))
                    after(v.tensor_tensor(a[2], a[2], a[3], ALU.add))
                    dve.wait_ge(swept, done[0])
                    after(v.tensor_tensor(Sr[:, :, to], Sr[:, :, to], a[0], ALU.add))
                    after(v.tensor_tensor(Si[:, :, to], Si[:, :, to], a[2], ALU.add))
                    dve.wait_ge(swept, done[0])

                for j in range(PAIRS):
                    dve.wait_ge(moved, 2 * j + 2)
                    for level in range(BIG):
                        pair_step(j, level, False)
                for level in range(BIG, LEVELS):
                    all_step(level, False)
                for level in range(LEVELS - 2, BIG - 1, -1):
                    all_step(level, True)
                for j in range(PAIRS):
                    for level in range(BIG - 1, -1, -1):
                        pair_step(j, level, True)
                    dve.sem_inc(ready, 1)
                for t in range(SSM_T):
                    dve.wait_ge(y_done, t + 1)
                    v.scalar_tensor_tensor(ygT[:, t, :], uT[:, t, :], skip[:, t:t + 1], c.ps[:, 4 + t, :], ALU.mult, ALU.add).then_inc(y_sum, 1)
                dve.wait_ge(y_sum, SSM_T)


def merge(c, w_in, w_glu, w_out, ygT, attT):
    nc = c.nc
    col_g = SSM_W + 3 * FOX_H * P + FOX_H
    w_view = w_in.rearrange("(k p) n -> p k n", p=P)
    glu = w_glu.rearrange("(k p) n -> p k n", p=P)
    with c.stage() as ctx:
        mixed = ctx.sbuf("mixed", [P, KD, T])
        sig = ctx.sbuf("sig", [P, 3, T])
        part = ctx.sbuf("part", [P, 2, T])
        w_in_sem, mm_done, sig_done, mixed_done = [ctx.sem(f"w{b}") for b in range(4)], ctx.sem("mm_done"), ctx.sem("sig_done"), ctx.sem("mixed_done")
        parted = ctx.sem("parted")
        kinds = ((w_view, col_g, KD, c.hT), (w_view, col_g + D, KD, c.hT), (glu, D, SSM_T, ygT), (glu, 0, SSM_T, ygT))
        slot = lambda b, kt: c.w_ring[:, b, 0:kt * P].rearrange("p (k n) -> p k n", n=P)
        with nc.Block() as block:

            @block.sync
            def _(sp):
                sp.sem_inc(mm_done, 4)
                with sp.Fori(0, KD) as i:
                    for b, (view, col, kt, _) in enumerate(kinds):
                        if b < 3:
                            sp.wait_ge(mm_done, i * 4 + (b + 1 + b // 2))
                        sp.dma_start(slot(b, kt), view[:, :, bass.ds(i * P + col, P)]).then_inc(w_in_sem[b], 16)

            @block.tensor
            def _(pe):
                pe.sem_inc(mixed_done, 1)
                with pe.Fori(0, KD) as i:
                    for b, (_, _, kt, rhs) in enumerate(kinds):
                        pe.wait_ge(w_in_sem[b], i * 16 + 16)
                        if b == 0:
                            pe.wait_ge(mixed_done, i + 1)
                        for k in range(kt):
                            mm = nc.tensor.matmul(c.ps[:, b, :], slot(b, kt)[:, k, :], rhs[:, k, :], start=(k == 0), stop=(k == kt - 1))
                        mm.then_inc(mm_done, 1)

            @block.scalar
            def _(act):
                with act.Fori(0, KD) as i:
                    act.wait_ge(mixed_done, i + 1)
                    for b in range(3):
                        act.wait_ge(mm_done, i * 4 + (4 + b + 1))
                        nc.scalar.activation(sig[:, b, :], c.ps[:, b, :], ACT.Sigmoid).then_inc(sig_done, 1)

            @block.vector
            def _(dve):
                with dve.Fori(0, KD) as i:
                    dve.wait_ge(sig_done, i * 3 + 2)
                    nc.vector.tensor_tensor(part[:, 0, :], sig[:, 1, :], tile_of(attT, i, 1, 0), ALU.mult).then_inc(parted, 1)
                    dve.wait_ge(sig_done, i * 3 + 3)
                    dve.wait_ge(mm_done, i * 4 + 8)
                    nc.vector.tensor_tensor(part[:, 1, :], sig[:, 2, :], c.ps[:, 3, :], ALU.mult).then_inc(parted, 1)
                    dve.wait_ge(parted, i * 3 + 2)
                    nc.vector.tensor_tensor(part[:, 1, :], part[:, 1, :], sig[:, 0, :], ALU.mult).then_inc(parted, 1)
                    dve.wait_ge(parted, i * 3 + 3)
                    nc.vector.tensor_tensor(tile_of(mixed, i, 1, 0), part[:, 0, :], part[:, 1, :], ALU.add).then_inc(mixed_done, 1)
                dve.wait_ge(mixed_done, KD + 1)
        project_add(c, 2, 4, columns(w_out, 0, 4), c.xT, rhs=mixed)


def first_mix(c, A):
    rms_norm(c, A["mix_norm_g"][0])
    with c.stage() as ctx:
        ygT = ctx.sbuf("ygT", [P, SSM_T, T])
        ssm(c, A, A["w_in"][0], ygT)
        attT = ctx.sbuf("attT", [P, FOX_H, T])
        fox_attention(c, A["w_in"][0], A["fox_forget_bias"][0], A["q_norm_g"][0], A["k_norm_g"][0], attT)
        merge(c, A["w_in"][0], A["ssm_w_glu"][0], A["w_out"][0], ygT, attT)


GROUP = 4
RING = 16
ROUNDS = SLOTS // RING


def peer(c, A):
    rms_norm(c, A["ffn_norm_g"][0])
    with c.stage() as ctx:
        idx = ctx.sbuf("idx", [P, TT * SLOTS], U32)
        gates = ctx.sbuf("gates", [P, TT * SLOTS])
        peer_route(c, A["peer_w_query"][0], A["peer_sub_keys"][0], idx, gates)
        rows = ctx.sbuf("rows", [P, TT, D])
        to_rows(c, rows)
        peer_experts(c, A["peer_uv"], idx, gates, rows)
        add_rows(c, rows)


def to_rows(c, rows):
    nc = c.nc
    with c.stage() as ctx:
        turned, copied = ctx.sem("turned"), ctx.sem("copied")
        with nc.Block() as block:

            @block.tensor
            def _(pe):
                for n in range(2 * TT):
                    t, h = n // 2, n % 2
                    for k in range(4):
                        tr = nc.tensor.transpose(c.ps[:, n, k * P:(k + 1) * P], c.hT[:, 4 * h + k, t * P:(t + 1) * P], c.ident[:, :])
                    tr.then_inc(turned, 1)

            @block.scalar
            def _(act):
                for n in range(2 * TT):
                    act.wait_ge(turned, n + 1)
                    nc.scalar.activation(rows[:, n // 2, (n % 2) * T:(n % 2 + 1) * T], c.ps[:, n, :], ACT.Copy).then_inc(copied, 1)
                act.wait_ge(copied, 2 * TT)


def add_rows(c, rows):
    nc = c.nc
    with c.stage() as ctx:
        turned, added = ctx.sem("turned"), ctx.sem("added")
        with nc.Block() as block:

            @block.tensor
            def _(pe):
                for k in range(KD):
                    for t in range(TT):
                        tr = nc.tensor.transpose(c.ps[:, k, t * P:(t + 1) * P], rows[:, t, k * P:(k + 1) * P], c.ident[:, :])
                    tr.then_inc(turned, 1)

            @block.vector
            def _(dve):
                for k in range(KD):
                    dve.wait_ge(turned, k + 1)
                    nc.vector.tensor_tensor(c.xT[:, k, :], c.xT[:, k, :], c.ps[:, k, :], ALU.add).then_inc(added, 1)
                dve.wait_ge(added, KD)


def peer_route(c, w_query, sub_keys, idx, gates):
    nc = c.nc
    HC = 2 * PEER_H
    with c.stage() as ctx:
        qT = ctx.sbuf("qT", [P, HC, T])
        project_copy(c, HC // 4, 4, columns(w_query, 0, 4), qT)
        keys = ctx.sbuf("keys", [P, HC, P])
        keysT = ctx.sbuf("keysT", [P, HC, P])
        scores = ctx.sbuf("scores", [P, TT, HC * PEER_K])
        work = ctx.sbuf("work", [P, HC, PEER_K])
        top = ctx.sbuf("top", [P, HC, TOPK])
        top_at = ctx.sbuf("top_at", [P, HC, TOPK], U32)
        top_atf = ctx.sbuf("top_atf", [P, PEER_H, 2, TOPK])
        cand = ctx.sbuf("cand", [P, PEER_H, TOPK * TOPK])
        best = ctx.sbuf("best", [P, PEER_H, TOPK])
        best_at = ctx.sbuf("best_at", [P, PEER_H, TOPK], U32)
        half_at = ctx.sbuf("half_at", [P, 2, SLOTS], U32)
        half_f = ctx.sbuf("half_f", [P, 2, SLOTS])
        hit = ctx.sbuf("hit", [P, SLOTS, TOPK])
        key_no = ctx.sbuf("key_no", [P, 2, SLOTS])
        iota = ctx.sbuf("iota", [P, TOPK])
        total = ctx.sbuf("total", [P, PEER_H])
        keys_in, turned, moved, scored, loaded, less, exped, routed, iota_set, taken = (
            ctx.sem(n) for n in ("keys_in", "turned", "moved", "scored", "loaded", "less", "exped", "routed", "iota_set", "taken"))
        with nc.Block() as block:

            @block.sync
            def _(sp):
                sp.dma_start(keys[:, :, :], sub_keys.rearrange("h c k d -> k (h c) d")).then_inc(keys_in, 16)
                sp.dma_start(iota[:, :], c.ins["c_iota"]).then_inc(iota_set, 16)

            @block.tensor
            def _(pe):
                pe.wait_ge(keys_in, 16)
                for n in range(HC // 4):
                    for y in range(4):
                        tr = nc.tensor.transpose(c.ps[:, n, y * P:(y + 1) * P], keys[:, 4 * n + y, :], c.ident[:, :])
                    tr.then_inc(turned, 1)
                pe.wait_ge(moved, HC // 4)
                for t in range(TT):
                    for n in range(HC // 4):
                        bank = (4 * t + n) % 8
                        if t >= 2:
                            pe.wait_ge(loaded, 4 * (t - 2) + n + 1)
                        for y in range(4):
                            hc = 4 * n + y
                            mm = nc.tensor.matmul(c.ps[:, bank, y * P:(y + 1) * P], qT[:, hc, t * P:(t + 1) * P], keysT[:, hc, :], start=True, stop=True)
                        mm.then_inc(scored, 1)

            @block.scalar
            def _(act):
                for n in range(HC // 4):
                    act.wait_ge(turned, n + 1)
                    nc.scalar.activation(keysT[:, 4 * n:4 * n + 4, :], c.ps[:, n, :], ACT.Copy).then_inc(moved, 1)
                for n in range(TT * HC // 4):
                    act.wait_ge(scored, n + 1)
                    nc.scalar.activation(scores[:, n // 4, (n % 4) * T:(n % 4 + 1) * T], c.ps[:, n % 8, :], ACT.Copy).then_inc(loaded, 1)
                with act.Fori(0, TT) as t:
                    act.wait_ge(less, t + 1)
                    nc.scalar.activation(best[:, :, :], best[:, :, :], ACT.Exp).then_inc(exped, 1)

            @block.vector
            def _(dve):
                v = nc.vector
                dve.wait_ge(iota_set, 16)
                dve.wait_ge(loaded, TT * HC // 4)
                per = 1 + 5 * HC + 1 + 5 * PEER_H + 3 + 1 + 1 + 2 * 3 + 1 + 3
                with dve.Fori(0, TT) as t:
                    step = Chain(dve, c.dve_step, t, per, c.dve_tick)

                    def top16(n, values, at, source):
                        for half in (slice(0, 8), slice(8, 16)):
                            for r in range(n):
                                step.mark(v.max(values[:, r, half], source[:, r, :]))
                            step.wait()
                            for r in range(n):
                                step.mark(v.max_index(at[:, r, half], values[:, r, half], source[:, r, :]))
                            step.wait()
                            if half.start == 0:
                                for r in range(n):
                                    step.mark(v.match_replace(source[:, r, :], values[:, r, half], source[:, r, :], LOWEST))
                                step.wait()

                    step(v.tensor_copy(work[:, :, :], scores[:, t, :]))
                    top16(HC, top, top_at, work)
                    pair = top[:, :, :].rearrange("p (h c) k -> p h c k", c=2)
                    sums = cand[:, :, :].rearrange("p h (i j) -> p h i j", j=TOPK)
                    wide = [P, PEER_H, TOPK, TOPK]
                    step(v.tensor_tensor(sums, pair[:, :, 0, :].unsqueeze(3).to_broadcast(wide), pair[:, :, 1, :].unsqueeze(2).to_broadcast(wide), ALU.add))
                    top16(PEER_H, best, best_at, cand)
                    flat = best_at[:, :, :].rearrange("p h s -> p (h s)")
                    step.mark(v.tensor_copy(top_atf[:, :, :, :], top_at[:, :, :].rearrange("p (h c) k -> p h c k", c=2)))
                    step.mark(v.tensor_scalar(half_at[:, 0, :], flat, 4, None, ALU.logical_shift_right))
                    step.mark(v.tensor_scalar(half_at[:, 1, :], flat, TOPK - 1, None, ALU.bitwise_and))
                    step.wait()
                    step(v.tensor_copy(half_f[:, :, :], half_at[:, :, :]))
                    step.mark(v.tensor_copy(total[:, :], best[:, :, 0]))
                    step.wait()
                    v.tensor_tensor(best[:, :, :], best[:, :, :], total[:, :].unsqueeze(2).to_broadcast([P, PEER_H, TOPK]), ALU.subtract).then_inc(less, 1)
                    for x in range(2):
                        step(v.tensor_tensor(hit[:, :, :], half_f[:, x, :].unsqueeze(2).to_broadcast([P, SLOTS, TOPK]),
                                             iota[:, :].unsqueeze(1).to_broadcast([P, SLOTS, TOPK]), ALU.is_equal))
                        hits = hit[:, :, :].rearrange("p (h s) k -> p h s k", h=PEER_H)
                        step(v.tensor_tensor(hits, hits, top_atf[:, :, x, :].unsqueeze(2).to_broadcast(wide), ALU.mult))
                        step(v.tensor_reduce(key_no[:, x, :], hit[:, :, :], AX.X, ALU.add))
                    step(v.scalar_tensor_tensor(idx[:, bass.ds(t * SLOTS, SLOTS)], key_no[:, 0, :], float(PEER_K), key_no[:, 1, :], ALU.mult, ALU.add))
                    dve.wait_ge(exped, t + 1)
                    step(v.tensor_reduce(total[:, :], best[:, :, :], AX.X, ALU.add))
                    step(v.reciprocal(total[:, :], total[:, :]))
                    gate = gates[:, bass.ds(t * SLOTS, SLOTS)].rearrange("p (h s) -> p h s", h=PEER_H)
                    step(v.tensor_tensor(gate, best[:, :, :], total[:, :].unsqueeze(2).to_broadcast([P, PEER_H, TOPK]), ALU.mult))
                step.ends(TT)


def peer_experts(c, uv, idx, gates, rows):
    nc = c.nc
    groups = RING // GROUP
    with c.stage() as ctx:
        ring = ctx.sbuf("ring", [P, RING, 2 * D])
        idx_now = ctx.sbuf("idx_now", [P, 2, RING], U32)
        spare = c.hT[:, :, :].rearrange("p (a b) t -> p a (b t)", b=2)
        h_row, sums = spare[:, 0, :], spare[:, 2:4, :]
        dots, acts, weights = (ctx.sbuf(n, [P, RING]) for n in ("dots", "acts", "weights"))
        gathered = [c.sem(f"gathered{s}") for s in range(RING)]
        idx_set = ctx.sem("idx_set")
        used, dotted, acted, weighed, summed, tile_done = (ctx.sem(n) for n in ("used", "dotted", "acted", "weighed", "summed", "tile_done"))
        with nc.Block() as block:

            @block.gpsimd
            def _(pool):
                pool.sem_inc(used, RING)
                with pool.Fori(0, TT * ROUNDS // 2) as r:
                    for x in range(2):
                        nc.gpsimd.tensor_copy(idx_now[:, x, :], idx[:, bass.ds(r * (2 * RING) + x * RING, RING)]).then_inc(idx_set, 1)
                        hold(pool, idx_set, r * 2 + (x + 1), c.pool_tick)
                        for s in range(RING):
                            hold(pool, used, r * (2 * RING) + (x * RING + s + 1), c.pool_tick)
                            nc.gpsimd.indirect_dma_start(ring[:, s, :], None, uv, bass.IndirectOffsetOnAxis(ap=idx_now[:, x, s:s + 1], axis=0)
                                                         ).then_inc(gathered[s], 16)

            @block.scalar
            def _(act):
                with act.Fori(0, TT * ROUNDS) as r:
                    for g in range(groups):
                        act.wait_ge(dotted, r * RING + (g + 1) * GROUP)
                        of = slice(g * GROUP, (g + 1) * GROUP)
                        nc.scalar.activation(acts[:, of], dots[:, of], ACT.Gelu_apprx_tanh).then_inc(acted, 1)

            @block.vector
            def _(dve):
                v = nc.vector

                with dve.Fori(0, TT) as t:
                    step = Chain(dve, c.dve_step, t, 2, c.dve_tick)
                    step.mark(v.tensor_copy(h_row, rows[:, t, :]))
                    step.mark(v.memset(sums[:, :, :], 0.0))
                    step.wait()
                    step.ends(TT)
                    with dve.Fori(0, ROUNDS) as n:
                        def dot(g):
                            for s in range(g * GROUP, (g + 1) * GROUP):
                                dve.wait_ge(gathered[s], t * (16 * ROUNDS) + n * 16 + 16)
                                v.tensor_tensor_reduce(out=ring[:, s, 0:D], in0=ring[:, s, 0:D], in1=h_row, scale=1.0, scalar=0.0,
                                                       op0=ALU.mult, op1=ALU.add, accum_out=dots[:, s:s + 1]).then_inc(dotted, 1)

                        def add(g):
                            of = slice(g * GROUP, (g + 1) * GROUP)
                            dve.wait_ge(acted, t * (groups * ROUNDS) + n * groups + (g + 1))
                            v.tensor_tensor(weights[:, of], acts[:, of], gates[:, bass.ds(t * SLOTS + n * RING + g * GROUP, GROUP)], ALU.mult).then_inc(weighed, 1)
                            dve.wait_ge(weighed, t * (groups * ROUNDS) + n * groups + (g + 1))
                            for s in range(g * GROUP, (g + 1) * GROUP):
                                dve.wait_ge(used, t * SLOTS + n * RING + (RING + s - 1))
                                half = sums[:, s % 2, :]
                                v.scalar_tensor_tensor(half, ring[:, s, D:2 * D], weights[:, s:s + 1], half, ALU.mult, ALU.add).then_inc(used, 1)

                        dot(0)
                        for g in range(1, groups):
                            dot(g)
                            add(g - 1)
                        add(groups - 1)
                    dve.wait_ge(used, t * SLOTS + (SLOTS + RING))
                    v.tensor_tensor(rows[:, t, :], sums[:, 0, :], sums[:, 1, :], ALU.add).then_inc(tile_done, 1)
                    dve.wait_ge(tile_done, t + 1)


def tile_norm(c, buf, first, tiles, gain, factor):
    nc = c.nc
    with c.stage() as ctx:
        squares = ctx.sbuf("squares", [P, tiles, T])
        rstd = ctx.sbuf("rstd", [P, tiles, T])
        gains = ctx.sbuf("gains", [P, 1])
        gain_in, squared, summed, inverted, rooted, normed = (ctx.sem(n) for n in ("gain_in", "squared", "summed", "inverted", "rooted", "normed"))
        with nc.Block() as block:

            @block.sync
            def _(sp):
                sp.dma_start(gains[:, :], gain.rearrange("(p a) -> p a", a=1)).then_inc(gain_in, 16)

            @block.scalar
            def _(act):
                for b in range(tiles):
                    nc.scalar.activation(squares[:, b, :], buf[:, first + b, :], ACT.Square).then_inc(squared, 1)
                for b in range(tiles):
                    act.wait_ge(inverted, b + 1)
                    nc.scalar.activation(rstd[:, b, :], rstd[:, b, :], ACT.Sqrt).then_inc(rooted, 1)

            @block.tensor
            def _(pe):
                for b in range(tiles):
                    pe.wait_ge(squared, b + 1)
                    nc.tensor.matmul(c.ps[:, b, :], c.ones[:, :], squares[:, b, :], start=True, stop=True).then_inc(summed, 1)

            @block.vector
            def _(dve):
                step = Chain(dve, c.dve_step)
                dve.wait_ge(gain_in, 16)
                step(nc.vector.tensor_scalar(gains[:, :], gains[:, :], factor, None, ALU.mult))
                for b in range(tiles):
                    dve.wait_ge(summed, b + 1)
                    step(nc.vector.tensor_scalar(rstd[:, b, :], c.ps[:, b, :], 1.0 / P, EPS, ALU.mult, ALU.add))
                    nc.vector.reciprocal(rstd[:, b, :], rstd[:, b, :]).then_inc(inverted, 1)
                for b in range(tiles):
                    dve.wait_ge(rooted, b + 1)
                    tile = buf[:, first + b, :]
                    nc.vector.scalar_tensor_tensor(tile, tile, gains[:, 0:1], rstd[:, b, :], ALU.mult, ALU.mult).then_inc(normed, 1)
                dve.wait_ge(normed, tiles)


class Rope:

    def __init__(self, c, ctx, dim):
        nc = c.nc
        self.swap = ctx.sbuf("swap", [P, P])
        self.cos = ctx.sbuf("cos", [P, T])
        self.sin = ctx.sbuf("sin", [P, T])
        tables_in = ctx.sem("tables_in")
        with nc.Block() as block:

            @block.sync
            def _(sp):
                sp.dma_start(self.swap[:, :], c.ins[f"c_swap{dim}"]).then_inc(tables_in, 16)
                sp.dma_start(self.cos[:, :], c.ins[f"c_cos{dim}"]).then_inc(tables_in, 16)
                sp.dma_start(self.sin[:, :], c.ins[f"c_sin{dim}"]).then_inc(tables_in, 16)
                sp.wait_ge(tables_in, 48)
        self.tables = (self.swap, self.cos, self.sin)


def repeated(w, col, n):
    view = w.rearrange("(k p) n -> p k n", p=P)

    def source(i, b):
        return [((slice(None), slice(None), slice(r * n, (r + 1) * n)), view[:, :, col:col + n]) for r in range(P // n)]
    return source


A_SCALE = (64 + 32) ** -0.5
EV = dict(nope=0, rope=512, ckv=768, krope=896, iq=928, ik=1440, iw=1504, qb=1512, kb=2024, vb=2536)


def even_mix(c, A):
    rms_norm(c, A["norm_mix"][0])
    w_in = A["ev_w_in"][0]
    with c.stage() as ctx:
        oT = ctx.sbuf("oT", [P, KD, T])
        rows = [ctx.sbuf(n, [P, TT, w]) for n, w in (("ckv", P), ("iw", DSA_H), ("vb", T))]
        project_rows(c, w_in, [(EV["ckv"], P, rows[0], ACT.Copy), (EV["iw"], DSA_H, rows[1], ACT.Copy), (EV["vb"], T, rows[2], ACT.Copy)])
        rope64 = Rope(c, ctx, 64)
        differential(c, A, w_in, rope64, rows[2], oT)
        selected(c, A, w_in, rope64, rows[0], rows[1], oT)
        project_add(c, 2, 4, columns(A["ev_w_out"][0], 0, 4), c.xT, rhs=oT)


def differential(c, A, w_in, rope64, vb, oT):
    nc = c.nc
    lam_init = 0.8 - 0.6
    with c.stage() as ctx:
        qkT = ctx.sbuf("qkT", [P, 2 * DIFF_H, T])
        project_rope(c, 2, 4, columns(w_in, EV["qb"], 4), rope64.tables, 1.0, qkT)
        lam = ctx.sbuf("lam", [P, 4, 64])
        both = ctx.sbuf("both", [P, 2, 64])
        dots = ctx.sbuf("dots", [P, 2])
        minus = ctx.sbuf("minus", [P, 1])
        lam_in, dotted, exped = ctx.sem("lam_in"), ctx.sem("dotted"), ctx.sem("exped")
        with nc.Block() as block:

            @block.sync
            def _(sp):
                sp.dma_start(lam[:, :, :], A["ev_lambda"][0].partition_broadcast(P)).then_inc(lam_in, 16)

            @block.vector
            def _(dve):
                step = Chain(dve, c.dve_step)
                dve.wait_ge(lam_in, 16)
                step(nc.vector.tensor_tensor(both[:, :, :], lam[:, 0::2, :], lam[:, 1::2, :], ALU.mult))
                nc.vector.tensor_reduce(dots[:, :], both[:, :, :], AX.X, ALU.add).then_inc(dotted, 1)
                dve.wait_ge(exped, 1)
                step(nc.vector.scalar_tensor_tensor(minus[:, :], dots[:, 1:2], -lam_init, dots[:, 0:1], ALU.add, ALU.subtract))

            @block.scalar
            def _(act):
                act.wait_ge(dotted, 1)
                nc.scalar.activation(dots[:, :], dots[:, :], ACT.Exp).then_inc(exped, 1)
        slots = [[ctx.sbuf(f"{n}{s}", shape) for n, shape in (("q", [P, T]), ("k", [P, T]), ("v", [P, TT, P]))] for s in range(2)]
        half = lambda s: slice(64 * s, 64 * (s + 1))

        def stage(s):
            def f(h):
                q, k, v = slots[s]
                return [(q[:, :], qkT[:, h, :]), (k[:, :], qkT[:, h + DIFF_H, :]),
                        (v[:, :, :], vb[:, :, bass.ds(h * P, P)])]
            return f
        units = [dict(q=slots[s][0][half(s), :], k=slots[s][1][half(s), :], v=lambda j, s=s: slots[s][2][:, j, :], mask=None, slot=s,
                      gate=(lambda i, t: minus[:, 0:1]) if s else None, out=c.ps[:, 7, :], sum=c.ps[:, 7, :],
                      first=s == 0, last=s == 1) for s in range(2)]
        attention(c, DIFF_H, units, 64 ** -0.5, {s: stage(s) for s in range(2)}, {1: lambda h: oT[:, h + 4, :]})
    tile_norm(c, oT, 4, DIFF_H, A["ev_subln"][0], 1.0 - lam_init)


def selected(c, A, w_in, rope64, ckv, iw, oT):
    nc = c.nc
    with c.stage() as ctx:
        add_mask = ctx.sbuf("add_mask", [P, TT, T])
        choose_keys(c, w_in, rope64, iw, add_mask)
        keysT = ctx.sbuf("keysT", [P, T])
        latents(c, A["ev_kv_gain"][0], ckv, keysT)
        krT = ctx.sbuf("krT", [P, 1, T])
        q_lat = ctx.sbuf("q_lat", [P, DSA_H, T])
        q_rot = ctx.sbuf("q_rot", [P, DSA_H, T])
        outT = ctx.sbuf("outT", [P, DSA_H, T])
        w_uv = ctx.sbuf("w_uv", [P, DSA_H, 64])
        with c.stage() as inner:
            rope32 = Rope(c, inner, 32)
            qrT = inner.sbuf("qrT", [P, 2, T])
            qnT = inner.sbuf("qnT", [P, 4, T])
            w_uk = inner.sbuf("w_uk", [P, 4, P])
            head_rows = inner.sbuf("head_rows", [P, 4])
            project_rope(c, 1, 1, repeated(w_in, EV["krope"], 32), rope32.tables, 1.0, krT)
            project_rope(c, 1, 2, columns(w_in, EV["rope"], 2), rope32.tables, A_SCALE, qrT)
            project_copy(c, 1, 4, columns(w_in, EV["nope"], 4), qnT)
            up_in, made, copied, masked = (inner.sem(n) for n in ("up_in", "made", "copied", "masked"))
            with nc.Block() as block:

                @block.sync
                def _(sp):
                    sp.dma_start(w_uk[:, :, :], A["ev_w_uk"][0].rearrange("(j two) d c -> (two d) j c", two=2)).then_inc(up_in, 16)
                    sp.dma_start(head_rows[:, :], c.ins["c_head_rows"]).then_inc(up_in, 16)
                    sp.dma_start(w_uv[:, :, :], A["ev_w_uv"][0].rearrange("h c d -> c h d")).then_inc(up_in, 16)

                @block.tensor
                def _(pe):
                    pe.wait_ge(up_in, 48)
                    for h in range(DSA_H):
                        r = slice(64 * (h % 2), 64 * (h % 2) + 64)
                        nc.tensor.matmul(c.ps[:, h, :], w_uk[r, h // 2, :], qnT[r, h // 2, :], start=True, stop=True).then_inc(made, 1)

                @block.scalar
                def _(act):
                    for h in range(DSA_H):
                        act.wait_ge(made, h + 1)
                        nc.scalar.activation(q_lat[:, h, :], c.ps[:, h, :], ACT.Copy, scale=A_SCALE).then_inc(copied, 1)
                    act.wait_ge(copied, DSA_H)

                @block.vector
                def _(dve):
                    dve.wait_ge(up_in, 48)
                    for h in range(DSA_H):
                        nc.vector.tensor_scalar(q_rot[:, h, :], qrT[:, h // 4, :], head_rows[:, h % 4:h % 4 + 1], None, ALU.mult).then_inc(masked, 1)
                    dve.wait_ge(masked, DSA_H)
        slots = [[ctx.sbuf(f"{n}{s}", [P, T]) for n in ("q", "q2")] for s in range(2)]

        def stage(s):
            def f(i):
                return [(slots[s][0][:, :], q_lat[:, i * 2 + s, :]), (slots[s][1][:, :], q_rot[:, i * 2 + s, :])]
            return f
        units = [dict(q=slots[s][0], k=keysT, q2=slots[s][1], k2=krT[:, 0, :], v=lambda j: ckv[:, j, :],
                      mask=lambda t: add_mask[:, t, 0:P * (t + 1)], slot=s, out=c.ps[:, 7, :], sum=c.ps[:, 7, :],
                      first=True, last=True) for s in range(2)]
        attention(c, DSA_H // 2, units, 1.0, {s: stage(s) for s in range(2)}, {s: (lambda i, s=s: outT[:, i * 2 + s, :]) for s in range(2)})
        with c.stage() as inner:
            made, copied = inner.sem("made"), inner.sem("copied")
            with nc.Block() as block:

                @block.tensor
                def _(pe):
                    for h in range(DSA_H):
                        r = slice(64 * (h % 2), 64 * (h % 2) + 64)
                        nc.tensor.matmul(c.ps[r, h // 2, :], w_uv[:, h, :], outT[:, h, :], start=True, stop=True).then_inc(made, 1)

                @block.scalar
                def _(act):
                    for j in range(DSA_H // 2):
                        act.wait_ge(made, 2 * j + 2)
                        nc.scalar.activation(oT[:, j, :], c.ps[:, j, :], ACT.Copy).then_inc(copied, 1)
                    act.wait_ge(copied, DSA_H // 2)


def latents(c, gain, ckv, keysT):
    nc = c.nc
    with c.stage() as ctx:
        gains = ctx.sbuf("gains", [P, P])
        squares = ctx.sbuf("squares", [P, TT, P])
        rstd = ctx.sbuf("rstd", [P, TT])
        gain_in, squared, inverted, rooted, normed, turned, copied = (
            ctx.sem(n) for n in ("gain_in", "squared", "inverted", "rooted", "normed", "turned", "copied"))
        with nc.Block() as block:

            @block.sync
            def _(sp):
                sp.dma_start(gains[:, :], gain.partition_broadcast(P)).then_inc(gain_in, 16)

            @block.scalar
            def _(act):
                for t in range(TT):
                    nc.scalar.activation(squares[:, t, :], ckv[:, t, :], ACT.Square, accum_out=rstd[:, t:t + 1]).then_inc(squared, 1)
                act.wait_ge(inverted, 1)
                nc.scalar.activation(rstd[:, :], rstd[:, :], ACT.Sqrt).then_inc(rooted, 1)
                act.wait_ge(turned, 1)
                nc.scalar.activation(keysT[:, :], c.ps[:, 0, :], ACT.Copy).then_inc(copied, 1)
                act.wait_ge(copied, 1)

            @block.vector
            def _(dve):
                step = Chain(dve, c.dve_step)
                dve.wait_ge(squared, TT)
                step(nc.vector.tensor_scalar(rstd[:, :], rstd[:, :], 1.0 / P, EPS, ALU.mult, ALU.add))
                nc.vector.reciprocal(rstd[:, :], rstd[:, :]).then_inc(inverted, 1)
                dve.wait_ge(rooted, 1)
                dve.wait_ge(gain_in, 16)
                for t in range(TT):
                    nc.vector.scalar_tensor_tensor(ckv[:, t, :], ckv[:, t, :], rstd[:, t:t + 1], gains[:, :], ALU.mult, ALU.mult).then_inc(normed, 1)

            @block.tensor
            def _(pe):
                for t in range(TT):
                    pe.wait_ge(normed, t + 1)
                    tr = nc.tensor.transpose(c.ps[:, 0, t * P:(t + 1) * P], ckv[:, t, :], c.ident[:, :])
                tr.then_inc(turned, 1)


def choose_keys(c, w_in, rope64, iw, add_mask):
    nc = c.nc
    IH = DSA_H
    width = [P * (t + 1) for t in range(TT)]
    with c.stage() as ctx:
        iqT = ctx.sbuf("iqT", [P, IH // 2, T])
        ikT = ctx.sbuf("ikT", [P, 1, T])
        project_rope(c, 1, 4, columns(w_in, EV["iq"], 4), rope64.tables, 1.0, iqT)
        project_rope(c, 1, 1, repeated(w_in, EV["ik"], 64), rope64.tables, 1.0, ikT)
        relus = ctx.sbuf("relus", [P, 4, T])
        score = ctx.sbuf("score", [P, TT, T])
        work = ctx.sbuf("work", [P, TT, T])
        best = ctx.sbuf("best", [P, TT, 8])
        weights = ctx.sbuf("weights", [P, TT, IH])
        made, rectified, summed = ctx.sem("made"), ctx.sem("rectified"), ctx.sem("summed")
        steps = [(t, h) for t in range(1, TT) for h in range(IH)]
        with nc.Block() as block:

            @block.tensor
            def _(pe):
                for n, (t, h) in enumerate(steps):
                    if n >= 4:
                        pe.wait_ge(rectified, n - 3)
                    r = slice(64 * (h % 2), 64 * (h % 2) + 64)
                    nc.tensor.matmul(c.ps[:, n % 4, 0:width[t]], iqT[r, h // 2, t * P:(t + 1) * P], ikT[r, 0, 0:width[t]],
                                     start=True, stop=True).then_inc(made, 1)

            @block.scalar
            def _(act):
                for n, (t, h) in enumerate(steps):
                    act.wait_ge(made, n + 1)
                    if n >= 4:
                        act.wait_ge(summed, n - 3)
                    nc.scalar.activation(relus[:, n % 4, 0:width[t]], c.ps[:, n % 4, 0:width[t]], ACT.Relu, scale=64 ** -0.5).then_inc(rectified, 1)

            @block.vector
            def _(dve):
                v = nc.vector
                step = Chain(dve, c.dve_step)
                step(v.tensor_scalar(weights[:, :, :], iw[:, :, :], float(IH) ** -0.5, None, ALU.mult))
                for n, (t, h) in enumerate(steps):
                    dve.wait_ge(rectified, n + 1)
                    s, w = score[:, t, 0:width[t]], weights[:, t, h:h + 1]
                    if h == 0:
                        v.tensor_scalar(s, relus[:, n % 4, 0:width[t]], w, None, ALU.mult).then_inc(summed, 1)
                    else:
                        dve.wait_ge(summed, n)
                        v.scalar_tensor_tensor(s, relus[:, n % 4, 0:width[t]], w, s, ALU.mult, ALU.add).then_inc(summed, 1)
                dve.wait_ge(summed, len(steps))
                for t in range(1, TT):
                    last = score[:, t, t * P:(t + 1) * P]
                    step.mark(v.tensor_tensor(last, last, c.causal[:, :], ALU.add))
                step.wait()
                for t in range(1, TT):
                    step.mark(v.tensor_copy(work[:, t, 0:width[t]], score[:, t, 0:width[t]]))
                step.wait()
                for _ in range(DSA_SEL // 8):
                    for t in range(1, TT):
                        step.mark(v.max(best[:, t, :], work[:, t, 0:width[t]]))
                    step.wait()
                    for t in range(1, TT):
                        step.mark(v.match_replace(work[:, t, 0:width[t]], best[:, t, :], work[:, t, 0:width[t]], LOWEST))
                    step.wait()
                for t in range(1, TT):
                    step.mark(v.tensor_tensor(work[:, t, 0:width[t]], work[:, t, 0:width[t]], score[:, t, 0:width[t]], ALU.is_equal))
                step.wait()
                for t in range(1, TT):
                    step.mark(v.tensor_scalar(add_mask[:, t, 0:width[t]], work[:, t, 0:width[t]], NEG, None, ALU.mult))
                step.mark(v.tensor_copy(add_mask[:, 0, 0:P], c.causal[:, :]))
                step.wait()


OD = dict(q=0, kc=1024, vc=1280, ks=1536, vs=1792, kw=2048, vw=2304, gates=2560)
GW = NSA_G * NSA_D


def odd_mix(c, A):
    nc = c.nc
    w_in = A["od_w_in"][0]
    rms_norm(c, A["norm_mix"][1])
    with c.stage() as ctx:
        oT = ctx.sbuf("oT", [P, KD, T])
        with c.stage() as ctx:
            qT = ctx.sbuf("qT", [P, KD, T])
            kT = ctx.sbuf("kT", [P, 6, T])
            vs, vw = (ctx.sbuf(n, [P, TT, GW]) for n in ("vs", "vw"))
            gates = ctx.sbuf("gates", [P, TT, 3 * NSA_H])
            order = ctx.sbuf("order", [P, TT, 3, NSA_H])
            pcT = ctx.sbuf("pcT", [P, 4, T])
            vcr = ctx.sbuf("vcr", [P, 2, NSA_D])
            with c.stage() as inner:
                project_rows(c, w_in, [(OD["vs"], GW, vs, ACT.Copy), (OD["vw"], GW, vw, ACT.Copy), (OD["gates"], 3 * NSA_H, gates, ACT.Sigmoid)])
                rope64 = Rope(c, inner, 64)
                view = w_in.rearrange("(k p) n -> p k n", p=P)

                def q_tile(i, j):
                    return [((slice(None), slice(None), slice(64 * b, 64 * b + 64)),
                             view[:, :, bass.ds(i * 512 + (b * 256 + j * 64), 64)]) for b in range(2)]

                def k_tile(i, b):
                    return [(ALL, view[:, :, bass.ds(i * 512 + (OD["kc"] + b * P), P)])]
                project_rope(c, 2, 4, q_tile, rope64.tables, NSA_D ** -0.5, qT)
                project_rope(c, 3, 2, k_tile, rope64.tables, 1.0, kT)
            reorder_gates(c, gates, order)
            compressed(c, A, w_in, qT, kT, order, pcT, vcr)
            nsa_attention(c, qT, kT, vs, vw, order, pcT, vcr, oT)
        w_out = A["od_w_out"][0]

        def out_tile(i, m):
            return [((slice(64 * b, 64 * b + 64), slice(4 * g, 4 * g + 4), slice(None)),
                     w_out[g * 512 + b * 256:g * 512 + b * 256 + 256, :].rearrange("(j d) n -> d j n", d=64)[:, :, bass.ds(i * 512 + m * P, P)])
                    for b in range(2) for g in range(2)]
        project_add(c, 2, 4, out_tile, c.xT, rhs=oT)


def reorder_gates(c, gates, order):
    nc = c.nc
    with c.stage() as ctx:
        with nc.Block() as block:

            @block.vector
            def _(dve):
                step = Chain(dve, c.dve_step)
                for t in range(TT):
                    for kind in range(3):
                        for i in range(2):
                            step.mark(nc.vector.tensor_copy(order[:, t, kind, 8 * i:8 * i + 8].rearrange("p (j b) -> p j b", b=2),
                                                            gates[:, t, 24 * i + kind:24 * i + 24:3].rearrange("p (b j) -> p j b", b=2)))
                step.wait()


def compressed(c, A, w_in, qT, kT, order, pcT, vcr):
    nc = c.nc
    NP = CMP_N + 1
    with c.stage() as ctx:
        vcT = ctx.sbuf("vcT", [P, 2, T])
        project_copy(c, 1, 2, columns(w_in, OD["vc"], 2), vcT)
        w1 = ctx.sbuf("w1", [P, 2, CMP_LEN, P])
        w2 = ctx.sbuf("w2", [P, 2, NSA_D])
        peT = ctx.sbuf("peT", [NSA_D, 2, CMP_LEN])
        pe_bias = ctx.sbuf("pe_bias", [P, 2])
        hidden = ctx.sbuf("hidden", [P, 2, 2, 2, NP])
        spread = ctx.sbuf("spread", [P, 2, 2, 2, NP])
        kcT = ctx.sbuf("kcT", [P, 2, NP])
        masks = ctx.sbuf("masks", [P, 2, TT, NP])
        s = ctx.sbuf("s", [P, TT, NSA_H, NP])
        stat = ctx.sbuf("stat", [P, 2, TT, NSA_H])
        cmp_in, padded, made, biased, hid, spread_done, kv_made, kv_done = (
            ctx.sem(n) for n in ("cmp_in", "padded", "made", "biased", "hid", "spread_done", "kv_made", "kv_done"))
        scored, less, exped, weighed, turned, copied = (ctx.sem(n) for n in ("scored", "less", "exped", "weighed", "turned", "copied"))
        n_in = 16 * (4 + 1 + 2 + 2)
        source = (kT, vcT)
        half = lambda b: slice(64 * b, 64 * b + 64)
        with nc.Block() as block:

            @block.sync
            def _(sp):
                for z in range(2):
                    for b in range(2):
                        sp.dma_start(w1[half(b), z, :, :], A["od_cmp_w1"][0, z].rearrange("(l d) e -> d l e", d=NSA_D)).then_inc(cmp_in, 16)
                    sp.dma_start(peT[:, z, :], A["od_cmp_pe"][0, z].rearrange("l d -> d l"), allow_slow_non_contiguous=True).then_inc(cmp_in, 16)
                sp.dma_start(w2[:, :, :], A["od_cmp_w2"][0].rearrange("z e d -> e z d")).then_inc(cmp_in, 16)
                sp.dma_start(masks[:, 0, :, :], c.ins["c_cmp_add"]).then_inc(cmp_in, 16)
                sp.dma_start(masks[:, 1, :, :], c.ins["c_cmp_seen"]).then_inc(cmp_in, 16)

            @block.gpsimd
            def _(pool):
                nc.gpsimd.memset(hidden[:, :, :, :, :], 0.0).then_inc(padded, 1)

            @block.tensor
            def _(pe):
                pe.wait_ge(cmp_in, n_in)
                for z in range(2):
                    for l in range(CMP_LEN):
                        mm = nc.tensor.matmul(c.ps[:, 2 * z, 0:1], w1[0:NSA_D, z, l, :], peT[:, z, l:l + 1], start=(l == 0), stop=(l == CMP_LEN - 1))
                    mm.then_inc(made, 1)
                    for b in range(2):
                        for l in range(CMP_LEN):
                            block_tokens = source[z][half(b), 0:2, l:l + CMP_STRIDE * (CMP_N - 1) + 1:CMP_STRIDE]
                            mm = nc.tensor.matmul(c.ps[:, 4 + 2 * z + b, 0:2 * CMP_N].rearrange("p (i n) -> p i n", i=2), w1[half(b), z, l, :], block_tokens,
                                                  start=(l == 0), stop=(l == CMP_LEN - 1))
                        mm.then_inc(made, 1)
                pe.wait_ge(hid, 4)
                for b in range(2):
                    mm = nc.tensor.matmul(c.ps[half(b), 0, 0:2 * NP], w2[:, 0, :], hidden[:, 0, b, :, :].rearrange("p i n -> p (i n)"), start=True, stop=True)
                mm.then_inc(kv_made, 1)
                pe.wait_ge(spread_done, 2)
                for i in range(2):
                    mm = nc.tensor.matmul(c.ps[:, 1, i * NSA_D:(i + 1) * NSA_D], spread[:, i, :, :, :].rearrange("p a b n -> p (a b n)"), w2[:, 1, :],
                                          start=True, stop=True)
                mm.then_inc(kv_made, 1)
                pe.wait_ge(kv_done, 2)
                for t in range(TT):
                    for h in range(NSA_H):
                        i, j, b = h // 8, (h // 2) % 4, h % 2
                        mm = nc.tensor.matmul(c.ps[:, 2 * t + b, (h // 2) * NP:(h // 2 + 1) * NP], qT[half(b), 4 * i + j, t * P:(t + 1) * P], kcT[half(b), i, :],
                                              start=True, stop=True)
                    mm.then_inc(scored, 1)
                for t in range(TT):
                    pe.wait_ge(weighed, t + 1)
                    for m in range(4):
                        tr = nc.tensor.transpose(c.ps[:, t, m * P:(m + 1) * P], s[:, t, 4 * m:4 * m + 4, :].rearrange("p h n -> p (h n)"), c.ident[:, :])
                    tr.then_inc(turned, 1)

            @block.scalar
            def _(act):
                act.wait_ge(padded, 1)
                for z in range(2):
                    act.wait_ge(made, 3 * z + 1)
                    nc.scalar.activation(pe_bias[:, z:z + 1], c.ps[:, 2 * z, 0:1], ACT.Copy).then_inc(biased, 1)
                    act.wait_ge(biased, z + 1)
                    for b in range(2):
                        act.wait_ge(made, 3 * z + b + 2)
                        nc.scalar.activation(hidden[:, z, b, :, 0:CMP_N], c.ps[:, 4 + 2 * z + b, 0:2 * CMP_N].rearrange("p (i n) -> p i n", i=2),
                                             ACT.Gelu_apprx_tanh, bias=pe_bias[:, z:z + 1]).then_inc(hid, 1)
                act.wait_ge(kv_made, 1)
                nc.scalar.activation(kcT[:, :, :], c.ps[:, 0, 0:2 * NP].rearrange("p (i n) -> p i n", i=2), ACT.Copy).then_inc(kv_done, 1)
                act.wait_ge(kv_made, 2)
                nc.scalar.activation(vcr[:, :, :], c.ps[:, 1, 0:P].rearrange("p (i d) -> p i d", i=2), ACT.Copy).then_inc(kv_done, 1)
                for t in range(TT):
                    act.wait_ge(less, t + 1)
                    nc.scalar.activation(s[:, t, :, :], s[:, t, :, :], ACT.Exp).then_inc(exped, 1)
                for t in range(TT):
                    act.wait_ge(turned, t + 1)
                    nc.scalar.activation(pcT[:, :, t * P:(t + 1) * P], c.ps[:, t, :].rearrange("p (m q) -> p m q", m=4), ACT.Copy).then_inc(copied, 1)
                act.wait_ge(copied, TT)

            @block.vector
            def _(dve):
                v = nc.vector
                step = Chain(dve, c.dve_step)
                dve.wait_ge(hid, 4)
                for a in range(2):
                    v.tensor_copy(spread[:, :, a, :, :], hidden[:, 1, :, :, :].rearrange("p b i n -> p i b n")).then_inc(spread_done, 1)
                full = [P, NSA_H, NP]
                for t in range(TT):
                    dve.wait_ge(scored, t + 1)
                    st, top, den = s[:, t, :, :], stat[:, 0, t, :], stat[:, 1, t, :]
                    for b in range(2):
                        step.mark(v.tensor_tensor(s[:, t, b::2, :], c.ps[:, 2 * t + b, 0:NSA_H // 2 * NP].rearrange("p (h n) -> p h n", n=NP),
                                                  masks[:, 0, t, :].unsqueeze(1).to_broadcast([P, NSA_H // 2, NP]), ALU.add))
                    step.wait()
                    step(v.tensor_reduce(top, st, AX.X, ALU.max))
                    v.tensor_tensor(st, st, top.unsqueeze(2).to_broadcast(full), ALU.subtract).then_inc(less, 1)
                for t in range(TT):
                    dve.wait_ge(exped, t + 1)
                    st, zero, den = s[:, t, :, :], stat[:, 0, t, :], stat[:, 1, t, :]
                    step(v.tensor_tensor(st, st, masks[:, 1, t, :].unsqueeze(1).to_broadcast(full), ALU.mult))
                    step(v.tensor_reduce(den, st, AX.X, ALU.add))
                    step(v.tensor_scalar(zero, den, 0.0, None, ALU.is_equal))
                    step(v.tensor_tensor(den, den, zero, ALU.add))
                    step(v.reciprocal(den, den))
                    step(v.tensor_tensor(den, den, order[:, t, 0, :], ALU.mult))
                    v.tensor_tensor(st, st, den.unsqueeze(2).to_broadcast(full), ALU.mult).then_inc(weighed, 1)


def nsa_attention(c, qT, kT, vs, vw, order, pcT, vcr, oT):
    with c.stage() as ctx:
        q = [ctx.sbuf(f"q{jj}", [P, T]) for jj in range(2)]
        k = [ctx.sbuf(n, [P, T]) for n in ("k_sel", "k_win")]
        v = [ctx.sbuf(n, [P, TT, P]) for n in ("v_sel", "v_win")]
        pc = ctx.sbuf("pc", [P, T])
        vc = ctx.sbuf("vc", [P, NSA_D])

        def stage_all(m):
            i = m // 2
            return [(q[0][:, :], qT[:, m * 2, :]), (k[0][:, :], kT[:, i + 2, :]), (v[0][:, :, :], vs[:, :, bass.ds(i * P, P)]),
                    (pc[:, :], pcT[:, m, :]), (vc[:, :], vcr[:, i, :]), (k[1][:, :], kT[:, i + 4, :]), (v[1][:, :, :], vw[:, :, bass.ds(i * P, P)]),
                    (q[1][:, :], qT[:, m * 2 + 1, :])]
        units = []
        for jj in range(2):
            for b in range(2):
                half = slice(64 * b, 64 * b + 64)
                rows = slice(32 * (2 * jj + b), 32 * (2 * jj + b) + 32)
                for kind in range(2):
                    unit = dict(q=q[jj][half, :], k=k[kind][half, :], v=lambda j, kind=kind, half=half: v[kind][:, j, half], mask=None, slot=0,
                                gate=lambda m, t, kind=kind, at=2 * jj + b: order[:, t, 1 + kind, bass.ds(m * 4 + at, 1)],
                                out=c.ps[half, 7, :], sum=c.ps[:, 7, :], first=kind == 0, last=kind == 1)
                    if kind == 0:
                        unit["add"] = (vc[rows, :], pc[rows, :])
                    units.append(unit)
        attention(c, 4, units, 1.0, {0: stage_all}, {3: lambda m: oT[:, m * 2, :], 7: lambda m: oT[:, m * 2 + 1, :]})


FIRST = ("mix_norm_g w_in ssm_a_re ssm_a_im ssm_log_step ssm_b_re ssm_b_im ssm_c_re ssm_c_im ssm_d ssm_w_glu "
         "fox_forget_bias q_norm_g k_norm_g w_out ffn_norm_g peer_w_query peer_sub_keys").split()
SECOND = ("norm_mix norm_ffn norm_final ev_w_in ev_kv_gain ev_w_uk ev_w_uv ev_lambda ev_subln ev_w_out "
          "od_w_in od_cmp_pe od_cmp_w1 od_cmp_w2 od_w_out ffn_w_gate ffn_w_up ffn_w_down").split()


def constants():
    row, token = np.arange(P), np.arange(T)
    made = {
        "c_ident": np.eye(P),
        "c_causal": np.where(row[None] <= row[:, None], 0.0, NEG),
        "c_minus_tri": np.where(row[:, None] <= token[None], -1.0, 0.0),
        "c_iota": np.tile(np.arange(TOPK), (P, 1)),
        "c_head_rows": row[:, None] // 32 == np.arange(4)[None],
    }
    for dim in (32, 64):
        rates = (10000.0 ** (-np.arange(0, dim, 2) / dim)).astype(np.float32)
        angles = (token.astype(np.float32)[:, None] * rates[None]).T
        made[f"c_cos{dim}"] = np.tile(np.cos(angles), (P // dim * 2, 1))
        made[f"c_sin{dim}"] = np.tile(np.sin(angles), (P // dim * 2, 1))
        swap = np.zeros((P, P))
        for r in range(P):
            second = r % dim >= dim // 2
            swap[r - dim // 2 if second else r + dim // 2, r] = 1.0 if second else -1.0
        made[f"c_swap{dim}"] = swap
    block = np.arange(CMP_N + 1)
    query = np.arange(TT)[None, :, None] * P + row[:, None, None]
    seen = (block * CMP_STRIDE + CMP_LEN - 1 <= query) & (block < CMP_N)
    made["c_cmp_add"], made["c_cmp_seen"] = np.where(seen, 0.0, NEG), seen
    return {name: table.astype(np.float32) for name, table in made.items()}


def build(nc, ins, out):
    with ExitStack() as ctx:
        c = Core(nc, ctx, ins)
        load_consts(c)
        first_mix(c, ins)
        peer(c, ins)
        even_mix(c, ins)
        ffn(c, ins["norm_ffn"][0], ins["ffn_w_gate"][0], ins["ffn_w_up"][0], ins["ffn_w_down"][0])
        odd_mix(c, ins)
        ffn(c, ins["norm_ffn"][1], ins["ffn_w_gate"][1], ins["ffn_w_up"][1], ins["ffn_w_down"][1])
        store_normed(c, ins["norm_final"], out)


def kernel(**inputs):
    import concourse.bacc as bacc
    from concourse.bass_utils import run_bass_kernel_spmd

    arrays = {"x": inputs["x"]}
    arrays.update({name: inputs[name] for name in FIRST})
    arrays.update({name: inputs[name + "_2"] for name in SECOND})
    arrays["peer_uv"] = np.concatenate([np.asarray(inputs["peer_u"])[0], np.asarray(inputs["peer_v"])[0]], axis=1)
    arrays.update(constants())
    arrays = {name: np.ascontiguousarray(a) for name, a in arrays.items()}
    nc = bacc.Bacc("TRN2", target_bir_lowering=False, num_devices=1)
    ins = {name: nc.dram_tensor(f"in_{name}_dram", a.shape, mybir.dt.from_np(a.dtype), kind="ExternalInput").ap() for name, a in arrays.items()}
    out = nc.dram_tensor("out_0_dram", (1, T, D), F32, kind="ExternalOutput").ap()
    build(nc, ins, out)
    result = run_bass_kernel_spmd(nc, [{f"in_{name}_dram": a for name, a in arrays.items()}], core_ids=[0])
    return result.results[0]["out_0_dram"]
```

```python
import math
from collections import namedtuple
from contextlib import ExitStack

import numpy as np
import concourse.bass as bass
from concourse import mybir

F32 = mybir.dt.float32
F32R = mybir.dt.float32r
U32 = mybir.dt.uint32
ALU = mybir.AluOpType
ACT = mybir.ActivationFunctionType
AX = mybir.AxisListType

P = 128
T = 512
TT = T // P
D = 1024
KD = D // P
EPS = 1e-6
NEG = -1.0e30
LOWEST = -3.0e38

SSM_W, SSM_H, SSM_G, SSM_S = 512, 16, 32, 64
PAIRS = SSM_G // 2
SSM_T = SSM_W // P
FOX_H = 8
PEER_H, PEER_K, TOPK = 8, 128, 16
SLOTS = PEER_H * TOPK

DSA_H, DSA_SEL = 8, T // 4
DIFF_H = 4
NSA_G, NSA_HPG, NSA_D = 4, 4, 64
NSA_H = NSA_G * NSA_HPG
CMP_LEN, CMP_STRIDE = 32, 16
CMP_N = T // CMP_STRIDE - 1
D_FF = 2816
KF = D_FF // P

W_SLOTS = 4
W_SLOT = KD * P


class Tally:

    def __init__(self, sem):
        self.sem = sem
        self.n = 0

    def inc(self, ins, by=1):
        ins.then_inc(self.sem, by)
        self.n += by
        return self.n


def hold(eng, sem, value, tick):
    eng.wait_ge(sem, value)
    eng.sem_inc(tick, 1)


class Chain:

    def __init__(self, eng, tally, turn=None, per=0, tick=None):
        self.eng, self.tally, self.turn, self.per, self.tick = eng, tally, turn, per, tick
        self.base = tally.n
        self.k = 0

    def __call__(self, ins):
        self.k += 1
        ins.then_inc(self.tally.sem, 1)
        if self.turn is None:
            self.tally.n += 1
        self.wait()

    def mark(self, ins):
        self.k += 1
        ins.then_inc(self.tally.sem, 1)
        if self.turn is None:
            self.tally.n += 1

    def wait(self):
        if self.turn is None:
            self.eng.wait_ge(self.tally.sem, self.tally.n)
        elif self.tick is None:
            self.eng.wait_ge(self.tally.sem, self.turn * self.per + (self.base + self.k))
        else:
            hold(self.eng, self.tally.sem, self.turn * self.per + (self.base + self.k), self.tick)

    def ends(self, turns):
        assert self.k == self.per, (self.k, self.per)
        self.tally.n += turns * self.per


Halves = namedtuple("Halves", "high low")


def rounded(ap):
    return ap.bitcast(F32R)


def high_half(nc, high, whole):
    return nc.scalar.activation(rounded(high), whole, ACT.Copy)


def low_half(eng, low, whole, high):
    return eng.tensor_tensor(rounded(low), whole, high, ALU.subtract)


def product(nc, out, w_high, w_low, x_high, x_low, start, stop):
    nc.tensor.matmul(out, rounded(w_high), rounded(x_low), start=start, stop=False)
    nc.tensor.matmul(out, rounded(w_high), rounded(x_high), start=False, stop=False)
    return nc.tensor.matmul(out, rounded(w_low), rounded(x_high), start=False, stop=stop)


class Core:

    def __init__(self, nc, ctx, ins):
        self.nc, self.ctx, self.ins = nc, ctx, ins
        self.names = 0
        self.xT = self.sbuf(ctx, "xT", [P, KD, T])
        self.w_ring = self.sbuf(ctx, "w_ring", [P, W_SLOTS, W_SLOT])
        self.h = None
        self.ident = self.sbuf(ctx, "ident", [P, P])
        self.ones = self.sbuf(ctx, "ones", [P, P])
        self.eps = self.sbuf(ctx, "eps", [P, 1])
        self.causal = self.sbuf(ctx, "causal", [P, P])
        self.ps = ctx.enter_context(nc.psum_tensor("ps", [P, 8, T], F32))
        self.rows_in = [Tally(self.sem(f"rows_in{b}")) for b in range(2)]
        self.w_in = [Tally(self.sem(f"w_in{b}")) for b in range(W_SLOTS)]
        self.act_step = Tally(self.sem("act_step"))
        self.dve_step = Tally(self.sem("dve_step"))
        self.x_saved, self.x_back = self.sem("x_saved"), self.sem("x_back")
        self.x_dram = nc.dram_tensor("x_transposed", (P, KD, T), F32).ap()
        self.dve_tick, self.pool_tick, self.sp_tick = self.sem("dve_tick"), self.sem("pool_tick"), self.sem("sp_tick")

    def sbuf(self, ctx, name, shape, dt=F32):
        self.names += 1
        return ctx.enter_context(self.nc.sbuf_tensor(f"{name}_{self.names}", shape, dt))

    def halves(self, ctx, name, shape):
        return Halves(ctx.sbuf(f"{name}_high", shape), ctx.sbuf(f"{name}_low", shape))

    def sem(self, name):
        self.names += 1
        return self.nc.alloc_semaphore(f"{name}_{self.names}")

    def stage(self):
        return Stage(self)


class Stage:

    def __init__(self, core):
        self.core = core
        self.memory = ExitStack()
        self.sems = []

    def __enter__(self):
        return self

    def __exit__(self, *failed):
        if not any(failed) and self.sems:
            self.core.nc.clear_and_free_semaphores(self.sems)
            self.core.nc.all_engine_barrier(sem_only=True)
        self.memory.close()

    def sbuf(self, name, shape, dt=F32):
        return self.core.sbuf(self.memory, name, shape, dt)

    def sem(self, name):
        self.sems.append(self.core.sem(name))
        return self.sems[-1]


def load_consts(c):
    nc = c.nc
    with c.stage() as ctx:
        x_rows = ctx.sbuf("x_rows", [P, TT, D])
        consts_in, x_in = ctx.sem("consts_in"), ctx.sem("x_in")
        ones_set, transposed, copied = ctx.sem("ones_set"), ctx.sem("transposed"), ctx.sem("copied")
        with nc.Block() as block:

            @block.sync
            def _(sp):
                sp.dma_start(c.ident[:, :], c.ins["c_ident"]).then_inc(consts_in, 16)
                sp.dma_start(c.causal[:, :], c.ins["c_causal"]).then_inc(consts_in, 16)
                sp.dma_start(x_rows[:, :, :], c.ins["x"][0].rearrange("(t p) d -> p t d", p=P)).then_inc(x_in, 16)

            @block.gpsimd
            def _(pool):

                nc.gpsimd.memset(c.ones[:, :], 1.0).then_inc(ones_set, 1)
                nc.gpsimd.memset(c.eps[:, :], EPS).then_inc(ones_set, 1)
                pool.wait_ge(ones_set, 2)

            @block.tensor
            def _(pe):
                pe.wait_ge(consts_in, 32)
                pe.wait_ge(x_in, 16)
                for k in range(KD):
                    for t in range(TT):
                        tr = nc.tensor.transpose(c.ps[:, k, t * P:(t + 1) * P], x_rows[:, t, k * P:(k + 1) * P], c.ident[:, :])
                    tr.then_inc(transposed, 1)

            @block.scalar
            def _(act):
                for k in range(KD):
                    act.wait_ge(transposed, k + 1)
                    nc.scalar.activation(c.xT[:, k, :], c.ps[:, k, :], ACT.Copy).then_inc(copied, 1)
                act.wait_ge(copied, KD)


def rms_norm(c, gain, dest, ahead=None):
    nc = c.nc
    halves = isinstance(dest, Halves)
    if ahead is not None:
        ahead.count(c)
    with c.stage() as ctx:
        gains = ctx.sbuf("gains", [P, KD])
        squares = ctx.sbuf("squares", [P, KD, T])
        rstd = ctx.sbuf("rstd", [P, T])
        gain_in, squared, summed = ctx.sem("gain_in"), ctx.sem("squared"), ctx.sem("summed")
        inverted, rooted, normed, high, low = (ctx.sem(n) for n in ("inverted", "rooted", "normed", "high", "low"))
        whole = squares if halves else dest
        with nc.Block() as block:

            @block.sync
            def _(sp):
                sp.dma_start(gains[:, :], gain.rearrange("(k p) -> p k", p=P), allow_slow_non_contiguous=True).then_inc(gain_in, 16)
                if ahead is not None:
                    for b in range(ahead.per_turn):
                        ahead.load(c, sp, 0, b)

            @block.scalar
            def _(act):
                for k in range(KD):
                    nc.scalar.activation(squares[:, k, :], c.xT[:, k, :], ACT.Square).then_inc(squared, 1)
                act.wait_ge(summed, 1)
                nc.scalar.activation(rstd[:, :], c.ps[:, 0, :], ACT.Sqrt, bias=c.eps[:, 0:1], scale=1.0 / D).then_inc(rooted, 1)
                if halves:
                    for k in range(KD):
                        act.wait_ge(normed, k + 1)
                        high_half(nc, dest.high[:, k, :], whole[:, k, :]).then_inc(high, 1)

            @block.tensor
            def _(pe):
                for k in range(KD):
                    pe.wait_ge(squared, k + 1)
                    mm = nc.tensor.matmul(c.ps[:, 0, :], c.ones[:, :], squares[:, k, :], start=(k == 0), stop=(k == KD - 1))
                mm.then_inc(summed, 1)

            @block.gpsimd
            def _(pool):
                if halves:
                    for n, k in enumerate(range(0, KD, 2)):
                        pool.wait_ge(high, k + 1)
                        low_half(nc.gpsimd, dest.low[:, k, :], whole[:, k, :], dest.high[:, k, :]).then_inc(low, 1)
                    pool.wait_ge(low, KD)

            @block.vector
            def _(dve):
                dve.wait_ge(rooted, 1)
                nc.vector.reciprocal(rstd[:, :], rstd[:, :]).then_inc(inverted, 1)
                dve.wait_ge(gain_in, 16)
                dve.wait_ge(inverted, 1)
                for k in range(KD):
                    nc.vector.scalar_tensor_tensor(whole[:, k, :], c.xT[:, k, :], gains[:, k:k + 1], rstd[:, :], ALU.mult, ALU.mult).then_inc(normed, 1)
                dve.wait_ge(normed, KD)
                if halves:
                    for k in range(1, KD, 2):
                        dve.wait_ge(high, k + 1)
                        low_half(nc.vector, dest.low[:, k, :], whole[:, k, :], dest.high[:, k, :]).then_inc(low, 1)


class Weights:

    def __init__(self, turns, per_turn, source, kt=KD, parts=1):
        self.turns, self.per_turn, self.source, self.parts = turns, per_turn, source, parts
        self.kt = [kt] * per_turn if isinstance(kt, int) else kt
        self.pieces = len(source(0, 0))
        self.base = None

    def slot(self, buf, b):
        return buf[:, b, 0:self.kt[b] * P].rearrange("p (k n) -> p k n", n=P)

    def load(self, c, sp, i, b):
        for place, view in self.source(i, b):
            sp.dma_start(self.slot(c.w_ring, b)[place], view).then_inc(c.w_in[b].sem, 16)

    def ring_slots(self, b):
        return (b,)

    def count(self, c):
        if self.base is None:
            self.base = [c.w_in[b].n for b in range(self.per_turn)]
            for b in range(self.per_turn):
                c.w_in[b].n += 16 * self.pieces * self.turns
            return True
        return False


def project(c, w, evacuate, rhs=None, ahead=None, whole=None, before={}, after={}):
    nc = c.nc
    rhs = c.h if rhs is None else rhs
    rhs = rhs if isinstance(rhs, list) else [rhs] * w.per_turn
    turns, per_turn, parts = w.turns, w.per_turn, w.parts
    ctx = c.stage()
    mm_done, bank_free, high, low = (ctx.sem(n) for n in ("mm_done", "bank_free", "high", "low"))
    x_high, x_low = ctx.sem("x_high"), ctx.sem("x_low")
    w_halves = c.halves(ctx, "w", [P, per_turn, max(w.kt) * P])
    fresh = w.count(c)
    if ahead is not None:
        ahead.count(c)

    def ready(i, b):
        return i * per_turn + (per_turn + b + 1)

    def freed(i, b):
        return i * per_turn + (b + 1)

    def turn_loop(eng, body, first=0, last=turns):
        if last - first == 1:
            body(first)
        elif last > first:
            with eng.Fori(first, last) as i:
                body(i)

    with nc.Block() as block:

        @block.sync
        def _(sp):
            if fresh:
                for b in range(per_turn):
                    w.load(c, sp, 0, b)
            if "sp" in before:
                before["sp"](sp)

            def body(i):
                for b in range(per_turn):
                    hold(sp, low, (i - 1) * per_turn + (b + 1), c.sp_tick)
                    w.load(c, sp, i, b)
            turn_loop(sp, body, 1)
            if ahead is not None:
                for b in range(ahead.per_turn):
                    mine = [s for s in ahead.ring_slots(b) if s < per_turn]
                    if mine:
                        sp.wait_ge(low, (turns - 1) * per_turn + (max(mine) + 1))
                    ahead.load(c, sp, 0, b)

        @block.gpsimd
        def _(pool):
            def body(i):
                for b in range(per_turn):
                    pool.wait_ge(high, i * per_turn + (b + 1))
                    low_half(nc.gpsimd, *(buf[:, b, 0:w.kt[b] * P] for buf in (w_halves.low, c.w_ring, w_halves.high))).then_inc(low, 1)
            turn_loop(pool, body)

        @block.tensor
        def _(pe):
            pe.sem_inc(mm_done, per_turn)
            pe.sem_inc(bank_free, per_turn)
            if "pe" in before:
                before["pe"](pe)
            if whole is not None:
                pe.wait_ge(x_low, whole.shape[1])

            def body(i):
                for b in range(per_turn):
                    part, bank = b % parts, b // parts
                    pe.wait_ge(low, i * per_turn + (b + 1))
                    if part == 0:
                        pe.wait_ge(bank_free, freed(i, b))
                    for k in range(w.kt[b]):
                        x = sum(w.kt[b - part:b]) + k
                        mm = product(nc, c.ps[:, bank, :], w.slot(w_halves.high, b)[:, k, :], w.slot(w_halves.low, b)[:, k, :],
                                     rhs[b].high[:, x, :], rhs[b].low[:, x, :],
                                     start=(part == 0 and k == 0), stop=(part == parts - 1 and k == w.kt[b] - 1))
                    mm.then_inc(mm_done, 1)
                    if "pe" in evacuate and b >= 1:
                        evacuate["pe"](pe, i, b - 1)
                if "pe" in evacuate:
                    evacuate["pe"](pe, i, per_turn - 1)
            turn_loop(pe, body)
            if "pe" in after:
                after["pe"](pe)

        @block.scalar
        def _(act):
            def split(i, b):
                act.wait_ge(c.w_in[b].sem, i * (16 * w.pieces) + (w.base[b] + 16 * w.pieces))
                act.wait_ge(mm_done, freed(i, b))
                high_half(nc, w_halves.high[:, b, 0:w.kt[b] * P], c.w_ring[:, b, 0:w.kt[b] * P]).then_inc(high, 1)

            def start():
                if whole is not None:
                    for k in range(whole.shape[1]):
                        high_half(nc, rhs[0].high[:, k, :], whole[:, k, :]).then_inc(x_high, 1)

            if "act" not in evacuate:
                start()
                turn_loop(act, lambda i: [split(i, b) for b in range(per_turn)])
                return
            lag = 1 if per_turn > 2 else 0
            for b in range(per_turn if turns == 1 else per_turn - lag):
                split(0, b)
                if b == 0:
                    start()
            if "act" in before:
                before["act"](act)

            def body(i, final=False):
                def next_split(b):
                    if turns > 1 and b < lag:
                        split(i, per_turn - lag + b)
                    elif not final:
                        split(i + 1, b - lag)
                evacuate["act"](act, i, lambda b: act.wait_ge(mm_done, ready(i, b)), bank_free, next_split)
            turn_loop(act, body, 0, turns - 1)
            body(turns - 1, True)
            act.wait_ge(bank_free, per_turn * (turns + 1))
            if "act" in after:
                after["act"](act)

        @block.vector
        def _(dve):
            if "dve" in before:
                before["dve"](dve)
            if whole is not None:
                for k in range(whole.shape[1]):
                    dve.wait_ge(x_high, k + 1)
                    low_half(nc.vector, rhs[0].low[:, k, :], whole[:, k, :], rhs[0].high[:, k, :]).then_inc(x_low, 1)
            if "dve" in evacuate:
                turn_loop(dve, lambda i: evacuate["dve"](dve, i, lambda b: dve.wait_ge(mm_done, ready(i, parts * b + parts - 1)), bank_free))
                dve.wait_ge(bank_free, per_turn * (turns + 1))
            if "dve" in after:
                after["dve"](dve)
    ctx.__exit__()


ALL = (slice(None), slice(None), slice(None))


def columns(w, turns, per_turn, col0=0):
    view = w.rearrange("(k p) n -> p k n", p=P)

    def source(i, b):
        at = i * (per_turn * P) + (col0 + b * P)
        return [(ALL, view[:, :, bass.ds(at, P)])]
    return Weights(turns, per_turn, source, view.shape[1])


def tile_of(buf, i, per_turn, b):
    return buf[:, i * per_turn + b, :]


def project_copy(c, w, dest, ahead=None, before={}, after={}):
    nc = c.nc

    def act(eng, i, wait_tile, bank_free, split):
        for b in range(w.per_turn):
            wait_tile(b)
            nc.scalar.activation(tile_of(dest, i, w.per_turn, b), c.ps[:, b, :], ACT.Copy).then_inc(bank_free, 1)
            split(b)
    project(c, w, {"act": act}, ahead=ahead, before=before, after=after)


def project_add(c, w, dest, rhs, whole=None, ahead=None, before={}):
    nc = c.nc

    def dve(eng, i, wait_tile, bank_free):
        for b in range(w.per_turn // w.parts):
            wait_tile(b)
            d = tile_of(dest, i, w.per_turn // w.parts, b)
            nc.vector.tensor_tensor(d, d, c.ps[:, b, :], ALU.add).then_inc(bank_free, w.parts)
    project(c, w, {"dve": dve}, rhs, ahead, whole, before)


def project_swiglu(c, w, dest, ahead=None):
    nc = c.nc
    with c.stage() as ctx:
        gate = ctx.sbuf("gate", [P, 2, T])
        gated, made, dest_high, dest_low = (ctx.sem(n) for n in ("gated", "made", "dest_high", "dest_low"))

        def act(eng, i, wait_tile, bank_free, split):
            for j in range(2):
                wait_tile(2 * j)
                eng.wait_ge(dest_low, i * 2 + (j + 1))
                nc.scalar.activation(gate[:, j, :], c.ps[:, 2 * j, :], ACT.Silu).then_inc(gated, 1)
                split(2 * j)
                eng.wait_ge(made, i * 2 + (j + 1))
                high_half(nc, tile_of(dest.high, i, 2, j), gate[:, j, :]).then_inc(dest_high, 1)
                split(2 * j + 1)

        def dve(eng, i, wait_tile, bank_free):
            for j in range(2):
                wait_tile(2 * j + 1)
                eng.wait_ge(gated, i * 2 + (j + 1))
                nc.vector.tensor_tensor(gate[:, j, :], gate[:, j, :], c.ps[:, 2 * j + 1, :], ALU.mult).then_inc(made, 1)
                eng.wait_ge(made, i * 2 + (j + 1))
                eng.sem_inc(bank_free, 2)
                eng.wait_ge(dest_high, i * 2 + (j + 1))
                low_half(nc.vector, tile_of(dest.low, i, 2, j), gate[:, j, :], tile_of(dest.high, i, 2, j)).then_inc(dest_low, 1)

        project(c, w, {"act": act, "dve": dve}, ahead=ahead, before={"dve": lambda eng: eng.sem_inc(dest_low, 2)},
                after={"dve": lambda eng: eng.wait_ge(dest_low, 2 * w.turns + 2)})


def project_rope(c, w, tables, scale, dest, ahead=None):
    nc = c.nc
    per_turn = w.per_turn
    swap, cos, sin = tables
    with c.stage() as ctx:
        raw = ctx.sbuf("raw", [P, per_turn, T])
        part = ctx.sbuf("part", [P, per_turn, 2, T])
        copied, swapped, scaled = ctx.sem("copied"), ctx.sem("swapped"), ctx.sem("scaled")

        def act(eng, i, wait_tile, bank_free, split):
            for b in range(per_turn):
                wait_tile(b)
                nc.scalar.activation(raw[:, b, :], c.ps[:, b, :], ACT.Copy).then_inc(copied, 1)
                split(b)

        def pe(eng, i, b):
            eng.wait_ge(copied, i * per_turn + (b + 1))
            nc.tensor.matmul(c.ps[:, 4 + b, :], swap[:, :], raw[:, b, :], start=True, stop=True).then_inc(swapped, 1)

        def dve(eng, i, wait_tile, bank_free):
            for b in range(per_turn):
                eng.wait_ge(swapped, i * per_turn + (b + 1))
                nc.vector.scalar_tensor_tensor(part[:, b, 0, :], c.ps[:, b, :], scale, cos[:, :], ALU.mult, ALU.mult).then_inc(scaled, 1)
                nc.vector.scalar_tensor_tensor(part[:, b, 1, :], c.ps[:, 4 + b, :], scale, sin[:, :], ALU.mult, ALU.mult).then_inc(scaled, 1)
                eng.wait_ge(scaled, i * (2 * per_turn) + (2 * b + 2))
                nc.vector.tensor_tensor(tile_of(dest, i, per_turn, b), part[:, b, 0, :], part[:, b, 1, :], ALU.add).then_inc(bank_free, 1)
        project(c, w, {"act": act, "pe": pe, "dve": dve}, ahead=ahead)


ROWS_N = 256


class RowWeights:
    per_turn = 2

    def __init__(self, w, outputs):
        self.view = w.rearrange("(k p) n -> p k n", p=P)
        pieces = [(col + at, min(ROWS_N, n - at), dest[:, :, at:at + min(ROWS_N, n - at)], func)
                  for col, n, dest, func in outputs for at in range(0, n, ROWS_N)]
        self.chunks = []
        for col, n, dest, func in pieces:
            at = self.columns(-1) if self.chunks else ROWS_N
            if at + n > ROWS_N:
                self.chunks.append([])
                at = 0
            self.chunks[-1].append((at, col, n, dest, func))
        self.base = None

    def columns(self, j):
        return sum(n for _, _, n, _, _ in self.chunks[j])

    def ring_slots(self, b):
        return (2 * b, 2 * b + 1)

    def slot(self, buf, j):
        return buf[:, j % 2, 0:KD * self.columns(j)].rearrange("p (k n) -> p k n", k=KD)

    def whole(self, c):
        return c.w_ring[:, :, :].rearrange("p (s two) n -> p s (two n)", two=2)

    def load(self, c, sp, i, b):
        j = 2 * i + b
        if j < len(self.chunks):
            for at, col, n, _, _ in self.chunks[j]:
                sp.dma_start(self.slot(self.whole(c), j)[:, :, at:at + n], self.view[:, :, col:col + n]).then_inc(c.rows_in[b].sem, 16)

    def loaded(self, j):
        return self.base[j % 2] + 16 * sum(len(self.chunks[x]) for x in range(j % 2, j + 1, 2))

    def count(self, c):
        if self.base is not None:
            return False
        self.base = [c.rows_in[b].n for b in range(2)]
        for b in range(2):
            c.rows_in[b].n += 16 * sum(len(x) for x in self.chunks[b::2])
        return True


def project_rows(c, w, beside={}, ahead=None):
    nc = c.nc
    n_chunks = len(w.chunks)
    parts = TT * sum(len(x) - 1 for x in w.chunks)
    fresh = w.count(c)
    if ahead is not None:
        ahead.count(c)
    ctx = c.stage()
    high, low, mm_done, copied, part_copied = (ctx.sem(n) for n in ("rows_high", "rows_low", "rows_done", "rows_copied", "rows_part_copied"))
    w_high, w_low = c.halves(ctx, "w_rows", [P, 2, KD * ROWS_N])
    part = lambda buf, j: buf[:, j % 2, 0:KD * w.columns(j)]
    with nc.Block() as block:

        @block.sync
        def _(sp):
            for j in range(n_chunks):
                if j >= 2:
                    sp.wait_ge(low, j - 1)
                if j >= 2 or fresh:
                    w.load(c, sp, j // 2, j % 2)
            if ahead is not None:
                sp.wait_ge(low, n_chunks)
                for b in range(ahead.per_turn):
                    ahead.load(c, sp, 0, b)

        @block.gpsimd
        def _(pool):
            for j in range(n_chunks):
                pool.wait_ge(high, j + 1)
                low_half(nc.gpsimd, part(w_low, j), part(w.whole(c), j), part(w_high, j)).then_inc(low, 1)

        @block.tensor
        def _(pe):
            for j in range(n_chunks):
                pe.wait_ge(low, j + 1)
                for t in range(TT):
                    if j >= 1:
                        pe.wait_ge(copied, TT * (j - 1) + t + 1)
                    for k in range(KD):
                        tokens = slice(t * P, (t + 1) * P)
                        mm = product(nc, c.ps[:, t, 0:w.columns(j)], c.h.high[:, k, tokens], c.h.low[:, k, tokens],
                                     w.slot(w_high, j)[:, k, :], w.slot(w_low, j)[:, k, :], start=(k == 0), stop=(k == KD - 1))
                    mm.then_inc(mm_done, 1)
                    if "pe" in beside:
                        beside["pe"](pe, TT * j + t)

        @block.scalar
        def _(act):
            def split(j):
                if j < n_chunks:
                    act.wait_ge(c.rows_in[j % 2].sem, w.loaded(j))
                    if j >= 2:
                        act.wait_ge(mm_done, TT * (j - 1))
                    high_half(nc, part(w_high, j), part(w.whole(c), j)).then_inc(high, 1)

            split(0)
            split(1)
            if "act_first" in beside:
                beside["act_first"](act)
            for j in range(n_chunks):
                for t in range(TT):
                    act.wait_ge(mm_done, TT * j + t + 1)
                    for x, (at, _, n, dest, func) in enumerate(w.chunks[j]):
                        copy = nc.scalar.activation(dest[:, t, :], c.ps[:, t, at:at + n], func)
                        copy.then_inc(copied if x == len(w.chunks[j]) - 1 else part_copied, 1)
                    if "act" in beside:
                        beside["act"](act, TT * j + t)
                split(j + 2)
            act.wait_ge(copied, TT * n_chunks)
            if parts > 0:
                act.wait_ge(part_copied, parts)

        if "dve" in beside:
            block.vector(beside["dve"])
    ctx.__exit__()


def ffn_weights(w_gate, w_up, w_down):
    gate, up, down = (w.rearrange("(k p) n -> p k n", p=P) for w in (w_gate, w_up, w_down))

    def pair(i, b):
        return [(ALL, (gate, up)[b % 2][:, :, bass.ds(i * (2 * P) + b // 2 * P, P)])]

    parts = [KD, KF // 3, KF // 3]

    def part(i, b):
        at = sum(parts[:b])
        return [(ALL, down[:, at:at + parts[b], bass.ds(i * P, P)])]
    return Weights(KF // 2, 4, pair), Weights(KD, len(parts), part, parts, parts=len(parts))


def ffn(c, gain, weights, ahead=None):
    w_gate_up, w_down = weights
    with c.stage() as ctx:
        a = c.halves(ctx, "a", [P, KF, T])
        with c.stage() as inner:
            c.h = c.halves(inner, "h", [P, KD, T])
            rms_norm(c, gain, c.h)
            project_swiglu(c, w_gate_up, a, ahead=w_down)
        project_add(c, w_down, c.xT, a, ahead=ahead)


def store_normed(c, gain, out):
    nc = c.nc
    with c.stage() as ctx:
        normed = ctx.sbuf("normed", [P, KD, T])
        rms_norm(c, gain, normed)
        rows = ctx.sbuf("rows", [P, TT, D])
        transposed, copied, stored = ctx.sem("transposed"), ctx.sem("copied"), ctx.sem("stored")
        out_rows = out[0].rearrange("(t p) d -> p t d", p=P)
        with nc.Block() as block:

            @block.tensor
            def _(pe):
                for t in range(TT):
                    for h in range(2):
                        for k in range(4):
                            tr = nc.tensor.transpose(c.ps[:, 2 * t + h, k * P:(k + 1) * P], normed[:, 4 * h + k, t * P:(t + 1) * P], c.ident[:, :])
                        tr.then_inc(transposed, 1)

            @block.scalar
            def _(act):
                for t in range(TT):
                    for h in range(2):
                        act.wait_ge(transposed, 2 * t + h + 1)
                        nc.scalar.activation(rows[:, t, h * T:(h + 1) * T], c.ps[:, 2 * t + h, :], ACT.Copy).then_inc(copied, 1)

            @block.sync
            def _(sp):
                for t in range(TT):
                    sp.wait_ge(copied, 2 * t + 2)
                    sp.dma_start(out_rows[:, t, :], rows[:, t, :]).then_inc(stored, 16)
                sp.wait_ge(stored, 16 * TT)


def attention(c, turns, units, scale, staging, sinks, lag=3):
    nc = c.nc
    steps = [(u, t) for u in range(len(units)) for t in range(TT)]
    n_steps, n_units, n_sinks = len(steps), len(units), len(sinks)
    s_banks, p_bufs = (0, 1, 2), 4
    pt_bank = 3
    act_tiles, dve_tiles = (1, 3), (0, 2)
    movers = len(act_tiles)
    slots = sorted(staging)
    last_user = {s: max(u for u in range(n_units) if s in units[u]["slots"]) for s in slots}
    width = [P * (t + 1) for t in range(TT)]
    with c.stage() as ctx:
        probs = ctx.sbuf("probs", [P, p_bufs, T])
        probsT = ctx.sbuf("probsT", [P, 2, TT, T])
        stat = ctx.sbuf("stat", [P, 3, p_bufs])
        top, total, inverse = stat[:, 0, :], stat[:, 1, :], stat[:, 2, :]
        scored, topped, exped, summed, normed = (ctx.sem(x) for x in ("scored", "topped", "exped", "inverted", "normed"))
        p_used, pt_act, pt_dve, pv_done, o_read = (ctx.sem(x) for x in ("p_used", "pt_act", "pt_dve", "pv_done", "o_read"))
        staged = {s: ctx.sem(f"staged{s}") for s in slots}
        scaled = ctx.sem("scaled")
        copies = {s: len(staging[s](0)) for s in slots}

        def loop(eng, body):
            with eng.Fori(0, turns) as i:
                body(i)

        def moved(eng, i, u, t):
            tiles, sem = (act_tiles, pt_act) if t in act_tiles else (dve_tiles, pt_dve)
            eng.wait_ge(sem, i * (n_units * movers) + (u * movers + tiles.index(t) + 1))

        with nc.Block() as block:

            @block.sync
            def _(sp):
                sp.sem_inc(pv_done, n_units)

                def body(i):
                    for s in sorted(slots, key=lambda s: last_user[s]):
                        hold(sp, pv_done, i * n_units + (last_user[s] + 1), c.sp_tick)
                        for dest, source in staging[s](i):
                            sp.dma_start(dest, source).then_inc(staged[s], 16)
                loop(sp, body)

            @block.tensor
            def _(pe):
                def score(i, s):
                    u, t = steps[s]
                    unit = units[u]
                    if t == 0:
                        for slot in unit["slots"]:
                            pe.wait_ge(staged[slot], i * (16 * copies[slot]) + 16 * copies[slot])
                    if s >= len(s_banks):
                        pe.wait_ge(exped, i * n_steps + (s - len(s_banks) + 1))
                    w, bank = width[t], s_banks[s % len(s_banks)]
                    out, q = c.ps[:, bank, 0:w], slice(t * P, (t + 1) * P)
                    nc.tensor.matmul(out, unit["q"][:, q], unit["k"](i)[:, 0:w], start=True, stop=False)
                    if "q2" in unit:
                        nc.tensor.matmul(out, unit["q2"][:, q], unit["k2"](i)[:, 0:w], start=False, stop=False)
                    if "bias" in unit:
                        nc.tensor.matmul(out, unit["ones"], unit["bias"](i)[:, 0:w], start=False, stop=False)
                    if unit["mask"] is not None:
                        mm = nc.tensor.matmul(out, c.ident[:, :], unit["mask"](t), start=False, stop=True)
                    else:
                        mm = nc.tensor.matmul(c.ps[:, bank, w - P:w], c.ident[:, :], c.causal[:, :], start=False, stop=True)
                    mm.then_inc(scored, 1)

                def transposes(i, s):
                    u, t = steps[s]
                    pe.wait_ge(normed, i * n_steps + (s + 1))
                    moved(pe, i, u, t)
                    for j in range(t + 1):
                        tr = nc.tensor.transpose(c.ps[:, pt_bank + t, j * P:(j + 1) * P], probs[:, s % p_bufs, j * P:(j + 1) * P], c.ident[:, :])
                    tr.then_inc(p_used, 1)
                    if t == 1 and u >= 1:
                        weigh(i, u - 1)

                def weigh(i, u):
                    unit = units[u]
                    for t in (act_tiles[-1], dve_tiles[-1]):
                        moved(pe, i, u + 1, t)
                    if unit["first"]:
                        done = sum(1 for x in sinks if x < u)
                        pe.wait_ge(o_read, i * n_sinks + (done + n_sinks))
                    for j in range(TT):
                        mm = nc.tensor.matmul(unit["out"][:, j * P:T], unit["v"](j), probsT[:, u % 2, j, j * P:T],
                                              start=unit["first"] and j == 0, stop=unit["last"] and j == TT - 1 and "add" not in unit,
                                              skip_group_check=True)
                    if "add" in unit:
                        mm = nc.tensor.matmul(unit["out"], unit["add"], unit["add_to"](i), start=False, stop=unit["last"], skip_group_check=True)
                    mm.then_inc(pv_done, 1)

                pe.sem_inc(o_read, n_sinks)
                pe.sem_inc(pt_act, movers)
                pe.sem_inc(pt_dve, movers)

                def body(i):
                    for s in range(n_steps + lag):
                        if s < n_steps:
                            score(i, s)
                        if s >= lag:
                            transposes(i, s - lag)
                    weigh(i, n_units - 1)
                loop(pe, body)

            def move(eng, i, s, sem, copy):
                u, t = steps[s]
                eng.wait_ge(p_used, i * n_steps + (s + 1))
                if t in (act_tiles[0], dve_tiles[0]):
                    eng.wait_ge(pv_done, i * n_units + (n_units + u - 1))
                copy(probsT[:, u % 2, 0:t + 1, t * P:(t + 1) * P],
                     c.ps[:, pt_bank + t, 0:width[t]].rearrange("p (j q) -> p j q", q=P)).then_inc(sem, 1)

            @block.scalar
            def _(act):
                def read_out(i, u):
                    act.wait_ge(pv_done, i * n_units + (n_units + u + 1))
                    nc.scalar.activation(sinks[u](i), units[u]["sum"], ACT.Copy).then_inc(o_read, 1)

                def body(i):
                    for s in range(n_steps + lag):
                        if s < n_steps:
                            u, t = steps[s]
                            act.wait_ge(topped, i * n_steps + (s + 1))
                            if s >= p_bufs:
                                act.wait_ge(p_used, i * n_steps + (s - p_bufs + 1))
                            nc.scalar.activation(probs[:, s % p_bufs, 0:width[t]], c.ps[:, s_banks[s % len(s_banks)], 0:width[t]], ACT.Exp,
                                                 bias=top[:, s % p_bufs:s % p_bufs + 1], scale=scale,
                                                 accum_out=total[:, s % p_bufs:s % p_bufs + 1]).then_inc(exped, 1)
                        if s >= lag:
                            u, t = steps[s - lag]
                            if t in act_tiles:
                                move(act, i, s - lag, pt_act, lambda d, x: nc.scalar.activation(d, x, ACT.Copy))
                            if t == 2 and u >= 1 and u - 1 in sinks:
                                read_out(i, u - 1)
                    read_out(i, n_units - 1)
                loop(act, body)
                act.wait_ge(o_read, n_sinks * (turns + 1))

            @block.vector
            def _(dve):
                def body(i):
                    def normalise(s):
                        u, t = steps[s]
                        dve.wait_ge(exped, i * n_steps + (s + 1))
                        one = slice(s % p_bufs, s % p_bufs + 1)
                        nc.vector.reciprocal(inverse[:, one], total[:, one]).then_inc(summed, 1)
                        dve.wait_ge(summed, i * n_steps + (s + 1))
                        p = probs[:, s % p_bufs, 0:width[t]]
                        gate = units[u]["gate"](i, t) if units[u].get("gate") else None
                        if gate is None:
                            op = nc.vector.tensor_scalar(p, p, inverse[:, one], None, ALU.mult)
                        else:
                            op = nc.vector.tensor_scalar(p, p, inverse[:, one], gate, ALU.mult, ALU.mult)
                        op.then_inc(normed, 1)

                    for s in range(n_steps + lag):
                        if s < n_steps:
                            u, t = steps[s]
                            dve.wait_ge(scored, i * n_steps + (s + 1))
                            one = top[:, s % p_bufs:s % p_bufs + 1]
                            top_op = nc.vector.tensor_reduce(one, c.ps[:, s_banks[s % len(s_banks)], 0:width[t]], AX.X, ALU.max, negate=True)
                            if scale == 1.0:
                                top_op.then_inc(topped, 1)
                            else:
                                top_op.then_inc(scaled, 1)
                                dve.wait_ge(scaled, i * n_steps + (s + 1))
                                nc.vector.tensor_scalar(one, one, scale, None, ALU.mult).then_inc(topped, 1)
                        if 1 <= s <= n_steps:
                            normalise(s - 1)
                        if s >= lag and steps[s - lag][1] in dve_tiles:
                            move(dve, i, s - lag, pt_dve, nc.vector.tensor_copy)
                loop(dve, body)


def head_norm_beside_rows(c, w, buf, gains, ahead):
    nc = c.nc
    tiles, ring = buf.shape[1], 4
    with c.stage() as ctx:
        squares = ctx.sbuf("squares", [P, ring, T])
        rstd = ctx.sbuf("rstd", [P, ring, T])
        squared, summed, inverted, rooted, normed = (ctx.sem(n) for n in ("squared", "summed", "inverted", "rooted", "normed"))
        units = TT * len(w.chunks)
        per = -(-tiles // units)
        of = lambda n: range(n * per, min((n + 1) * per, tiles)) if n >= 0 else ()

        def square(act, n):
            if n >= ring:
                act.wait_ge(summed, n - ring + 1)
            nc.scalar.activation(squares[:, n % ring, :], buf[:, n, :], ACT.Square).then_inc(squared, 1)

        def pe_part(pe, unit):
            for n in of(unit):
                pe.wait_ge(squared, n + 1)
                if n >= ring:
                    pe.wait_ge(rooted, n - ring + 1)
                nc.tensor.matmul(c.ps[:, 4 + n % 4, :], c.ones[:, :], squares[:, n % ring, :], start=True, stop=True).then_inc(summed, 1)

        def act_first(act):
            for n in range(ring):
                square(act, n)

        def act_part(act, unit):
            for n in of(unit):
                act.wait_ge(summed, n + 1)
                if n >= ring:
                    act.wait_ge(normed, n - ring + 1)
                nc.scalar.activation(rstd[:, n % ring, :], c.ps[:, 4 + n % 4, :], ACT.Sqrt, bias=c.eps[:, 0:1], scale=1.0 / P).then_inc(rooted, 1)
                if n + ring < tiles:
                    square(act, n + ring)

        def dve_part(dve):
            def apply(n):
                dve.wait_ge(inverted, n + 1)
                nc.vector.scalar_tensor_tensor(buf[:, n, :], buf[:, n, :], gains[:, n:n + 1], rstd[:, n % ring, :], ALU.mult, ALU.mult).then_inc(normed, 1)

            for n in range(tiles):
                dve.wait_ge(rooted, n + 1)
                nc.vector.reciprocal(rstd[:, n % ring, :], rstd[:, n % ring, :]).then_inc(inverted, 1)
                if n >= 1:
                    apply(n - 1)
            apply(tiles - 1)
            dve.wait_ge(normed, tiles)
        project_rows(c, w, {"pe": pe_part, "act_first": act_first, "act": act_part, "dve": dve_part}, ahead)


def fox_attention(c, w_in, f_bias, q_gain, k_gain, qkT, ahead):
    nc = c.nc
    with c.stage() as ctx:
        v = ctx.sbuf("v", [P, TT, FOX_H * P])
        f = ctx.sbuf("f", [P, TT, FOX_H])
        gains = ctx.sbuf("gains", [P, 2 * FOX_H])
        pair = ctx.sbuf("pair", [P, 2])
        bias = ctx.sbuf("bias", [P, FOX_H])
        minus_tri = ctx.sbuf("minus_tri", [P, T])
        cum = ctx.sbuf("cum", [FOX_H, T])
        cum_rows = ctx.sbuf("cum_rows", [1, FOX_H, T])
        g_in, g_set = ctx.sem("gains_in"), ctx.sem("gains_set")
        with nc.Block() as block:

            @block.sync
            def _(sp):
                sp.dma_start(pair[:, 0:1], q_gain.rearrange("(p a) -> p a", a=1)).then_inc(g_in, 16)
                sp.dma_start(pair[:, 1:2], k_gain.rearrange("(p a) -> p a", a=1)).then_inc(g_in, 16)
                sp.dma_start(bias[:, :], f_bias.partition_broadcast(P)).then_inc(g_in, 16)
                sp.dma_start(minus_tri[:, :], c.ins["c_minus_tri"]).then_inc(g_in, 16)
                sp.dma_start(c.xT[:, :, :], c.x_dram).then_inc(c.x_back, 16)
                sp.wait_ge(g_in, 64)

            @block.vector
            def _(dve):
                dve.wait_ge(g_in, 64)
                nc.vector.tensor_scalar(gains[:, 0:FOX_H], pair[:, 0:1].to_broadcast([P, FOX_H]), float(P) ** -0.5, None, ALU.mult).then_inc(g_set, 1)
                nc.vector.tensor_copy(gains[:, FOX_H:], pair[:, 1:2].to_broadcast([P, FOX_H])).then_inc(g_set, 1)
                dve.wait_ge(g_set, 2)
        at = SSM_W + 2 * FOX_H * P
        w_rows = RowWeights(w_in, [(at, FOX_H * P, v, ACT.Copy), (at + FOX_H * P, FOX_H, f, ACT.Copy)])
        head_norm_beside_rows(c, w_rows, qkT, gains, ahead)
        forget_sums(c, f, bias, minus_tri, cum, cum_rows)
        per_turn = FOX_H // 2
        slots = [(ctx.sbuf(f"q{s}", [P, T]), ctx.sbuf(f"v{s}", [P, TT, P])) for s in range(per_turn)]

        def stage(s):
            q, vv = slots[s]
            return lambda i: [(q[:, :], tile_of(qkT, i, per_turn, s)), (vv[:, :, :], v[:, :, bass.ds(i * (per_turn * P) + s * P, P)])]

        def head(s):
            q, vv = slots[s]
            return dict(q=q, k=lambda i: tile_of(qkT, i, per_turn, s + FOX_H), v=lambda j: vv[:, j, :], mask=None, slots=[s],
                        ones=c.ones[0:1, :], bias=lambda i: tile_of(cum_rows, i, per_turn, s), out=c.ps[:, 7, :], sum=c.ps[:, 7, :], first=True, last=True)
        attention(c, FOX_H // per_turn, [head(s) for s in range(per_turn)], 1.0, {s: stage(s) for s in range(per_turn)},
                  {s: (lambda i, s=s: tile_of(qkT, i, per_turn, s)) for s in range(per_turn)})


def forget_sums(c, f, bias, minus_tri, cum, cum_rows):
    nc = c.nc
    with c.stage() as ctx:
        z, e, low = (ctx.sbuf(n, [P, TT, FOX_H]) for n in ("z", "e", "low"))
        zed, exped, logged, ready, summed, copied, moved = (ctx.sem(n) for n in ("zed", "exped", "logged", "ready", "summed", "copied", "moved"))
        with nc.Block() as block:

            @block.vector
            def _(dve):
                step = Chain(dve, c.dve_step)
                step(nc.vector.tensor_tensor(z[:, :, :], f[:, :, :], bias[:, :].unsqueeze(1).to_broadcast([P, TT, FOX_H]), ALU.add))
                nc.vector.tensor_scalar(low[:, :, :], z[:, :, :], 0.0, None, ALU.min).then_inc(zed, 1)
                dve.wait_ge(logged, 1)
                nc.vector.tensor_tensor(z[:, :, :], low[:, :, :], e[:, :, :], ALU.subtract).then_inc(ready, 1)
                dve.wait_ge(ready, 1)

            @block.scalar
            def _(act):
                act.wait_ge(zed, 1)
                nc.scalar.activation(e[:, :, :], z[:, :, :], ACT.Abs).then_inc(exped, 1)
                act.wait_ge(exped, 1)
                nc.scalar.activation(e[:, :, :], e[:, :, :], ACT.Exp, scale=-1.0).then_inc(exped, 1)
                act.wait_ge(exped, 2)
                nc.scalar.activation(e[:, :, :], e[:, :, :], ACT.Ln, bias=1.0).then_inc(logged, 1)
                act.wait_ge(summed, 1)
                nc.scalar.activation(cum[:, :], c.ps[0:FOX_H, 0, :], ACT.Copy).then_inc(copied, 1)

            @block.tensor
            def _(pe):
                pe.wait_ge(ready, 1)
                for t in range(TT):
                    mm = nc.tensor.matmul(c.ps[0:FOX_H, 0, t * P:T], z[:, t, :], minus_tri[:, 0:T - t * P],
                                          start=(t == 0), stop=(t == TT - 1), skip_group_check=True)
                mm.then_inc(summed, 1)

            @block.sync
            def _(sp):
                sp.wait_ge(copied, 1)
                sp.dma_start(cum_rows[0:1, :, :], cum[:, :]).then_inc(moved, 16)
                sp.wait_ge(moved, 16)


def ssm(c, A, w_u, w_qk, qkT, ygT):
    nc = c.nc
    with c.stage() as ctx:
        uT = ygT
        project_copy(c, w_u, uT, ahead=w_qk)
        PM = [P, PAIRS]
        names = ("ar", "ai", "dt", "mag", "th", "turn", "cos", "sin", "lre", "lim", "nr", "den", "cre", "cim", "t0", "t1", "half_pi")
        m = {n: ctx.sbuf(n, PM) for n in names}
        powers = ctx.sbuf("powers", [P, 9, 3, PAIRS])
        S = [ctx.sbuf(n, [P, PAIRS, T]) for n in ("s_re", "s_im")]
        b_in, tmp = ([S[x][:, :, y * SSM_H:(y + 1) * SSM_H] for x in range(2)] for y in range(2))
        wide = [S[x][:, :, P:2 * P] for x in range(2)]
        bT = [ctx.sbuf(n, [P, PAIRS, P]) for n in ("bT_re", "bT_im")]
        cT = [c.xT[:, 4 * x:4 * x + 4, :].rearrange("p k (j n) -> p (k j) n", n=P) for x in range(2)]
        skip = ctx.sbuf("skip", [P, SSM_T])
        param_in, zeroed, c_in = ctx.sem("param_in"), ctx.sem("zeroed"), ctx.sem("c_in")
        mag_set, angle, trig, b_wide, b_turned, b_moved, c_turned, c_moved, b_free = (
            ctx.sem(n) for n in ("mag_set", "angle", "trig", "b_wide", "b_turned", "b_moved", "c_turned", "c_moved", "b_free"))
        by_state = lambda a: a.rearrange("(j two) s -> (two s) j", two=2)
        dt2 = A["ssm_log_step"][0].rearrange("(j two) -> two j", two=2)
        with nc.Block() as block:

            @block.sync
            def _(sp):
                sp.dma_start(m["ar"][:, :], by_state(A["ssm_a_re"][0]), allow_slow_non_contiguous=True).then_inc(param_in, 16)
                sp.dma_start(m["ai"][:, :], by_state(A["ssm_a_im"][0]), allow_slow_non_contiguous=True).then_inc(param_in, 16)
                for two in range(2):
                    sp.dma_start(m["dt"][two * SSM_S:(two + 1) * SSM_S, :], dt2[two].partition_broadcast(SSM_S), allow_slow_non_contiguous=True).then_inc(param_in, 16)
                sp.dma_start(skip[:, :], A["ssm_d"][0].rearrange("(t p) -> p t", p=P), allow_slow_non_contiguous=True).then_inc(param_in, 16)
                for x, name in enumerate(("ssm_b_re", "ssm_b_im")):
                    sp.dma_start(b_in[x][:, :, :], A[name][0].rearrange("(j two) s h -> (two s) j h", two=2)).then_inc(param_in, 16)
                sp.dma_start(c.x_dram, c.xT[:, :, :]).then_inc(c.x_saved, 16)
                sp.wait_ge(param_in, 16 * 7)
                sp.wait_ge(c.x_saved, 16)
                sp.wait_ge(zeroed, 4)
                for x, name in enumerate(("ssm_c_re", "ssm_c_im")):
                    view = A[name][0].rearrange("(t g) h s -> g h t s", g=8)
                    for g in range(8):
                        at = g % 2 * SSM_S
                        sp.dma_start(wide[x][g * SSM_H:(g + 1) * SSM_H, g // 2::4, at:at + SSM_S], view[g]).then_inc(c_in, 16)
                sp.wait_ge(c_in, 16 * 16)

            @block.gpsimd
            def _(pool):
                for x in range(2):
                    nc.gpsimd.memset(wide[x][:, :, :], 0.0).then_inc(zeroed, 1)
                nc.gpsimd.memset(m["half_pi"][:, :], math.pi / 2).then_inc(zeroed, 1)
                pool.wait_ge(b_moved, 8)
                for x in range(2):
                    nc.gpsimd.memset(wide[x][:, :, :], 0.0).then_inc(b_free, 1)
                pool.wait_ge(b_free, 2)
                pool.sem_inc(zeroed, 1)

            @block.scalar
            def _(act):
                act.wait_ge(param_in, 16 * 7)
                nc.scalar.activation(m["dt"][:, :], m["dt"][:, :], ACT.Exp).then_inc(mag_set, 1)
                act.wait_ge(angle, 1)
                nc.scalar.activation(m["mag"][:, :], m["mag"][:, :], ACT.Exp).then_inc(trig, 1)
                act.wait_ge(angle, 2)
                act.wait_ge(zeroed, 3)
                nc.scalar.activation(m["sin"][:, :], m["th"][:, :], ACT.Sin).then_inc(trig, 1)
                nc.scalar.activation(m["turn"][:, :], m["th"][:, :], ACT.Abs).then_inc(trig, 1)
                act.wait_ge(trig, 3)
                nc.scalar.activation(m["cos"][:, :], m["turn"][:, :], ACT.Sin, bias=m["half_pi"][:, 0:1], scale=-1.0).then_inc(trig, 1)
                act.wait_ge(trig, 4)
                for n in range(8):
                    x, q = n // 4, n % 4
                    act.wait_ge(b_turned, n + 1)
                    nc.scalar.activation(bT[x][:, 4 * q:4 * q + 4, :], c.ps[:, n, :], ACT.Copy).then_inc(b_moved, 1)
                for n in range(8):
                    x, q = n // 4, n % 4
                    act.wait_ge(c_turned, n + 1)
                    nc.scalar.activation(cT[x][:, 4 * q:4 * q + 4, :], c.ps[:, n, :], ACT.Copy, scale=(1.0, -1.0)[x]).then_inc(c_moved, 1)
                act.wait_ge(c_moved, 8)

            @block.vector
            def _(dve):
                v = nc.vector
                step = Chain(dve, c.dve_step)
                tt = lambda o, a, b, op: step(v.tensor_tensor(m[o][:, :], m[a][:, :], m[b][:, :], op))
                dve.wait_ge(param_in, 16 * 7)
                dve.wait_ge(mag_set, 1)
                step(v.tensor_tensor(m["th"][:, :], m["ai"][:, :], m["dt"][:, :], ALU.mult))
                v.tensor_tensor(m["mag"][:, :], m["ar"][:, :], m["dt"][:, :], ALU.mult).then_inc(angle, 1)
                step(v.tensor_scalar(m["turn"][:, :], m["th"][:, :], 1.0 / (2 * math.pi), 12582912.0, ALU.mult, ALU.add))
                step(v.tensor_scalar(m["turn"][:, :], m["turn"][:, :], 12582912.0, None, ALU.subtract))
                for part in (6.28125, 0.0019350051879882812, 3.019915981956753e-07):
                    step(v.scalar_tensor_tensor(m["th"][:, :], m["turn"][:, :], -part, m["th"][:, :], ALU.mult, ALU.add))
                v.tensor_scalar(m["th"][:, :], m["th"][:, :], 3.1415925, -3.1415925, ALU.min, ALU.max).then_inc(angle, 1)
                dve.wait_ge(trig, 4)
                tt("lre", "mag", "cos", ALU.mult)
                tt("lim", "mag", "sin", ALU.mult)
                step(v.tensor_scalar(m["nr"][:, :], m["lre"][:, :], 1.0, None, ALU.subtract))
                tt("den", "ar", "ar", ALU.mult)
                tt("t0", "ai", "ai", ALU.mult)
                tt("den", "den", "t0", ALU.add)
                step(v.reciprocal(m["den"][:, :], m["den"][:, :]))
                tt("t0", "nr", "ar", ALU.mult)
                tt("t1", "lim", "ai", ALU.mult)
                tt("t0", "t0", "t1", ALU.add)
                tt("cre", "t0", "den", ALU.mult)
                tt("t0", "lim", "ar", ALU.mult)
                tt("t1", "nr", "ai", ALU.mult)
                tt("t0", "t0", "t1", ALU.subtract)
                tt("cim", "t0", "den", ALU.mult)
                dve.wait_ge(zeroed, 3)
                spread = lambda n: m[n][:, :].unsqueeze(2).to_broadcast([P, PAIRS, SSM_H])
                for x, (first, second, op) in enumerate(((("cre", 0), ("cim", 1), ALU.subtract), (("cre", 1), ("cim", 0), ALU.add))):
                    step(v.tensor_tensor(tmp[0][:, :, :], spread(first[0]), b_in[first[1]][:, :, :], ALU.mult))
                    step(v.tensor_tensor(tmp[1][:, :, :], spread(second[0]), b_in[second[1]][:, :, :], ALU.mult))
                    for two in range(2):
                        rows = slice(two * SSM_S, (two + 1) * SSM_S)
                        for q in range(4):
                            at = (2 * q + two) * SSM_H
                            step(v.tensor_tensor(wide[x][rows, q::4, at:at + SSM_H], tmp[0][rows, q::4, :], tmp[1][rows, q::4, :], op))
                    dve.sem_inc(b_wide, 1)
                for lv in range(9):
                    re, im, neg = (powers[:, lv, z, :] for z in range(3))
                    if lv == 0:
                        step(v.tensor_copy(re, m["lre"][:, :]))
                        step(v.tensor_copy(im, m["lim"][:, :]))
                    else:
                        r0, i0, n0 = (powers[:, lv - 1, z, :] for z in range(3))
                        step(v.tensor_tensor(m["t0"][:, :], i0, i0, ALU.mult))
                        step(v.tensor_tensor(m["t1"][:, :], r0, r0, ALU.mult))
                        step(v.tensor_tensor(re, m["t1"][:, :], m["t0"][:, :], ALU.subtract))
                        step(v.tensor_tensor(m["t0"][:, :], r0, i0, ALU.mult))
                        step(v.tensor_scalar(im, m["t0"][:, :], 2.0, None, ALU.mult))
                    step(v.tensor_scalar(neg, im, -1.0, None, ALU.mult))

            @block.tensor
            def _(pe):
                for n in range(8):
                    x, q = n // 4, n % 4
                    pe.wait_ge(b_wide, x + 1)
                    for y in range(4):
                        tr = nc.tensor.transpose(c.ps[:, n, y * P:(y + 1) * P], wide[x][:, 4 * q + y, :], c.ident[:, :])
                    tr.then_inc(b_turned, 1)
                pe.wait_ge(c_in, 16 * 16)
                for n in range(8):
                    x, q = n // 4, n % 4
                    pe.wait_ge(b_moved, n + 1)
                    for y in range(4):
                        tr = nc.tensor.transpose(c.ps[:, n, y * P:(y + 1) * P], wide[x][:, 4 * q + y, :], c.ident[:, :])
                    tr.then_inc(c_turned, 1)
        scan(c, uT, bT, cT, powers, skip, S, ygT, w_qk, qkT)


def scan(c, uT, bT, cT, powers, skip, S, ygT, w_qk, qkT):
    nc = c.nc
    LEVELS = 9
    BIG = 3
    with c.stage() as ctx:
        n_small = T >> (BIG + 1)
        small = [bT[x // 2][:, :, 0:n_small] if x % 2 else c.ps[:, 4 + x, :].rearrange("p (j n) -> p j n", j=PAIRS) for x in range(4)]
        filled, moved, swept, ready, y_done, y_sum, y_out = (
            ctx.sem(n) for n in ("filled", "moved", "swept", "ready", "y_done", "y_sum", "y_out"))
        def fill(pe):
            for j in range(PAIRS):
                for x in range(2):
                    n = 2 * j + x
                    if n >= 4:
                        pe.wait_ge(moved, n - 3)
                    nc.tensor.matmul(c.ps[:, 4 + n % 4, :], bT[x][:, j, :], uT[:, j // 4, :], start=True, stop=True).then_inc(filled, 1)

        def outputs(pe):
            for t in range(SSM_T):
                for q in range(4):
                    j = 4 * t + q
                    pe.wait_ge(ready, j + 1)
                    for x in range(2):
                        mm = nc.tensor.matmul(c.ps[:, 4 + t, :], cT[x][:, j, :], S[x][:, j, :], start=(q == 0 and x == 0), stop=(q == 3 and x == 1))
                mm.then_inc(y_done, 1)

        def move(act):
            for j in range(PAIRS):
                for x in range(2):
                    act.wait_ge(filled, 2 * j + x + 1)
                    nc.scalar.activation(S[x][:, j, :], c.ps[:, 4 + (2 * j + x) % 4, :], ACT.Copy).then_inc(moved, 1)

        def gelus(act):
            for t in range(SSM_T):
                act.wait_ge(y_sum, t + 1)
                nc.scalar.activation(ygT[:, t, :], ygT[:, t, :], ACT.Gelu_apprx_tanh).then_inc(y_out, 1)
            act.wait_ge(y_out, SSM_T)

        def sweeps(dve):
            v = nc.vector
            done = [0]

            def after(ins, n=1):
                done[0] += 1
                ins.then_inc(swept, 1)

            def views(level, down):
                d = 1 << level
                if down:
                    return slice(3 * d - 1, T, 2 * d), slice(2 * d - 1, T - d, 2 * d)
                return slice(2 * d - 1, T, 2 * d), slice(d - 1, T, 2 * d)

            def pair_step(j, level, down):
                to, of = views(level, down)
                re, im, neg = (powers[:, level, z, j:j + 1] for z in range(3))
                Sr, Si = S[0][:, j, :], S[1][:, j, :]
                after(v.scalar_tensor_tensor(Sr[:, to], Sr[:, of], re, Sr[:, to], ALU.mult, ALU.add))
                after(v.scalar_tensor_tensor(Si[:, to], Si[:, of], re, Si[:, to], ALU.mult, ALU.add))
                dve.wait_ge(swept, done[0])
                after(v.scalar_tensor_tensor(Sr[:, to], Si[:, of], neg, Sr[:, to], ALU.mult, ALU.add))
                after(v.scalar_tensor_tensor(Si[:, to], Sr[:, of], im, Si[:, to], ALU.mult, ALU.add))
                dve.wait_ge(swept, done[0])

            def all_step(level, down):
                to, of = views(level, down)
                n = len(range(*to.indices(T)))
                a = [s[:, :, 0:n] for s in small]
                lam = [powers[:, level, z, :].unsqueeze(2).to_broadcast([P, PAIRS, n]) for z in range(3)]
                Sr, Si = S[0], S[1]
                after(v.tensor_tensor(a[0], Sr[:, :, of], lam[0], ALU.mult))
                after(v.tensor_tensor(a[1], Si[:, :, of], lam[2], ALU.mult))
                after(v.tensor_tensor(a[2], Si[:, :, of], lam[0], ALU.mult))
                after(v.tensor_tensor(a[3], Sr[:, :, of], lam[1], ALU.mult))
                dve.wait_ge(swept, done[0])
                after(v.tensor_tensor(a[0], a[0], a[1], ALU.add))
                after(v.tensor_tensor(a[2], a[2], a[3], ALU.add))
                dve.wait_ge(swept, done[0])
                after(v.tensor_tensor(Sr[:, :, to], Sr[:, :, to], a[0], ALU.add))
                after(v.tensor_tensor(Si[:, :, to], Si[:, :, to], a[2], ALU.add))
                dve.wait_ge(swept, done[0])

            for j in range(PAIRS):
                dve.wait_ge(moved, 2 * j + 2)
                for level in range(BIG):
                    pair_step(j, level, False)
            for level in range(BIG, LEVELS):
                all_step(level, False)
            for level in range(LEVELS - 2, BIG - 1, -1):
                all_step(level, True)
            for j in range(PAIRS):
                for level in range(BIG - 1, -1, -1):
                    pair_step(j, level, True)
                dve.sem_inc(ready, 1)
            for t in range(SSM_T):
                dve.wait_ge(y_done, t + 1)
                v.scalar_tensor_tensor(ygT[:, t, :], uT[:, t, :], skip[:, t:t + 1], c.ps[:, 4 + t, :], ALU.mult, ALU.add).then_inc(y_sum, 1)
            dve.wait_ge(y_sum, SSM_T)

        project_copy(c, w_qk, qkT, before={"pe": fill, "act": move}, after={"pe": outputs, "act": gelus, "dve": sweeps})


def merge(c, A, ygT, attT, weights, ahead):
    nc = c.nc
    w_merge, w_out = weights
    with c.stage() as ctx:
        mixed = ctx.sbuf("mixed", [P, KD, T])
        sig = ctx.sbuf("sig", [P, 3, T])
        part = ctx.sbuf("part", [P, 2, T])
        yg = c.halves(ctx, "yg", [P, SSM_T, T])
        mixed_done, parted, yg_split, yg_low = (ctx.sem(n) for n in ("mixed_done", "parted", "yg_split", "yg_low"))

        def yg_high_half(act):
            for k in range(SSM_T):
                high_half(nc, yg.high[:, k, :], ygT[:, k, :]).then_inc(yg_split, 1)

        def start(pe):
            pe.sem_inc(mixed_done, 1)
            pe.wait_ge(yg_low, SSM_T)

        def act(eng, i, wait_tile, bank_free, split):
            for b in range(3):
                wait_tile(b)
                if b == 0:
                    eng.wait_ge(mixed_done, i + 1)
                nc.scalar.activation(sig[:, b, :], c.ps[:, b, :], ACT.Sigmoid).then_inc(bank_free, 1)
                split(b)
            split(3)

        def dve(eng, i, wait_tile, bank_free):
            eng.wait_ge(bank_free, i * 4 + (4 + 2))
            nc.vector.tensor_tensor(part[:, 0, :], sig[:, 1, :], tile_of(attT, i, 1, 0), ALU.mult).then_inc(parted, 1)
            eng.wait_ge(bank_free, i * 4 + (4 + 3))
            wait_tile(3)
            nc.vector.tensor_tensor(part[:, 1, :], sig[:, 2, :], c.ps[:, 3, :], ALU.mult).then_inc(bank_free, 1)
            eng.wait_ge(bank_free, i * 4 + (4 + 4))
            nc.vector.tensor_tensor(part[:, 1, :], part[:, 1, :], sig[:, 0, :], ALU.mult).then_inc(parted, 1)
            eng.wait_ge(parted, i * 2 + 2)
            nc.vector.tensor_tensor(tile_of(mixed, i, 1, 0), part[:, 0, :], part[:, 1, :], ALU.add).then_inc(mixed_done, 1)

        def yg_low_half(dve):
            for k in range(SSM_T):
                dve.wait_ge(yg_split, k + 1)
                low_half(nc.vector, yg.low[:, k, :], ygT[:, k, :], yg.high[:, k, :]).then_inc(yg_low, 1)
        project(c, w_merge, {"act": act, "dve": dve}, [c.h, c.h, yg, yg], w_out, before={"pe": start, "act": yg_high_half, "dve": yg_low_half},
                after={"dve": lambda eng: eng.wait_ge(mixed_done, KD + 1)})
        project_add(c, w_out, c.xT, c.h, mixed, ahead, {"dve": lambda dve: dve.wait_ge(c.x_back, 16)})


def merge_weights(w_in, w_glu):
    col_g = SSM_W + 3 * FOX_H * P + FOX_H
    wide, glu = w_in.rearrange("(k p) n -> p k n", p=P), w_glu.rearrange("(k p) n -> p k n", p=P)
    kinds = ((wide, col_g), (wide, col_g + D), (glu, D), (glu, 0))

    def source(i, b):
        view, col = kinds[b]
        return [(ALL, view[:, :, bass.ds(i * P + col, P)])]
    return Weights(KD, 4, source, [KD, KD, SSM_T, SSM_T])


def first_mix(c, A, ahead):
    w_in = A["w_in"][0]
    w_u, w_qk = columns(w_in, 1, SSM_T), columns(w_in, FOX_H, 2, SSM_W)
    w_merge, w_out = merge_weights(w_in, A["ssm_w_glu"][0]), columns(A["w_out"][0], 2, 4)
    with c.stage() as ctx:
        c.h = c.halves(ctx, "h", [P, KD, T])
        rms_norm(c, A["mix_norm_g"][0], c.h, w_u)
        ygT = ctx.sbuf("ygT", [P, SSM_T, T])
        qkT = ctx.sbuf("qkT", [P, 2 * FOX_H, T])
        ssm(c, A, w_u, w_qk, qkT, ygT)
        fox_attention(c, w_in, A["fox_forget_bias"][0], A["q_norm_g"][0], A["k_norm_g"][0], qkT, w_merge)
        merge(c, A, ygT, qkT, (w_merge, w_out), ahead)


GROUP = 4
RING = 16
ROUNDS = SLOTS // RING


def peer(c, A, w_query):
    with c.stage() as ctx:
        route = Route(c, ctx)
        rows = ctx.sbuf("rows", [P, TT, D])
        with c.stage() as inner:
            c.h = c.halves(inner, "h", [P, KD, T])
            rms_norm(c, A["ffn_norm_g"][0], c.h)
            to_rows(c, rows)
            peer_scores(c, w_query, A["peer_sub_keys"][0], route)
        peer_experts(c, A["peer_uv"], route, rows)
        add_rows(c, rows)


def to_rows(c, rows):
    nc = c.nc
    with c.stage() as ctx:
        high, low = [ctx.sem(f"{h}_turned") for h in ("high", "low")]
        copied, added = ctx.sem("copied"), ctx.sem("added")
        part = lambda n: rows[:, n // 2, (n % 2) * T:(n % 2 + 1) * T]
        with nc.Block() as block:

            @block.tensor
            def _(pe):
                for n in range(2 * TT):
                    t, h = n // 2, n % 2
                    for x, (buf, turned) in enumerate(zip(c.h, (high, low))):
                        if n >= 4:
                            pe.wait_ge(added, n - 3)
                        for k in range(4):
                            tr = nc.tensor.transpose(c.ps[:, 4 * x + n % 4, k * P:(k + 1) * P], buf[:, 4 * h + k, t * P:(t + 1) * P], c.ident[:, :])
                        tr.then_inc(turned, 1)

            @block.scalar
            def _(act):
                for n in range(2 * TT):
                    act.wait_ge(high, n + 1)
                    nc.scalar.activation(part(n), c.ps[:, n % 4, :], ACT.Copy).then_inc(copied, 1)

            @block.vector
            def _(dve):
                for n in range(2 * TT):
                    dve.wait_ge(copied, n + 1)
                    dve.wait_ge(low, n + 1)
                    nc.vector.tensor_tensor(part(n), part(n), c.ps[:, 4 + n % 4, :], ALU.add).then_inc(added, 1)
                dve.wait_ge(added, 2 * TT)


def add_rows(c, rows):
    nc = c.nc
    with c.stage() as ctx:
        turned, added = ctx.sem("turned"), ctx.sem("added")
        with nc.Block() as block:

            @block.tensor
            def _(pe):
                for k in range(KD):
                    for t in range(TT):
                        tr = nc.tensor.transpose(c.ps[:, k, t * P:(t + 1) * P], rows[:, t, k * P:(k + 1) * P], c.ident[:, :])
                    tr.then_inc(turned, 1)

            @block.vector
            def _(dve):
                for k in range(KD):
                    dve.wait_ge(turned, k + 1)
                    nc.vector.tensor_tensor(c.xT[:, k, :], c.xT[:, k, :], c.ps[:, k, :], ALU.add).then_inc(added, 1)
                dve.wait_ge(added, KD)


HC = 2 * PEER_H


def peer_scores(c, w_query, sub_keys, route):
    nc = c.nc
    with c.stage() as ctx:
        qT = ctx.sbuf("qT", [P, HC, T])
        keys = ctx.sbuf("keys", [P, HC, P])
        keysT = ctx.sbuf("keysT", [P, HC, P])
        keys_in, turned, moved, scored, copied, stored = (ctx.sem(n) for n in ("keys_in", "turned", "moved", "scored", "copied", "stored"))
        quarters = HC // 4

        def load_keys(sp):
            sp.dma_start(keys[:, :, :], sub_keys.rearrange("h c k d -> k (h c) d")).then_inc(keys_in, 16)

        def store(sp):
            for t in range(1, TT):
                sp.wait_ge(copied, quarters * (t + 1))
                sp.dma_start(route.scores[t], scores[:, t - 1, :]).then_inc(stored, 16)
            sp.wait_ge(stored, 16 * (TT - 1))

        def turn_keys(pe):
            pe.wait_ge(keys_in, 16)
            for n in range(quarters):
                for y in range(4):
                    tr = nc.tensor.transpose(c.ps[:, 4 + n, y * P:(y + 1) * P], keys[:, 4 * n + y, :], c.ident[:, :])
                tr.then_inc(turned, 1)

        def move_keys(act):
            for n in range(quarters):
                act.wait_ge(turned, n + 1)
                nc.scalar.activation(keysT[:, 4 * n:4 * n + 4, :], c.ps[:, 4 + n, :], ACT.Copy).then_inc(moved, 1)
            act.wait_ge(moved, quarters)

        project_copy(c, w_query, qT, before={"sp": load_keys, "pe": turn_keys, "act": move_keys})
        scores = ctx.sbuf("scores", [P, TT - 1, HC * PEER_K])
        with nc.Block() as block:

            @block.tensor
            def _(pe):
                for n in range(TT * quarters):
                    if n >= 8:
                        pe.wait_ge(copied, n - 7)
                    t, quarter = n // quarters, n % quarters
                    for y in range(4):
                        hc = 4 * quarter + y
                        mm = nc.tensor.matmul(c.ps[:, n % 8, y * P:(y + 1) * P], qT[:, hc, t * P:(t + 1) * P], keysT[:, hc, :], start=True, stop=True)
                    mm.then_inc(scored, 1)

            @block.scalar
            def _(act):
                for n in range(TT * quarters):
                    act.wait_ge(scored, n + 1)
                    t, quarter = n // quarters, n % quarters
                    dest = route.work[:, 4 * quarter:4 * quarter + 4, :] if t == 0 else scores[:, t - 1, quarter * T:(quarter + 1) * T]
                    nc.scalar.activation(dest, c.ps[:, n % 8, :], ACT.Copy).then_inc(copied, 1)
                act.wait_ge(copied, TT * quarters)

            block.sync(store)


class Route:

    def __init__(self, c, ctx):
        self.c = c
        self.scores = c.nc.dram_tensor("peer_scores", (TT, P, HC * PEER_K), F32).ap()
        self.idx = ctx.sbuf("idx", [P, TT * SLOTS], U32)
        self.gates = ctx.sbuf("gates", [P, TT * SLOTS])
        self.work = ctx.sbuf("work", [P, HC, PEER_K])
        flat = self.work[:, :, :].rearrange("p r k -> p (r k)")
        self.sums = flat.rearrange("p (h s) -> p h s", h=PEER_H)
        self.hit = flat.rearrange("p (s k) -> p s k", k=TOPK)
        self.top = ctx.sbuf("top", [P, HC, TOPK])
        self.top_at = ctx.sbuf("top_at", [P, HC, TOPK], U32)
        self.top_atf = ctx.sbuf("top_atf", [P, PEER_H, 2, TOPK])
        self.best = ctx.sbuf("best", [P, PEER_H, TOPK])
        self.best_at = ctx.sbuf("best_at", [P, PEER_H, TOPK], U32)
        self.half_at = ctx.sbuf("half_at", [P, 2, SLOTS], U32)
        self.half_f = ctx.sbuf("half_f", [P, 2, SLOTS])
        self.key_no = ctx.sbuf("key_no", [P, 2, SLOTS])
        self.iota = ctx.sbuf("iota", [P, TOPK])
        self.total = ctx.sbuf("total", [P, PEER_H])
        self.scores_in, self.less, self.exped, self.routed = (ctx.sem(n) for n in ("scores_in", "less", "exped", "routed"))

    STEPS = 5 * HC + 1 + 5 * PEER_H + 3 + 1 + 1 + 2 * 3 + 1 + 3

    def top16(self, step, n, values, at, source):
        v = self.c.nc.vector
        for half in (slice(0, 8), slice(8, 16)):
            for r in range(n):
                step.mark(v.max(values[:, r, half], source[:, r, :]))
            step.wait()
            for r in range(n):
                step.mark(v.max_index(at[:, r, half], values[:, r, half], source[:, r, :]))
            step.wait()
            if half.start == 0:
                for r in range(n):
                    step.mark(v.match_replace(source[:, r, :], values[:, r, half], source[:, r, :], LOWEST))
                step.wait()

    def halves(self, step):
        self.top16(step, HC, self.top, self.top_at, self.work)

    def pairs(self, step):
        v = self.c.nc.vector
        pair = self.top[:, :, :].rearrange("p (h c) k -> p h c k", c=2)
        sums = self.sums.rearrange("p h (i j) -> p h i j", j=TOPK)
        wide = [P, PEER_H, TOPK, TOPK]
        step(v.tensor_tensor(sums, pair[:, :, 0, :].unsqueeze(3).to_broadcast(wide), pair[:, :, 1, :].unsqueeze(2).to_broadcast(wide), ALU.add))
        self.top16(step, PEER_H, self.best, self.best_at, self.sums)
        step(v.tensor_copy(self.total[:, :], self.best[:, :, 0]))
        v.tensor_tensor(self.best[:, :, :], self.best[:, :, :], self.total[:, :].unsqueeze(2).to_broadcast([P, PEER_H, TOPK]), ALU.subtract).then_inc(self.less, 1)

    def exp(self, act, t):
        act.wait_ge(self.less, t + 1)
        self.c.nc.scalar.activation(self.best[:, :, :], self.best[:, :, :], ACT.Exp).then_inc(self.exped, 1)

    def experts(self, step, dve, t, at):
        v = self.c.nc.vector
        wide = [P, PEER_H, TOPK, TOPK]
        flat = self.best_at[:, :, :].rearrange("p h s -> p (h s)")
        step.mark(v.tensor_copy(self.top_atf[:, :, :, :], self.top_at[:, :, :].rearrange("p (h c) k -> p h c k", c=2)))
        step.mark(v.tensor_scalar(self.half_at[:, 0, :], flat, 4, None, ALU.logical_shift_right))
        step.mark(v.tensor_scalar(self.half_at[:, 1, :], flat, TOPK - 1, None, ALU.bitwise_and))
        step.wait()
        step(v.tensor_copy(self.half_f[:, :, :], self.half_at[:, :, :]))
        hit = self.hit
        for x in range(2):
            step(v.tensor_tensor(hit, self.half_f[:, x, :].unsqueeze(2).to_broadcast([P, SLOTS, TOPK]),
                                 self.iota[:, :].unsqueeze(1).to_broadcast([P, SLOTS, TOPK]), ALU.is_equal))
            hits = hit.rearrange("p (h s) k -> p h s k", h=PEER_H)
            step(v.tensor_tensor(hits, hits, self.top_atf[:, :, x, :].unsqueeze(2).to_broadcast(wide), ALU.mult))
            step(v.tensor_reduce(self.key_no[:, x, :], hit, AX.X, ALU.add))
        step(v.scalar_tensor_tensor(self.idx[:, at], self.key_no[:, 0, :], float(PEER_K), self.key_no[:, 1, :], ALU.mult, ALU.add))
        dve.wait_ge(self.exped, t + 1)
        step(v.tensor_reduce(self.total[:, :], self.best[:, :, :], AX.X, ALU.add))
        step(v.reciprocal(self.total[:, :], self.total[:, :]))
        gate = self.gates[:, at].rearrange("p (h s) -> p h s", h=PEER_H)
        step(v.tensor_tensor(gate, self.best[:, :, :], self.total[:, :].unsqueeze(2).to_broadcast([P, PEER_H, TOPK]), ALU.mult))
        dve.sem_inc(self.routed, 1)


def peer_experts(c, uv, route, rows):
    nc = c.nc
    groups = RING // GROUP
    sections = ((0, 3), (3, 5), (5, 6), (6, ROUNDS))
    with c.stage() as ctx:
        own = ctx.sbuf("ring", [P, RING, 2 * D])
        ring = [own[:, s, :] for s in range(RING)]
        idx_now = ctx.sbuf("idx_now", [P, 2, RING], U32)
        h_row, sums = c.w_ring[:, 0, :], c.w_ring[:, 2:4, :]
        dots, acts, weights = (ctx.sbuf(n, [P, RING]) for n in ("dots", "acts", "weights"))
        gathered = [c.sem(f"gathered{s}") for s in range(RING)]
        idx_set, iota_in = ctx.sem("idx_set"), ctx.sem("iota_in")
        used, dotted, acted, weighed, summed, tile_done = (ctx.sem(n) for n in ("used", "dotted", "acted", "weighed", "summed", "tile_done"))

        def rounds(eng, first, last, body):
            if last - first == 1:
                body(first)
            else:
                with eng.Fori(first, last) as n:
                    body(n)

        with nc.Block() as block:

            @block.sync
            def _(sp):
                sp.dma_start(route.iota[:, :], c.ins["c_iota"]).then_inc(iota_in, 16)
                with sp.Fori(1, TT) as t:
                    sp.wait_ge(route.routed, t)
                    sp.dma_start(route.work[:, :, :].rearrange("p r k -> p (r k)"), route.scores[bass.ds(t, 1), :, :].rearrange("a p n -> p (a n)")
                                 ).then_inc(route.scores_in, 16)

            @block.gpsimd
            def _(pool):
                pool.sem_inc(used, RING)
                with pool.Fori(0, TT) as t:
                    hold(pool, route.routed, t + 1, c.pool_tick)
                    with pool.Fori(0, ROUNDS // 2) as r:
                        for x in range(2):
                            nc.gpsimd.tensor_copy(idx_now[:, x, :], route.idx[:, bass.ds(t * SLOTS + r * (2 * RING) + x * RING, RING)]).then_inc(idx_set, 1)
                            hold(pool, idx_set, t * ROUNDS + r * 2 + (x + 1), c.pool_tick)
                            for s in range(RING):
                                hold(pool, used, t * SLOTS + r * (2 * RING) + (x * RING + s + 1), c.pool_tick)
                                nc.gpsimd.indirect_dma_start(ring[s], None, uv, bass.IndirectOffsetOnAxis(ap=idx_now[:, x, s:s + 1], axis=0)
                                                             ).then_inc(gathered[s], 16)

            @block.scalar
            def _(act):
                def gelus(t, first, last):
                    def body(n):
                        for g in range(groups):
                            act.wait_ge(dotted, t * SLOTS + n * RING + (g + 1) * GROUP)
                            of = slice(g * GROUP, (g + 1) * GROUP)
                            nc.scalar.activation(acts[:, of], dots[:, of], ACT.Gelu_apprx_tanh).then_inc(acted, 1)
                    rounds(act, first, last, body)

                route.exp(act, 0)
                with act.Fori(0, TT - 1) as t:
                    gelus(t, 0, sections[2][0])
                    route.exp(act, t + 1)
                    gelus(t, sections[2][0], ROUNDS)
                gelus(TT - 1, 0, ROUNDS)

            @block.vector
            def _(dve):
                v = nc.vector

                def weigh(t, first, last):
                    def body(n):
                        def dot(g):
                            for s in range(g * GROUP, (g + 1) * GROUP):
                                dve.wait_ge(gathered[s], t * (16 * ROUNDS) + n * 16 + 16)
                                v.tensor_tensor_reduce(out=ring[s][:, 0:D], in0=ring[s][:, 0:D], in1=h_row, scale=1.0, scalar=0.0,
                                                       op0=ALU.mult, op1=ALU.add, accum_out=dots[:, s:s + 1]).then_inc(dotted, 1)

                        def add(g):
                            of = slice(g * GROUP, (g + 1) * GROUP)
                            dve.wait_ge(acted, t * (groups * ROUNDS) + n * groups + (g + 1))
                            v.tensor_tensor(weights[:, of], acts[:, of], route.gates[:, bass.ds(t * SLOTS + n * RING + g * GROUP, GROUP)], ALU.mult).then_inc(weighed, 1)
                            dve.wait_ge(weighed, t * (groups * ROUNDS) + n * groups + (g + 1))
                            for s in range(g * GROUP, (g + 1) * GROUP):
                                dve.wait_ge(used, t * SLOTS + n * RING + (RING + s - 1))
                                half = sums[:, s % 2, :]
                                v.scalar_tensor_tensor(half, ring[s][:, D:2 * D], weights[:, s:s + 1], half, ALU.mult, ALU.add).then_inc(used, 1)

                        dot(0)
                        for g in range(1, groups):
                            dot(g)
                            add(g - 1)
                        add(groups - 1)
                    rounds(dve, first, last, body)

                def start(step, t):
                    step.mark(v.tensor_copy(h_row, rows[:, t, :]))
                    step.mark(v.memset(sums[:, :, :], 0.0))
                    step.wait()

                def finish(t):
                    dve.wait_ge(used, t * SLOTS + (SLOTS + RING))
                    v.tensor_tensor(rows[:, t, :], sums[:, 0, :], sums[:, 1, :], ALU.add).then_inc(tile_done, 1)
                    dve.wait_ge(tile_done, t + 1)

                dve.wait_ge(iota_in, 16)
                step = Chain(dve, c.dve_step)
                route.halves(step)
                route.pairs(step)
                dve.wait_ge(route.less, 1)
                route.experts(step, dve, 0, slice(0, SLOTS))
                with dve.Fori(0, TT - 1) as t:
                    step = Chain(dve, c.dve_step, t, 2 + Route.STEPS, c.dve_tick)
                    start(step, t)
                    weigh(t, *sections[0])
                    hold(dve, route.scores_in, t * 16 + 16, c.dve_tick)
                    route.halves(step)
                    weigh(t, *sections[1])
                    route.pairs(step)
                    weigh(t, *sections[2])
                    route.experts(step, dve, t + 1, bass.ds(t * SLOTS + SLOTS, SLOTS))
                    weigh(t, *sections[3])
                    finish(t)
                    step.ends(TT - 1)
                step = Chain(dve, c.dve_step)
                start(step, TT - 1)
                weigh(TT - 1, 0, ROUNDS)
                finish(TT - 1)


def tile_norm(c, buf, first, tiles, gain, factor):
    nc = c.nc
    with c.stage() as ctx:
        squares = ctx.sbuf("squares", [P, tiles, T])
        rstd = ctx.sbuf("rstd", [P, tiles, T])
        gains = ctx.sbuf("gains", [P, 1])
        gain_in, squared, summed, inverted, rooted, normed = (ctx.sem(n) for n in ("gain_in", "squared", "summed", "inverted", "rooted", "normed"))
        with nc.Block() as block:

            @block.sync
            def _(sp):
                sp.dma_start(gains[:, :], gain.rearrange("(p a) -> p a", a=1)).then_inc(gain_in, 16)

            @block.scalar
            def _(act):
                for b in range(tiles):
                    nc.scalar.activation(squares[:, b, :], buf[:, first + b, :], ACT.Square).then_inc(squared, 1)
                for b in range(tiles):
                    act.wait_ge(summed, b + 1)
                    nc.scalar.activation(rstd[:, b, :], c.ps[:, b, :], ACT.Sqrt, bias=c.eps[:, 0:1], scale=1.0 / P).then_inc(rooted, 1)

            @block.tensor
            def _(pe):
                for b in range(tiles):
                    pe.wait_ge(squared, b + 1)
                    nc.tensor.matmul(c.ps[:, b, :], c.ones[:, :], squares[:, b, :], start=True, stop=True).then_inc(summed, 1)

            @block.vector
            def _(dve):
                step = Chain(dve, c.dve_step)
                dve.wait_ge(gain_in, 16)
                step(nc.vector.tensor_scalar(gains[:, :], gains[:, :], factor, None, ALU.mult))
                for b in range(tiles):
                    dve.wait_ge(rooted, b + 1)
                    nc.vector.reciprocal(rstd[:, b, :], rstd[:, b, :]).then_inc(inverted, 1)
                for b in range(tiles):
                    dve.wait_ge(inverted, b + 1)
                    tile = buf[:, first + b, :]
                    nc.vector.scalar_tensor_tensor(tile, tile, gains[:, 0:1], rstd[:, b, :], ALU.mult, ALU.mult).then_inc(normed, 1)
                dve.wait_ge(normed, tiles)


class Rope:

    def __init__(self, c, ctx, dim):
        nc = c.nc
        self.swap = ctx.sbuf("swap", [P, P])
        self.cos = ctx.sbuf("cos", [P, T])
        self.sin = ctx.sbuf("sin", [P, T])
        tables_in = ctx.sem("tables_in")
        with nc.Block() as block:

            @block.sync
            def _(sp):
                sp.dma_start(self.swap[:, :], c.ins[f"c_swap{dim}"]).then_inc(tables_in, 16)
                sp.dma_start(self.cos[:, :], c.ins[f"c_cos{dim}"]).then_inc(tables_in, 16)
                sp.dma_start(self.sin[:, :], c.ins[f"c_sin{dim}"]).then_inc(tables_in, 16)
                sp.wait_ge(tables_in, 48)
        self.tables = (self.swap, self.cos, self.sin)


def repeated(w, col, n):
    view = w.rearrange("(k p) n -> p k n", p=P)

    def source(i, b):
        return [((slice(None), slice(None), slice(r * n, (r + 1) * n)), view[:, :, col:col + n]) for r in range(P // n)]
    return Weights(1, 1, source)


A_SCALE = (64 + 32) ** -0.5
EV = dict(nope=0, rope=512, ckv=768, krope=896, iq=928, ik=1440, iw=1504, qb=1512, kb=2024, vb=2536)


def even_weights(A):
    w_in = A["ev_w_in"][0]
    return dict(qk=columns(w_in, 2, 4, EV["qb"]), iq=columns(w_in, 1, 4, EV["iq"]), ik=repeated(w_in, EV["ik"], 64),
                krope=repeated(w_in, EV["krope"], 32), rope=columns(w_in, 1, 2, EV["rope"]), nope=columns(w_in, 1, 4, EV["nope"]),
                out=columns(A["ev_w_out"][0], 2, 4))


def even_mix(c, A, w, ahead):
    w_in = A["ev_w_in"][0]
    with c.stage() as ctx:
        c.h = c.halves(ctx, "h", [P, KD, T])
        oT = ctx.sbuf("oT", [P, KD, T])
        rows = [ctx.sbuf(n, [P, TT, w]) for n, w in (("ckv", P), ("iw", DSA_H), ("vb", T))]
        w_rows = RowWeights(w_in, [(EV["vb"], T, rows[2], ACT.Copy), (EV["ckv"], P, rows[0], ACT.Copy), (EV["iw"], DSA_H, rows[1], ACT.Copy)])
        rms_norm(c, A["norm_mix"][0], c.h, w_rows)
        project_rows(c, w_rows, ahead=w["qk"])
        rope64 = Rope(c, ctx, 64)
        differential(c, A, w, rope64, rows[2], oT)
        selected(c, A, w, rope64, rows[0], rows[1], oT)
        project_add(c, w["out"], c.xT, c.h, oT, ahead)


def differential(c, A, w, rope64, vb, oT):
    nc = c.nc
    lam_init = 0.8 - 0.6
    with c.stage() as ctx:
        qkT = ctx.sbuf("qkT", [P, 2 * DIFF_H, T])
        project_rope(c, w["qk"], rope64.tables, 1.0, qkT, w["iq"])
        lam = ctx.sbuf("lam", [P, 4, 64])
        both = ctx.sbuf("both", [P, 2, 64])
        dots = ctx.sbuf("dots", [P, 2])
        minus = ctx.sbuf("minus", [P, 1])
        lam_in, dotted, exped = ctx.sem("lam_in"), ctx.sem("dotted"), ctx.sem("exped")
        with nc.Block() as block:

            @block.sync
            def _(sp):
                sp.dma_start(lam[:, :, :], A["ev_lambda"][0].partition_broadcast(P)).then_inc(lam_in, 16)

            @block.vector
            def _(dve):
                step = Chain(dve, c.dve_step)
                dve.wait_ge(lam_in, 16)
                step(nc.vector.tensor_tensor(both[:, :, :], lam[:, 0::2, :], lam[:, 1::2, :], ALU.mult))
                nc.vector.tensor_reduce(dots[:, :], both[:, :, :], AX.X, ALU.add).then_inc(dotted, 1)
                dve.wait_ge(exped, 1)
                step(nc.vector.scalar_tensor_tensor(minus[:, :], dots[:, 1:2], -lam_init, dots[:, 0:1], ALU.add, ALU.subtract))

            @block.scalar
            def _(act):
                act.wait_ge(dotted, 1)
                nc.scalar.activation(dots[:, :], dots[:, :], ACT.Exp).then_inc(exped, 1)
        per_turn = DIFF_H // 2
        slots = [(ctx.sbuf(f"q{s}", [P, T]), ctx.sbuf(f"k{s}", [P, T]), ctx.sbuf(f"v{s}", [P, TT, P])) for s in range(per_turn)]

        def stage(s):
            q, k, v = slots[s]
            return lambda i: [(q[:, :], tile_of(qkT, i, per_turn, s)), (k[:, :], tile_of(qkT, i, per_turn, s + DIFF_H)), (v[:, :, :], vb[:, :, bass.ds(i * (per_turn * P) + s * P, P)])]

        def head_map(s, m):
            q, k, v = slots[s]
            half = slice(64 * m, 64 * m + 64)
            return dict(q=q[half, :], k=lambda i: k[half, :], v=lambda j: v[:, j, :], mask=None, slots=[s],
                        gate=(lambda i, t: minus[:, 0:1]) if m else None, out=c.ps[:, 7, :], sum=c.ps[:, 7, :], first=m == 0, last=m == 1)
        attention(c, DIFF_H // per_turn, [head_map(s, m) for s in range(per_turn) for m in range(2)], 64 ** -0.5,
                  {s: stage(s) for s in range(per_turn)}, {2 * s + 1: (lambda i, s=s: tile_of(oT, i, per_turn, s + 4)) for s in range(per_turn)})
    tile_norm(c, oT, 4, DIFF_H, A["ev_subln"][0], 1.0 - lam_init)


def selected(c, A, w, rope64, ckv, iw, oT):
    nc = c.nc
    with c.stage() as ctx:
        add_mask = ctx.sbuf("add_mask", [P, TT, T])
        choose_keys(c, w, rope64, iw, add_mask)
        keysT = ctx.sbuf("keysT", [P, T])
        latents(c, A["ev_kv_gain"][0], ckv, keysT)
        krT = ctx.sbuf("krT", [P, 1, T])
        q_lat = ctx.sbuf("q_lat", [P, DSA_H, T])
        q_rot = ctx.sbuf("q_rot", [P, DSA_H, T])
        w_uv = ctx.sbuf("w_uv", [P, DSA_H, 64])
        with c.stage() as inner:
            rope32 = Rope(c, inner, 32)
            qrT = inner.sbuf("qrT", [P, 2, T])
            qnT = inner.sbuf("qnT", [P, 4, T])
            w_uk = inner.sbuf("w_uk", [P, 4, P])
            head_rows = inner.sbuf("head_rows", [P, 4])
            project_rope(c, w["krope"], rope32.tables, 1.0, krT, w["rope"])
            project_rope(c, w["rope"], rope32.tables, A_SCALE, qrT, w["nope"])
            project_copy(c, w["nope"], qnT, w["out"])
            up_in, made, copied, masked = (inner.sem(n) for n in ("up_in", "made", "copied", "masked"))
            with nc.Block() as block:

                @block.sync
                def _(sp):
                    sp.dma_start(w_uk[:, :, :], A["ev_w_uk"][0].rearrange("(j two) d c -> (two d) j c", two=2)).then_inc(up_in, 16)
                    sp.dma_start(head_rows[:, :], c.ins["c_head_rows"]).then_inc(up_in, 16)
                    sp.dma_start(w_uv[:, :, :], A["ev_w_uv"][0].rearrange("h c d -> c h d")).then_inc(up_in, 16)

                @block.tensor
                def _(pe):
                    pe.wait_ge(up_in, 48)
                    for h in range(DSA_H):
                        r = slice(64 * (h % 2), 64 * (h % 2) + 64)
                        nc.tensor.matmul(c.ps[:, h, :], w_uk[r, h // 2, :], qnT[r, h // 2, :], start=True, stop=True).then_inc(made, 1)

                @block.scalar
                def _(act):
                    for h in range(DSA_H):
                        act.wait_ge(made, h + 1)
                        nc.scalar.activation(q_lat[:, h, :], c.ps[:, h, :], ACT.Copy, scale=A_SCALE).then_inc(copied, 1)
                    act.wait_ge(copied, DSA_H)

                @block.vector
                def _(dve):
                    dve.wait_ge(up_in, 48)
                    for h in range(DSA_H):
                        nc.vector.tensor_scalar(q_rot[:, h, :], qrT[:, h // 4, :], head_rows[:, h % 4:h % 4 + 1], None, ALU.mult).then_inc(masked, 1)
                    dve.wait_ge(masked, DSA_H)
        outT = ctx.sbuf("outT", [P, DSA_H, T])
        per_turn = DSA_H // 2
        slots = [[ctx.sbuf(f"{n}{s}", [P, T]) for n in ("q", "q2")] for s in range(per_turn)]

        def stage(s):
            q, q2 = slots[s]
            return lambda i: [(q[:, :], tile_of(q_lat, i, per_turn, s)), (q2[:, :], tile_of(q_rot, i, per_turn, s))]

        def head(s):
            q, q2 = slots[s]
            return dict(q=q, k=lambda i: keysT, q2=q2, k2=lambda i: krT[:, 0, :], v=lambda j: ckv[:, j, :], slots=[s],
                        mask=lambda t: add_mask[:, t, 0:P * (t + 1)], out=c.ps[:, 7, :], sum=c.ps[:, 7, :], first=True, last=True)
        attention(c, DSA_H // per_turn, [head(s) for s in range(per_turn)], 1.0, {s: stage(s) for s in range(per_turn)},
                  {s: (lambda i, s=s: tile_of(outT, i, per_turn, s)) for s in range(per_turn)})
        with c.stage() as inner:
            made, copied = inner.sem("made"), inner.sem("copied")
            with nc.Block() as block:

                @block.tensor
                def _(pe):
                    for h in range(DSA_H):
                        r = slice(64 * (h % 2), 64 * (h % 2) + 64)
                        nc.tensor.matmul(c.ps[r, h // 2, :], w_uv[:, h, :], outT[:, h, :], start=True, stop=True).then_inc(made, 1)

                @block.scalar
                def _(act):
                    for j in range(DSA_H // 2):
                        act.wait_ge(made, 2 * j + 2)
                        nc.scalar.activation(oT[:, j, :], c.ps[:, j, :], ACT.Copy).then_inc(copied, 1)
                    act.wait_ge(copied, DSA_H // 2)


def latents(c, gain, ckv, keysT):
    nc = c.nc
    with c.stage() as ctx:
        gains = ctx.sbuf("gains", [P, P])
        squares = ctx.sbuf("squares", [P, TT, P])
        rstd = ctx.sbuf("rstd", [P, TT])
        gain_in, squared, inverted, rooted, normed, turned, copied = (
            ctx.sem(n) for n in ("gain_in", "squared", "inverted", "rooted", "normed", "turned", "copied"))
        with nc.Block() as block:

            @block.sync
            def _(sp):
                sp.dma_start(gains[:, :], gain.partition_broadcast(P)).then_inc(gain_in, 16)

            @block.scalar
            def _(act):
                for t in range(TT):
                    nc.scalar.activation(squares[:, t, :], ckv[:, t, :], ACT.Square, accum_out=rstd[:, t:t + 1]).then_inc(squared, 1)
                act.wait_ge(inverted, 1)
                nc.scalar.activation(rstd[:, :], rstd[:, :], ACT.Sqrt).then_inc(rooted, 1)
                act.wait_ge(turned, 1)
                nc.scalar.activation(keysT[:, :], c.ps[:, 0, :], ACT.Copy).then_inc(copied, 1)
                act.wait_ge(copied, 1)

            @block.vector
            def _(dve):
                step = Chain(dve, c.dve_step)
                dve.wait_ge(squared, TT)
                step(nc.vector.tensor_scalar(rstd[:, :], rstd[:, :], 1.0 / P, EPS, ALU.mult, ALU.add))
                nc.vector.reciprocal(rstd[:, :], rstd[:, :]).then_inc(inverted, 1)
                dve.wait_ge(rooted, 1)
                dve.wait_ge(gain_in, 16)
                for t in range(TT):
                    nc.vector.scalar_tensor_tensor(ckv[:, t, :], ckv[:, t, :], rstd[:, t:t + 1], gains[:, :], ALU.mult, ALU.mult).then_inc(normed, 1)

            @block.tensor
            def _(pe):
                for t in range(TT):
                    pe.wait_ge(normed, t + 1)
                    tr = nc.tensor.transpose(c.ps[:, 0, t * P:(t + 1) * P], ckv[:, t, :], c.ident[:, :])
                tr.then_inc(turned, 1)


def choose_keys(c, w, rope64, iw, add_mask):
    nc = c.nc
    IH = DSA_H
    width = [P * (t + 1) for t in range(TT)]
    with c.stage() as ctx:
        iqT = ctx.sbuf("iqT", [P, IH // 2, T])
        ikT = ctx.sbuf("ikT", [P, 1, T])
        project_rope(c, w["iq"], rope64.tables, 1.0, iqT, w["ik"])
        project_rope(c, w["ik"], rope64.tables, 1.0, ikT, w["krope"])
        relus = ctx.sbuf("relus", [P, 4, T])
        score = ctx.sbuf("score", [P, TT, T])
        work = ctx.sbuf("work", [P, TT, T])
        best = ctx.sbuf("best", [P, TT, 8])
        weights = ctx.sbuf("weights", [P, TT, IH])
        made, rectified, summed = ctx.sem("made"), ctx.sem("rectified"), ctx.sem("summed")
        steps = [(t, h) for t in range(1, TT) for h in range(IH)]
        with nc.Block() as block:

            @block.tensor
            def _(pe):
                for n, (t, h) in enumerate(steps):
                    if n >= 4:
                        pe.wait_ge(rectified, n - 3)
                    r = slice(64 * (h % 2), 64 * (h % 2) + 64)
                    nc.tensor.matmul(c.ps[:, n % 4, 0:width[t]], iqT[r, h // 2, t * P:(t + 1) * P], ikT[r, 0, 0:width[t]],
                                     start=True, stop=True).then_inc(made, 1)

            @block.scalar
            def _(act):
                for n, (t, h) in enumerate(steps):
                    act.wait_ge(made, n + 1)
                    if n >= 4:
                        act.wait_ge(summed, n - 3)
                    nc.scalar.activation(relus[:, n % 4, 0:width[t]], c.ps[:, n % 4, 0:width[t]], ACT.Relu, scale=64 ** -0.5).then_inc(rectified, 1)

            @block.vector
            def _(dve):
                v = nc.vector
                step = Chain(dve, c.dve_step)
                step(v.tensor_scalar(weights[:, :, :], iw[:, :, :], float(IH) ** -0.5, None, ALU.mult))
                for n, (t, h) in enumerate(steps):
                    dve.wait_ge(rectified, n + 1)
                    s, factor = score[:, t, 0:width[t]], weights[:, t, h:h + 1]
                    if h == 0:
                        v.tensor_scalar(s, relus[:, n % 4, 0:width[t]], factor, None, ALU.mult).then_inc(summed, 1)
                    else:
                        dve.wait_ge(summed, n)
                        v.scalar_tensor_tensor(s, relus[:, n % 4, 0:width[t]], factor, s, ALU.mult, ALU.add).then_inc(summed, 1)
                dve.wait_ge(summed, len(steps))
                for t in range(1, TT):
                    last = score[:, t, t * P:(t + 1) * P]
                    step.mark(v.tensor_tensor(last, last, c.causal[:, :], ALU.add))
                step.wait()
                for t in range(1, TT):
                    step.mark(v.tensor_copy(work[:, t, 0:width[t]], score[:, t, 0:width[t]]))
                step.wait()
                for _ in range(DSA_SEL // 8):
                    for t in range(1, TT):
                        step.mark(v.max(best[:, t, :], work[:, t, 0:width[t]]))
                    step.wait()
                    for t in range(1, TT):
                        step.mark(v.match_replace(work[:, t, 0:width[t]], best[:, t, :], work[:, t, 0:width[t]], LOWEST))
                    step.wait()
                for t in range(1, TT):
                    step.mark(v.tensor_tensor(work[:, t, 0:width[t]], work[:, t, 0:width[t]], score[:, t, 0:width[t]], ALU.is_equal))
                step.wait()
                for t in range(1, TT):
                    step.mark(v.tensor_scalar(add_mask[:, t, 0:width[t]], work[:, t, 0:width[t]], NEG, None, ALU.mult))
                step.mark(v.tensor_copy(add_mask[:, 0, 0:P], c.causal[:, :]))
                step.wait()


OD = dict(q=0, kc=1024, vc=1280, ks=1536, vs=1792, kw=2048, vw=2304, gates=2560)
GW = NSA_G * NSA_D


def odd_weights(A):
    w_in, w_out = A["od_w_in"][0], A["od_w_out"][0]
    view = w_in.rearrange("(k p) n -> p k n", p=P)

    def q_tile(i, j):
        return [((slice(None), slice(None), slice(64 * b, 64 * b + 64)),
                 view[:, :, bass.ds(i * 512 + (b * 256 + j * 64), 64)]) for b in range(2)]

    def k_tile(i, b):
        return [(ALL, view[:, :, bass.ds(i * 512 + (OD["kc"] + b * P), P)])]

    def out_tile(i, m):
        return [((slice(64 * b, 64 * b + 64), slice(4 * g, 4 * g + 4), slice(None)),
                 w_out[g * 512 + b * 256:g * 512 + b * 256 + 256, :].rearrange("(j d) n -> d j n", d=64)[:, :, bass.ds(i * 512 + m * P, P)])
                for b in range(2) for g in range(2)]
    return dict(q=Weights(2, 4, q_tile), k=Weights(3, 2, k_tile), vc=columns(w_in, 1, 2, OD["vc"]), out=Weights(2, 4, out_tile))


def odd_mix(c, A, w, ahead):
    nc = c.nc
    w_in = A["od_w_in"][0]
    with c.stage() as ctx:
        c.h = c.halves(ctx, "h", [P, KD, T])
        oT = ctx.sbuf("oT", [P, KD, T])
        with c.stage() as ctx:
            qT = ctx.sbuf("qT", [P, KD, T])
            kT = ctx.sbuf("kT", [P, 6, T])
            vs, vw = (ctx.sbuf(n, [P, TT, GW]) for n in ("vs", "vw"))
            gates = ctx.sbuf("gates", [P, TT, 3 * NSA_H])
            order = ctx.sbuf("order", [P, TT, 3, NSA_H])
            pcT = ctx.sbuf("pcT", [P, 4, T])
            vcr = ctx.sbuf("vcr", [P, 2, NSA_D])
            with c.stage() as inner:
                w_rows = RowWeights(w_in, [(OD["vs"], GW, vs, ACT.Copy), (OD["vw"], GW, vw, ACT.Copy), (OD["gates"], 3 * NSA_H, gates, ACT.Sigmoid)])
                rms_norm(c, A["norm_mix"][1], c.h, w_rows)
                project_rows(c, w_rows, ahead=w["q"])
                rope64 = Rope(c, inner, 64)
                project_rope(c, w["q"], rope64.tables, NSA_D ** -0.5, qT, w["k"])
                project_rope(c, w["k"], rope64.tables, 1.0, kT, w["vc"])
            reorder_gates(c, gates, order)
            compressed(c, A, w, qT, kT, order, pcT, vcr)
            nsa_attention(c, qT, kT, vs, vw, order, pcT, vcr, oT)
        project_add(c, w["out"], c.xT, c.h, oT, ahead)


def reorder_gates(c, gates, order):
    nc = c.nc
    with c.stage() as ctx:
        with nc.Block() as block:

            @block.vector
            def _(dve):
                step = Chain(dve, c.dve_step)
                for t in range(TT):
                    for kind in range(3):
                        for i in range(2):
                            step.mark(nc.vector.tensor_copy(order[:, t, kind, 8 * i:8 * i + 8].rearrange("p (j b) -> p j b", b=2),
                                                            gates[:, t, 24 * i + kind:24 * i + 24:3].rearrange("p (b j) -> p j b", b=2)))
                step.wait()


def compressed(c, A, w, qT, kT, order, pcT, vcr):
    nc = c.nc
    NP = CMP_N + 1
    PAIRS_L = CMP_LEN // 2
    with c.stage() as ctx:
        w1 = ctx.sbuf("w1", [P, 2, PAIRS_L, P])
        w2 = ctx.sbuf("w2", [P, 2, NSA_D])
        pe_rows = ctx.sbuf("pe_rows", [PAIRS_L, 2, P])
        masks = ctx.sbuf("masks", [P, 2, TT, NP])
        cmp_in = ctx.sem("cmp_in")
        with nc.Block() as block:

            @block.sync
            def _(sp):
                for z in range(2):
                    sp.dma_start(w1[:, z, :, :], A["od_cmp_w1"][0, z].rearrange("(m f) e -> f m e", f=P)).then_inc(cmp_in, 16)
                    sp.dma_start(pe_rows[:, z, :], A["od_cmp_pe"][0, z].rearrange("(m two) d -> m (two d)", two=2)).then_inc(cmp_in, 16)
                sp.dma_start(w2[:, :, :], A["od_cmp_w2"][0].rearrange("z e d -> e z d")).then_inc(cmp_in, 16)
                sp.dma_start(masks[:, 0, :, :], c.ins["c_cmp_add"]).then_inc(cmp_in, 16)
                sp.dma_start(masks[:, 1, :, :], c.ins["c_cmp_seen"]).then_inc(cmp_in, 16)
        n_in = 16 * 7
        vcT = ctx.sbuf("vcT", [P, 2, T])
        project_copy(c, w["vc"], vcT, w["out"])
        tokens = ctx.sbuf("tokens", [P, 2, 2, 2, T])
        peT = ctx.sbuf("peT", [P, 2, PAIRS_L])
        pe_bias = ctx.sbuf("pe_bias", [P, 2])
        hidden = ctx.sbuf("hidden", [P, 2, 2, 2, NP])
        spread = ctx.sbuf("spread", [P, 2, 2, 2, NP])
        kcT = ctx.sbuf("kcT", [P, 2, NP])
        s = ctx.sbuf("s", [P, TT, NSA_H, NP])
        stat = ctx.sbuf("stat", [P, 2, TT, NSA_H])
        padded, made, biased, hid, spread_done, kv_made, kv_done, pe_turned, pe_moved = (
            ctx.sem(n) for n in ("padded", "made", "biased", "hid", "spread_done", "kv_made", "kv_done", "pe_turned", "pe_moved"))
        scored, less, exped, weighed, turned, copied = (ctx.sem(n) for n in ("scored", "less", "exped", "weighed", "turned", "copied"))
        tokens_in = [ctx.sem(f"tokens_in{z}") for z in range(2)]
        source = (kT, vcT)
        half = lambda b: slice(64 * b, 64 * b + 64)
        with nc.Block() as block:

            @block.sync
            def _(sp):
                for z in range(2):
                    for b in range(2):
                        for after in range(2):
                            sp.dma_start(tokens[half(after), z, b, :, 0:T - after], source[z][half(b), 0:2, after:T]).then_inc(tokens_in[z], 16)

            @block.gpsimd
            def _(pool):
                nc.gpsimd.memset(hidden[:, :, :, :, :], 0.0).then_inc(padded, 1)

            @block.tensor
            def _(pe):
                pe.wait_ge(cmp_in, n_in)
                for z in range(2):
                    tr = nc.tensor.transpose(c.ps[:, 1, z * PAIRS_L:(z + 1) * PAIRS_L], pe_rows[:, z, :], c.ident[0:PAIRS_L, 0:PAIRS_L])
                tr.then_inc(pe_turned, 1)
                pe.wait_ge(pe_moved, 1)
                for z in range(2):
                    for m in range(PAIRS_L):
                        mm = nc.tensor.matmul(c.ps[:, 2 * z, 0:1], w1[:, z, m, :], peT[:, z, m:m + 1], start=(m == 0), stop=(m == PAIRS_L - 1))
                    mm.then_inc(made, 1)
                    pe.wait_ge(tokens_in[z], 16 * 4)
                    for m in range(PAIRS_L):
                        block_tokens = tokens[:, z, :, :, 2 * m:2 * m + CMP_STRIDE * (CMP_N - 1) + 1:CMP_STRIDE]
                        mm = nc.tensor.matmul(c.ps[:, 4 + 2 * z, 0:4 * CMP_N].rearrange("p (b i n) -> p b i n", b=2, i=2), w1[:, z, m, :], block_tokens,
                                              start=(m == 0), stop=(m == PAIRS_L - 1))
                    mm.then_inc(made, 1)
                pe.wait_ge(hid, 4)
                for b in range(2):
                    mm = nc.tensor.matmul(c.ps[half(b), 0, 0:2 * NP], w2[:, 0, :], hidden[:, 0, b, :, :].rearrange("p i n -> p (i n)"), start=True, stop=True)
                mm.then_inc(kv_made, 1)
                pe.wait_ge(spread_done, 2)
                for i in range(2):
                    mm = nc.tensor.matmul(c.ps[:, 1, i * NSA_D:(i + 1) * NSA_D], spread[:, i, :, :, :].rearrange("p a b n -> p (a b n)"), w2[:, 1, :],
                                          start=True, stop=True)
                mm.then_inc(kv_made, 1)
                pe.wait_ge(kv_done, 2)
                for t in range(TT):
                    for h in range(NSA_H):
                        i, j, b = h // 8, (h // 2) % 4, h % 2
                        mm = nc.tensor.matmul(c.ps[:, 2 * t + b, (h // 2) * NP:(h // 2 + 1) * NP], qT[half(b), 4 * i + j, t * P:(t + 1) * P], kcT[half(b), i, :],
                                              start=True, stop=True)
                    mm.then_inc(scored, 1)
                for t in range(TT):
                    pe.wait_ge(weighed, t + 1)
                    for m in range(4):
                        tr = nc.tensor.transpose(c.ps[:, t, m * P:(m + 1) * P], s[:, t, 4 * m:4 * m + 4, :].rearrange("p h n -> p (h n)"), c.ident[:, :])
                    tr.then_inc(turned, 1)

            @block.scalar
            def _(act):
                act.wait_ge(pe_turned, 1)
                nc.scalar.activation(peT[:, :, :], c.ps[:, 1, 0:2 * PAIRS_L].rearrange("p (z m) -> p z m", z=2), ACT.Copy).then_inc(pe_moved, 1)
                act.wait_ge(padded, 1)
                for z in range(2):
                    act.wait_ge(made, 2 * z + 1)
                    nc.scalar.activation(pe_bias[:, z:z + 1], c.ps[:, 2 * z, 0:1], ACT.Copy).then_inc(biased, 1)
                    act.wait_ge(biased, z + 1)
                    for b in range(2):
                        act.wait_ge(made, 2 * z + 2)
                        nc.scalar.activation(hidden[:, z, b, :, 0:CMP_N], c.ps[:, 4 + 2 * z, 2 * b * CMP_N:2 * (b + 1) * CMP_N].rearrange("p (i n) -> p i n", i=2),
                                             ACT.Gelu_apprx_tanh, bias=pe_bias[:, z:z + 1]).then_inc(hid, 1)
                act.wait_ge(kv_made, 1)
                nc.scalar.activation(kcT[:, :, :], c.ps[:, 0, 0:2 * NP].rearrange("p (i n) -> p i n", i=2), ACT.Copy).then_inc(kv_done, 1)
                act.wait_ge(kv_made, 2)
                nc.scalar.activation(vcr[:, :, :], c.ps[:, 1, 0:P].rearrange("p (i d) -> p i d", i=2), ACT.Copy).then_inc(kv_done, 1)
                for t in range(TT):
                    act.wait_ge(less, t + 1)
                    nc.scalar.activation(s[:, t, :, :], s[:, t, :, :], ACT.Exp).then_inc(exped, 1)
                for t in range(TT):
                    act.wait_ge(turned, t + 1)
                    nc.scalar.activation(pcT[:, :, t * P:(t + 1) * P], c.ps[:, t, :].rearrange("p (m q) -> p m q", m=4), ACT.Copy).then_inc(copied, 1)
                act.wait_ge(copied, TT)

            @block.vector
            def _(dve):
                v = nc.vector
                step = Chain(dve, c.dve_step)
                dve.wait_ge(hid, 4)
                for a in range(2):
                    v.tensor_copy(spread[:, :, a, :, :], hidden[:, 1, :, :, :].rearrange("p b i n -> p i b n")).then_inc(spread_done, 1)
                full = [P, NSA_H, NP]
                for t in range(TT):
                    dve.wait_ge(scored, t + 1)
                    st, top, den = s[:, t, :, :], stat[:, 0, t, :], stat[:, 1, t, :]
                    for b in range(2):
                        step.mark(v.tensor_tensor(s[:, t, b::2, :], c.ps[:, 2 * t + b, 0:NSA_H // 2 * NP].rearrange("p (h n) -> p h n", n=NP),
                                                  masks[:, 0, t, :].unsqueeze(1).to_broadcast([P, NSA_H // 2, NP]), ALU.add))
                    step.wait()
                    step(v.tensor_reduce(top, st, AX.X, ALU.max))
                    v.tensor_tensor(st, st, top.unsqueeze(2).to_broadcast(full), ALU.subtract).then_inc(less, 1)
                for t in range(TT):
                    dve.wait_ge(exped, t + 1)
                    st, zero, den = s[:, t, :, :], stat[:, 0, t, :], stat[:, 1, t, :]
                    step(v.tensor_tensor(st, st, masks[:, 1, t, :].unsqueeze(1).to_broadcast(full), ALU.mult))
                    step(v.tensor_reduce(den, st, AX.X, ALU.add))
                    step(v.tensor_scalar(zero, den, 0.0, None, ALU.is_equal))
                    step(v.tensor_tensor(den, den, zero, ALU.add))
                    step(v.reciprocal(den, den))
                    step(v.tensor_tensor(den, den, order[:, t, 0, :], ALU.mult))
                    v.tensor_tensor(st, st, den.unsqueeze(2).to_broadcast(full), ALU.mult).then_inc(weighed, 1)


def nsa_attention(c, qT, kT, vs, vw, order, pcT, vcr, oT):
    with c.stage() as ctx:
        q = [ctx.sbuf(f"q{jj}", [P, T]) for jj in range(2)]
        k = [ctx.sbuf(n, [P, T]) for n in ("k_sel", "k_win")]
        v = [ctx.sbuf(n, [P, TT, P]) for n in ("v_sel", "v_win")]
        pc = ctx.sbuf("pc", [P, T])
        vc = ctx.sbuf("vc", [P, NSA_D])

        staging = {"q0": lambda m: [(q[0][:, :], qT[:, m * 2, :])], "q1": lambda m: [(q[1][:, :], qT[:, m * 2 + 1, :])],
                   "cmp": lambda m: [(vc[:, :], vcr[:, m // 2, :]), (pc[:, :], pcT[:, m, :])]}
        for kind, buf in enumerate((vs, vw)):
            staging[f"kv{kind}"] = lambda m, kind=kind, buf=buf: [(k[kind][:, :], kT[:, m // 2 + (2 + 2 * kind), :]),
                                                                  (v[kind][:, :, :], buf[:, :, bass.ds(m // 2 * P, P)])]

        def head(jj, b, kind):
            half = slice(64 * b, 64 * b + 64)
            unit = dict(q=q[jj][half, :], k=lambda m: k[kind][half, :], v=lambda j: v[kind][:, j, half], mask=None,
                        slots=[f"q{jj}", f"kv{kind}"] + ["cmp"] * (kind == 0),
                        gate=lambda m, t: order[:, t, 1 + kind, bass.ds(m * 4 + (2 * jj + b), 1)],
                        out=c.ps[half, 7, :], sum=c.ps[:, 7, :], first=kind == 0, last=kind == 1)
            if kind == 0:
                rows = slice(32 * (2 * jj + b), 32 * (2 * jj + b) + 32)
                unit["add"], unit["add_to"] = vc[rows, :], lambda m: pc[rows, :]
            return unit
        attention(c, 4, [head(jj, b, kind) for jj in range(2) for b in range(2) for kind in range(2)], 1.0, staging,
                  {3: lambda m: oT[:, m * 2, :], 7: lambda m: oT[:, m * 2 + 1, :]})


FIRST = ("mix_norm_g w_in ssm_a_re ssm_a_im ssm_log_step ssm_b_re ssm_b_im ssm_c_re ssm_c_im ssm_d ssm_w_glu "
         "fox_forget_bias q_norm_g k_norm_g w_out ffn_norm_g peer_w_query peer_sub_keys").split()
SECOND = ("norm_mix norm_ffn norm_final ev_w_in ev_kv_gain ev_w_uk ev_w_uv ev_lambda ev_subln ev_w_out "
          "od_w_in od_cmp_pe od_cmp_w1 od_cmp_w2 od_w_out ffn_w_gate ffn_w_up ffn_w_down").split()


def constants():
    row, token = np.arange(P), np.arange(T)
    made = {
        "c_ident": np.eye(P),
        "c_causal": np.where(row[None] <= row[:, None], 0.0, NEG),
        "c_minus_tri": np.where(row[:, None] <= token[None], -1.0, 0.0),
        "c_iota": np.tile(np.arange(TOPK), (P, 1)),
        "c_head_rows": row[:, None] // 32 == np.arange(4)[None],
    }
    for dim in (32, 64):
        rates = (10000.0 ** (-np.arange(0, dim, 2) / dim)).astype(np.float32)
        angles = (token.astype(np.float32)[:, None] * rates[None]).T
        made[f"c_cos{dim}"] = np.tile(np.cos(angles), (P // dim * 2, 1))
        made[f"c_sin{dim}"] = np.tile(np.sin(angles), (P // dim * 2, 1))
        swap = np.zeros((P, P))
        for r in range(P):
            second = r % dim >= dim // 2
            swap[r - dim // 2 if second else r + dim // 2, r] = 1.0 if second else -1.0
        made[f"c_swap{dim}"] = swap
    block = np.arange(CMP_N + 1)
    query = np.arange(TT)[None, :, None] * P + row[:, None, None]
    seen = (block * CMP_STRIDE + CMP_LEN - 1 <= query) & (block < CMP_N)
    made["c_cmp_add"], made["c_cmp_seen"] = np.where(seen, 0.0, NEG), seen
    return {name: table.astype(np.float32) for name, table in made.items()}


def build(nc, ins, out):
    with ExitStack() as ctx:
        c = Core(nc, ctx, ins)
        w_query = columns(ins["peer_w_query"][0], PEER_H // 2, 4)
        w_even, w_odd = even_weights(ins), odd_weights(ins)
        w_ffn = [ffn_weights(ins["ffn_w_gate"][n], ins["ffn_w_up"][n], ins["ffn_w_down"][n]) for n in range(2)]
        load_consts(c)
        first_mix(c, ins, w_query)
        peer(c, ins, w_query)
        even_mix(c, ins, w_even, w_ffn[0][0])
        ffn(c, ins["norm_ffn"][0], w_ffn[0])
        odd_mix(c, ins, w_odd, w_ffn[1][0])
        ffn(c, ins["norm_ffn"][1], w_ffn[1])
        store_normed(c, ins["norm_final"], out)


def kernel(**inputs):
    import concourse.bacc as bacc
    from concourse.bass_utils import run_bass_kernel_spmd

    arrays = {"x": inputs["x"]}
    arrays.update({name: inputs[name] for name in FIRST})
    arrays.update({name: inputs[name + "_2"] for name in SECOND})
    arrays["peer_uv"] = np.concatenate([np.asarray(inputs["peer_u"])[0], np.asarray(inputs["peer_v"])[0]], axis=1)
    arrays.update(constants())
    arrays = {name: np.ascontiguousarray(a) for name, a in arrays.items()}
    nc = bacc.Bacc("TRN2", target_bir_lowering=False, num_devices=1)
    ins = {name: nc.dram_tensor(f"in_{name}_dram", a.shape, mybir.dt.from_np(a.dtype), kind="ExternalInput").ap() for name, a in arrays.items()}
    out = nc.dram_tensor("out_0_dram", (1, T, D), F32, kind="ExternalOutput").ap()
    build(nc, ins, out)
    result = run_bass_kernel_spmd(nc, [{f"in_{name}_dram": a for name, a in arrays.items()}], core_ids=[0])
    return result.results[0]["out_0_dram"]
```

```python
import math
from collections import namedtuple
from contextlib import ExitStack

import numpy as np
import concourse.bass as bass
from concourse import mybir

F32 = mybir.dt.float32
BF16 = mybir.dt.bfloat16
F32R = mybir.dt.float32r
U32 = mybir.dt.uint32
ALU = mybir.AluOpType
ACT = mybir.ActivationFunctionType
AX = mybir.AxisListType

P = 128
T = 512
TT = T // P
D = 1024
KD = D // P
EPS = 1e-6
NEG = -1.0e30
LOWEST = -3.0e38

SSM_W, SSM_H, SSM_G, SSM_S = 512, 16, 32, 64
PAIRS = SSM_G // 2
SSM_T = SSM_W // P
FOX_H = 8
PEER_H, PEER_K, TOPK = 8, 128, 16
SLOTS = PEER_H * TOPK

DSA_H, DSA_SEL = 8, T // 4
DIFF_H = 4
NSA_G, NSA_HPG, NSA_D = 4, 4, 64
NSA_H = NSA_G * NSA_HPG
CMP_LEN, CMP_STRIDE = 32, 16
CMP_N = T // CMP_STRIDE - 1
D_FF = 2816
KF = D_FF // P

W_SLOTS = 4
W_SLOT = KD * P


class Tally:

    def __init__(self, sem):
        self.sem = sem
        self.n = 0

    def inc(self, ins, by=1):
        ins.then_inc(self.sem, by)
        self.n += by
        return self.n


def hold(eng, sem, value, tick):
    eng.wait_ge(sem, value)
    eng.sem_inc(tick, 1)


class Chain:

    def __init__(self, eng, tally, turn=None, per=0, tick=None):
        self.eng, self.tally, self.turn, self.per, self.tick = eng, tally, turn, per, tick
        self.base = tally.n
        self.k = 0

    def __call__(self, ins):
        self.k += 1
        ins.then_inc(self.tally.sem, 1)
        if self.turn is None:
            self.tally.n += 1
        self.wait()

    def mark(self, ins):
        self.k += 1
        ins.then_inc(self.tally.sem, 1)
        if self.turn is None:
            self.tally.n += 1

    def wait(self):
        if self.turn is None:
            self.eng.wait_ge(self.tally.sem, self.tally.n)
        elif self.tick is None:
            self.eng.wait_ge(self.tally.sem, self.turn * self.per + (self.base + self.k))
        else:
            hold(self.eng, self.tally.sem, self.turn * self.per + (self.base + self.k), self.tick)

    def ends(self, turns):
        assert self.k == self.per, (self.k, self.per)
        self.tally.n += turns * self.per


Halves = namedtuple("Halves", "high low")


def rounded(ap):
    return ap.bitcast(F32R)


def high_half(nc, high, whole):
    return nc.scalar.activation(rounded(high), whole, ACT.Copy)


def low_half(eng, low, whole, high):
    return eng.tensor_tensor(rounded(low), whole, high, ALU.subtract)


def product(nc, out, w_high, w_low, x_high, x_low, start, stop, **more):
    nc.tensor.matmul(out, rounded(w_high), rounded(x_low), start=start, stop=False, **more)
    nc.tensor.matmul(out, rounded(w_high), rounded(x_high), start=False, stop=False, **more)
    return nc.tensor.matmul(out, rounded(w_low), rounded(x_high), start=False, stop=stop, **more)


class Core:

    def __init__(self, nc, ctx, ins):
        self.nc, self.ctx, self.ins = nc, ctx, ins
        self.names = 0
        self.xT = self.sbuf(ctx, "xT", [P, KD, T])
        self.w_ring = self.sbuf(ctx, "w_ring", [P, W_SLOTS, W_SLOT])
        self.h = None
        self.ident = self.sbuf(ctx, "ident", [P, P])
        self.ones = self.sbuf(ctx, "ones", [P, P])
        self.eps = self.sbuf(ctx, "eps", [P, 1])
        self.causal = self.sbuf(ctx, "causal", [P, P])
        self.mask_ident = self.sbuf(ctx, "mask_ident", [P, P], BF16)
        self.mask_causal = self.sbuf(ctx, "mask_causal", [P, P], BF16)
        self.ps = ctx.enter_context(nc.psum_tensor("ps", [P, 8, T], F32))
        self.rows_in = [Tally(self.sem(f"rows_in{b}")) for b in range(2)]
        self.w_in = [Tally(self.sem(f"w_in{b}")) for b in range(W_SLOTS)]
        self.dve_step = Tally(self.sem("dve_step"))
        self.x_saved, self.x_back = self.sem("x_saved"), self.sem("x_back")
        self.x_dram = nc.dram_tensor("x_transposed", (P, KD, T), F32).ap()
        self.dve_tick, self.pool_tick, self.sp_tick = self.sem("dve_tick"), self.sem("pool_tick"), self.sem("sp_tick")

    def sbuf(self, ctx, name, shape, dt=F32):
        self.names += 1
        return ctx.enter_context(self.nc.sbuf_tensor(f"{name}_{self.names}", shape, dt))

    def halves(self, ctx, name, shape):
        return Halves(ctx.sbuf(f"{name}_high", shape), ctx.sbuf(f"{name}_low", shape))

    def sem(self, name):
        self.names += 1
        return self.nc.alloc_semaphore(f"{name}_{self.names}")

    def stage(self):
        return Stage(self)


class Stage:

    def __init__(self, core):
        self.core = core
        self.memory = ExitStack()
        self.sems = []

    def __enter__(self):
        return self

    def __exit__(self, *failed):
        if not any(failed) and self.sems:
            self.core.nc.clear_and_free_semaphores(self.sems)
            self.core.nc.all_engine_barrier(sem_only=True)
        self.memory.close()

    def sbuf(self, name, shape, dt=F32):
        return self.core.sbuf(self.memory, name, shape, dt)

    def sem(self, name):
        self.sems.append(self.core.sem(name))
        return self.sems[-1]


def load_consts(c):
    nc = c.nc
    with c.stage() as ctx:
        x_rows = ctx.sbuf("x_rows", [P, TT, D])
        consts_in, x_in = ctx.sem("consts_in"), ctx.sem("x_in")
        ones_set, masks_set, transposed, copied = ctx.sem("ones_set"), ctx.sem("masks_set"), ctx.sem("transposed"), ctx.sem("copied")
        with nc.Block() as block:

            @block.sync
            def _(sp):
                sp.dma_start(c.ident[:, :], c.ins["c_ident"]).then_inc(consts_in, 16)
                sp.dma_start(c.causal[:, :], c.ins["c_causal"]).then_inc(consts_in, 16)
                sp.dma_start(x_rows[:, :, :], c.ins["x"][0].rearrange("(t p) d -> p t d", p=P)).then_inc(x_in, 16)

            @block.vector
            def _(dve):
                dve.wait_ge(consts_in, 32)
                nc.vector.tensor_copy(c.mask_ident[:, :], c.ident[:, :]).then_inc(masks_set, 1)
                nc.vector.tensor_copy(c.mask_causal[:, :], c.causal[:, :]).then_inc(masks_set, 1)
                dve.wait_ge(masks_set, 2)

            @block.gpsimd
            def _(pool):
                nc.gpsimd.memset(c.ones[:, :], 1.0).then_inc(ones_set, 1)
                nc.gpsimd.memset(c.eps[:, :], EPS).then_inc(ones_set, 1)
                pool.wait_ge(ones_set, 2)

            @block.tensor
            def _(pe):
                pe.wait_ge(consts_in, 32)
                pe.wait_ge(x_in, 16)
                for k in range(KD):
                    for t in range(TT):
                        tr = nc.tensor.transpose(c.ps[:, k, t * P:(t + 1) * P], x_rows[:, t, k * P:(k + 1) * P], c.ident[:, :])
                    tr.then_inc(transposed, 1)

            @block.scalar
            def _(act):
                for k in range(KD):
                    act.wait_ge(transposed, k + 1)
                    nc.scalar.activation(c.xT[:, k, :], c.ps[:, k, :], ACT.Copy).then_inc(copied, 1)
                act.wait_ge(copied, KD)


class Norm:

    def __init__(self, c, ctx, gain, dest, rstd=None, squares=None):
        self.c, self.gain, self.dest = c, gain, dest
        self.gains = ctx.sbuf("gains", [P, KD])
        self.rstd = ctx.sbuf("rstd", [P, T]) if rstd is None else rstd
        self.halves = isinstance(dest, Halves)
        self.squared_x = ctx.sbuf("squares", [P, KD, T]) if squares is None else squares
        self.whole = self.squared_x if self.halves else dest
        self.gain_in, self.squared, self.summed, self.inverted, self.rooted, self.normed, self.high, self.low = (
            ctx.sem(n) for n in ("gain_in", "squared", "summed", "inverted", "rooted", "normed", "x_high", "x_low"))

    def load(self, sp):
        sp.dma_start(self.gains[:, :], self.gain.rearrange("(k p) -> p k", p=P), allow_slow_non_contiguous=True).then_inc(self.gain_in, 16)

    def square(self, act):
        for k in range(KD):
            self.c.nc.scalar.activation(self.squared_x[:, k, :], self.c.xT[:, k, :], ACT.Square).then_inc(self.squared, 1)

    def sum(self, pe):
        for k in range(KD):
            pe.wait_ge(self.squared, k + 1)
            mm = self.c.nc.tensor.matmul(self.c.ps[:, 7, :], self.c.ones[:, :], self.squared_x[:, k, :], start=(k == 0), stop=(k == KD - 1))
        mm.then_inc(self.summed, 1)
        pe.wait_ge(self.rooted, 1)

    def root(self, act):
        act.wait_ge(self.summed, 1)
        self.c.nc.scalar.activation(self.rstd[:, :], self.c.ps[:, 7, :], ACT.Sqrt, bias=self.c.eps[:, 0:1], scale=1.0 / D).then_inc(self.rooted, 1)

    def split(self, act):
        if self.halves:
            for k in range(KD):
                act.wait_ge(self.normed, k + 1)
                high_half(self.c.nc, self.dest.high[:, k, :], self.whole[:, k, :]).then_inc(self.high, 1)

    def apply(self, dve):
        v = self.c.nc.vector
        dve.wait_ge(self.rooted, 1)
        v.reciprocal(self.rstd[:, :], self.rstd[:, :]).then_inc(self.inverted, 1)
        dve.wait_ge(self.gain_in, 16)
        dve.wait_ge(self.inverted, 1)

        def rest(k):
            dve.wait_ge(self.high, k + 1)
            low_half(v, self.dest.low[:, k, :], self.whole[:, k, :], self.dest.high[:, k, :]).then_inc(self.low, 1)

        for k in range(KD):
            v.scalar_tensor_tensor(self.whole[:, k, :], self.c.xT[:, k, :], self.gains[:, k:k + 1], self.rstd[:, :], ALU.mult, ALU.mult).then_inc(self.normed, 1)
            if self.halves and k >= 1:
                rest(k - 1)
        if self.halves:
            rest(KD - 1)
        dve.wait_ge(self.normed, KD)

    def wait(self, pe, k):
        pe.wait_ge(self.low, k + 1)


class Weights:

    def __init__(self, turns, per_turn, source, kt=KD, parts=1):
        self.turns, self.per_turn, self.source, self.parts = turns, per_turn, source, parts
        self.kt = [kt] * per_turn if isinstance(kt, int) else kt
        self.pieces = [len(source(0, b)) for b in range(per_turn)]
        self.base = None

    def slot(self, buf, b):
        return buf[:, b, 0:self.kt[b] * P].rearrange("p (k n) -> p k n", n=P)

    def load(self, c, sp, i, b):
        for place, view in self.source(i, b):
            sp.dma_start(self.slot(c.w_ring, b)[place], view).then_inc(c.w_in[b].sem, 16)

    def ring_slots(self, b):
        return (b,)

    def count(self, c):
        if self.base is None:
            self.base = [c.w_in[b].n for b in range(self.per_turn)]
            for b in range(self.per_turn):
                c.w_in[b].n += 16 * self.pieces[b] * self.turns
            return True
        return False


def project(c, w, evacuate, rhs=None, ahead=None, whole=None, before={}, after={}, norm=None):
    nc = c.nc
    rhs = c.h if rhs is None else rhs
    rhs = rhs if isinstance(rhs, list) else [rhs] * w.per_turn
    turns, per_turn, parts = w.turns, w.per_turn, w.parts
    ctx = c.stage()
    mm_done, bank_free, high, low = (ctx.sem(n) for n in ("mm_done", "bank_free", "high", "low"))
    x_high, x_low = ctx.sem("x_high"), ctx.sem("x_low")
    w_halves = c.halves(ctx, "w", [P, per_turn, max(w.kt) * P])
    fresh = w.count(c)
    if ahead is not None:
        ahead.count(c)

    def ready(i, b):
        return i * per_turn + (per_turn + b + 1)

    def freed(i, b):
        return i * per_turn + (b + 1)

    def turn_loop(eng, body, first=0, last=turns):
        if last - first == 1:
            body(first)
        elif last > first:
            with eng.Fori(first, last) as i:
                body(i)

    with nc.Block() as block:

        @block.sync
        def _(sp):
            if fresh:
                for b in range(per_turn):
                    w.load(c, sp, 0, b)
            if norm is not None:
                norm.load(sp)
            if "sp" in before:
                before["sp"](sp)

            def body(i):
                for b in range(per_turn):
                    hold(sp, low, (i - 1) * per_turn + (b + 1), c.sp_tick)
                    w.load(c, sp, i, b)
            turn_loop(sp, body, 1)
            if ahead is not None:
                for b in range(ahead.per_turn):
                    mine = [s for s in ahead.ring_slots(b) if s < per_turn]
                    if mine:
                        sp.wait_ge(low, (turns - 1) * per_turn + (max(mine) + 1))
                    ahead.load(c, sp, 0, b)

        @block.gpsimd
        def _(pool):
            def body(i):
                for b in range(per_turn):
                    pool.wait_ge(high, i * per_turn + (b + 1))
                    low_half(nc.gpsimd, *(buf[:, b, 0:w.kt[b] * P] for buf in (w_halves.low, c.w_ring, w_halves.high))).then_inc(low, 1)
            turn_loop(pool, body)

        @block.tensor
        def _(pe):
            pe.sem_inc(mm_done, per_turn)
            pe.sem_inc(bank_free, per_turn)
            if norm is not None:
                norm.sum(pe)
            if "pe" in before:
                before["pe"](pe)
            if whole is not None:
                pe.wait_ge(x_low, whole.shape[1])

            def body(i):
                for b in range(per_turn):
                    part, bank = b % parts, b // parts
                    pe.wait_ge(low, i * per_turn + (b + 1))
                    if part == 0:
                        pe.wait_ge(bank_free, freed(i, b))
                    for k in range(w.kt[b]):
                        if norm is not None and b == 0:
                            norm.wait(pe, k)
                        x = sum(w.kt[b - part:b]) + k
                        mm = product(nc, c.ps[:, bank, :], w.slot(w_halves.high, b)[:, k, :], w.slot(w_halves.low, b)[:, k, :],
                                     rhs[b].high[:, x, :], rhs[b].low[:, x, :],
                                     start=(part == 0 and k == 0), stop=(part == parts - 1 and k == w.kt[b] - 1))
                    mm.then_inc(mm_done, 1)
                    if "pe" in evacuate and b >= 1:
                        evacuate["pe"](pe, i, b - 1, bank_free)
                if "pe" in evacuate:
                    evacuate["pe"](pe, i, per_turn - 1, bank_free)
            turn_loop(pe, body)
            if "pe" in after:
                after["pe"](pe)

        @block.scalar
        def _(act):
            def split(i, b):
                act.wait_ge(c.w_in[b].sem, i * (16 * w.pieces[b]) + (w.base[b] + 16 * w.pieces[b]))
                act.wait_ge(mm_done, freed(i, b))
                high_half(nc, w_halves.high[:, b, 0:w.kt[b] * P], c.w_ring[:, b, 0:w.kt[b] * P]).then_inc(high, 1)

            def start():
                if whole is not None:
                    for k in range(whole.shape[1]):
                        high_half(nc, rhs[0].high[:, k, :], whole[:, k, :]).then_inc(x_high, 1)

            if "act" not in evacuate:
                start()
                turn_loop(act, lambda i: [split(i, b) for b in range(per_turn)])
                return
            if norm is not None:
                norm.square(act)
            if "act_first" in before:
                before["act_first"](act)
            lag = 1 if per_turn > 2 else 0
            for b in range(per_turn if turns == 1 else per_turn - lag):
                split(0, b)
                if b == 0:
                    start()
                    if norm is not None:
                        norm.root(act)
            if norm is not None:
                norm.split(act)
            if "act" in before:
                before["act"](act)

            def body(i, final=False):
                def next_split(b):
                    if turns > 1 and b < lag:
                        split(i, per_turn - lag + b)
                    elif not final:
                        split(i + 1, b - lag)
                evacuate["act"](act, i, lambda b: act.wait_ge(mm_done, ready(i, b)), bank_free, next_split)
            turn_loop(act, body, 0, turns - 1)
            body(turns - 1, True)
            act.wait_ge(bank_free, per_turn * (turns + 1))
            if "act" in after:
                after["act"](act)

        @block.vector
        def _(dve):
            if norm is not None:
                norm.apply(dve)
            if "dve" in before:
                before["dve"](dve)
            if whole is not None:
                for k in range(whole.shape[1]):
                    dve.wait_ge(x_high, k + 1)
                    low_half(nc.vector, rhs[0].low[:, k, :], whole[:, k, :], rhs[0].high[:, k, :]).then_inc(x_low, 1)
            if "dve" in evacuate:
                turn_loop(dve, lambda i: evacuate["dve"](dve, i, lambda b: dve.wait_ge(mm_done, ready(i, parts * b + parts - 1)), bank_free))
                dve.wait_ge(bank_free, per_turn * (turns + 1))
            if "dve" in after:
                after["dve"](dve)
    ctx.__exit__()


ALL = (slice(None), slice(None), slice(None))


def columns(w, turns, per_turn, col0=0):
    view = w.rearrange("(k p) n -> p k n", p=P)

    def source(i, b):
        at = i * (per_turn * P) + (col0 + b * P)
        return [(ALL, view[:, :, bass.ds(at, P)])]
    return Weights(turns, per_turn, source, view.shape[1])


def tile_of(buf, i, per_turn, b):
    return buf[:, i * per_turn + b, :]


def project_copy(c, w, dest, ahead=None, before={}, after={}, norm=None):
    nc = c.nc

    def act(eng, i, wait_tile, bank_free, split):
        for b in range(w.per_turn):
            wait_tile(b)
            nc.scalar.activation(tile_of(dest, i, w.per_turn, b), c.ps[:, b, :], ACT.Copy).then_inc(bank_free, 1)
            split(b)
    project(c, w, {"act": act}, ahead=ahead, before=before, after=after, norm=norm)


def project_add(c, w, dest, rhs, whole=None, ahead=None, before={}):
    nc = c.nc

    def dve(eng, i, wait_tile, bank_free):
        for b in range(w.per_turn // w.parts):
            wait_tile(b)
            d = tile_of(dest, i, w.per_turn // w.parts, b)
            nc.vector.tensor_tensor(d, d, c.ps[:, b, :], ALU.add).then_inc(bank_free, w.parts)
    project(c, w, {"dve": dve}, rhs, ahead, whole, before)


def project_swiglu(c, w, gain, dest, ahead=None):
    nc = c.nc
    with c.stage() as ctx:
        gate = ctx.sbuf("gate", [P, 2, T])
        norm = Norm(c, ctx, gain, c.h, rstd=gate[:, 0, :])
        gated, made, dest_high, dest_low = (ctx.sem(n) for n in ("gated", "made", "dest_high", "dest_low"))

        def act(eng, i, wait_tile, bank_free, split):
            for j in range(2):
                wait_tile(2 * j)
                eng.wait_ge(dest_low, i * 2 + (j + 1))
                nc.scalar.activation(gate[:, j, :], c.ps[:, 2 * j, :], ACT.Silu).then_inc(gated, 1)
                split(2 * j)
                eng.wait_ge(made, i * 2 + (j + 1))
                high_half(nc, tile_of(dest.high, i, 2, j), gate[:, j, :]).then_inc(dest_high, 1)
                split(2 * j + 1)

        def dve(eng, i, wait_tile, bank_free):
            for j in range(2):
                wait_tile(2 * j + 1)
                eng.wait_ge(gated, i * 2 + (j + 1))
                nc.vector.tensor_tensor(gate[:, j, :], gate[:, j, :], c.ps[:, 2 * j + 1, :], ALU.mult).then_inc(made, 1)
                eng.wait_ge(made, i * 2 + (j + 1))
                eng.sem_inc(bank_free, 2)
                eng.wait_ge(dest_high, i * 2 + (j + 1))
                low_half(nc.vector, tile_of(dest.low, i, 2, j), gate[:, j, :], tile_of(dest.high, i, 2, j)).then_inc(dest_low, 1)

        project(c, w, {"act": act, "dve": dve}, ahead=ahead, before={"dve": lambda eng: eng.sem_inc(dest_low, 2)},
                after={"dve": lambda eng: eng.wait_ge(dest_low, 2 * w.turns + 2)}, norm=norm)


def project_rope(c, w, tables, scales, dest, ahead=None, before={}, after={}):
    nc = c.nc
    per_turn = w.per_turn
    with c.stage() as ctx:
        raw = ctx.sbuf("raw", [P, per_turn, T])
        part = ctx.sbuf("part", [P, per_turn, T])
        copied, swapped, scaled = ctx.sem("copied"), ctx.sem("swapped"), ctx.sem("scaled")

        def act(eng, i, wait_tile, bank_free, split):
            for b in range(per_turn):
                wait_tile(b)
                nc.scalar.activation(raw[:, b, :], c.ps[:, b, :], ACT.Copy).then_inc(copied, 1)
                split(b)

        def pe(eng, i, b, bank_free):
            eng.wait_ge(copied, i * per_turn + (b + 1))
            nc.tensor.matmul(c.ps[:, 4 + b, :], tables[b][0][:, :], raw[:, b, :], start=True, stop=True).then_inc(swapped, 1)

        def dve(eng, i, wait_tile, bank_free):
            for b in range(per_turn):
                eng.wait_ge(swapped, i * per_turn + (b + 1))
                nc.vector.scalar_tensor_tensor(dest(i, b), c.ps[:, b, :], scales[b], tables[b][1][:, :], ALU.mult, ALU.mult).then_inc(scaled, 1)
                nc.vector.scalar_tensor_tensor(part[:, b, :], c.ps[:, 4 + b, :], scales[b], tables[b][2][:, :], ALU.mult, ALU.mult).then_inc(scaled, 1)
                eng.wait_ge(scaled, i * (2 * per_turn) + (2 * b + 2))
                nc.vector.tensor_tensor(dest(i, b), dest(i, b), part[:, b, :], ALU.add).then_inc(bank_free, 1)
        project(c, w, {"act": act, "pe": pe, "dve": dve}, ahead=ahead, before=before, after=after)


ROWS_N = 256


class RowWeights:
    per_turn = 2

    def __init__(self, w, outputs, buffers=None):
        self.view = w.rearrange("(k p) n -> p k n", p=P)
        pieces = [(col + at, min(ROWS_N, n - at), (name, at), func) for col, n, name, func in outputs for at in range(0, n, ROWS_N)]
        self.buffers = buffers
        self.chunks = []
        for col, n, dest, func in pieces:
            at = self.columns(-1) if self.chunks else ROWS_N
            if at + n > ROWS_N:
                self.chunks.append([])
                at = 0
            self.chunks[-1].append((at, col, n, dest, func))
        assert all(self.columns(j) == ROWS_N for j in range(len(self.chunks) - 1))
        self.used = [len(x) for x in self.chunks]
        if self.columns(-1) < ROWS_N:
            self.chunks[-1].append((self.columns(-1), 0, ROWS_N - self.columns(-1), None, None))
        self.base = None

    def columns(self, j):
        return sum(n for _, _, n, _, _ in self.chunks[j])

    def ring_slots(self, b):
        return (2 * b, 2 * b + 1)

    def slot(self, buf, j):
        return buf[:, j % 2, 0:KD * self.columns(j)].rearrange("p (k n) -> p k n", k=KD)

    def whole(self, c):
        return c.w_ring[:, :, :].rearrange("p (s two) n -> p s (two n)", two=2)

    def load(self, c, sp, i, b):
        j = 2 * i + b
        if j < len(self.chunks):
            for at, col, n, _, _ in self.chunks[j]:
                sp.dma_start(self.slot(self.whole(c), j)[:, :, at:at + n], self.view[:, :, col:col + n]).then_inc(c.rows_in[b].sem, 16)

    def loaded(self, j):
        return self.base[j % 2] + 16 * sum(len(self.chunks[x]) for x in range(j % 2, j + 1, 2))

    def count(self, c):
        if self.base is not None:
            return False
        self.base = [c.rows_in[b].n for b in range(2)]
        for b in range(2):
            c.rows_in[b].n += 16 * sum(len(x) for x in self.chunks[b::2])
        return True


def project_rows(c, w, beside={}, ahead=None, norm=None):
    nc = c.nc
    n_chunks = len(w.chunks)
    parts = TT * sum(n - 1 for n in w.used)
    fresh = w.count(c)
    if ahead is not None:
        ahead.count(c)
    ctx = c.stage()
    high, low, mm_done, copied, part_copied = (ctx.sem(n) for n in ("rows_high", "rows_low", "rows_done", "rows_copied", "rows_part_copied"))
    w_high, w_low = c.halves(ctx, "w_rows", [P, 2, KD * ROWS_N])
    part = lambda buf, j: buf[:, j % 2, 0:KD * w.columns(j)]
    with nc.Block() as block:

        @block.sync
        def _(sp):
            if norm is not None:
                norm.load(sp)
            for j in range(n_chunks):
                if j >= 2:
                    sp.wait_ge(low, j - 1)
                if j >= 2 or fresh:
                    w.load(c, sp, j // 2, j % 2)
            if ahead is not None:
                sp.wait_ge(low, n_chunks)
                for b in range(ahead.per_turn):
                    ahead.load(c, sp, 0, b)

        @block.gpsimd
        def _(pool):
            for j in range(n_chunks):
                pool.wait_ge(high, j + 1)
                low_half(nc.gpsimd, part(w_low, j), part(w.whole(c), j), part(w_high, j)).then_inc(low, 1)

        @block.tensor
        def _(pe):
            if norm is not None:
                norm.sum(pe)
            for j in range(n_chunks):
                pe.wait_ge(low, j + 1)
                for t in range(TT):
                    if j >= 1:
                        pe.wait_ge(copied, TT * (j - 1) + t + 1)
                    for k in range(KD):
                        if norm is not None and j == t == 0:
                            norm.wait(pe, k)
                        tokens = slice(t * P, (t + 1) * P)
                        mm = product(nc, c.ps[:, t, 0:w.columns(j)], c.h.high[:, k, tokens], c.h.low[:, k, tokens],
                                     w.slot(w_high, j)[:, k, :], w.slot(w_low, j)[:, k, :], start=(k == 0), stop=(k == KD - 1))
                    mm.then_inc(mm_done, 1)
                    if "pe" in beside:
                        beside["pe"](pe, TT * j + t)

        @block.scalar
        def _(act):
            def split(j):
                if j < n_chunks:
                    act.wait_ge(c.rows_in[j % 2].sem, w.loaded(j))
                    if j >= 2:
                        act.wait_ge(mm_done, TT * (j - 1))
                    high_half(nc, part(w_high, j), part(w.whole(c), j)).then_inc(high, 1)

            if norm is not None:
                norm.square(act)
            split(0)
            if norm is not None:
                norm.root(act)
            split(1)
            if norm is not None:
                norm.split(act)
            if "act_first" in beside:
                beside["act_first"](act)
            for j in range(n_chunks):
                for t in range(TT):
                    act.wait_ge(mm_done, TT * j + t + 1)
                    for x, (at, _, n, (name, to), func) in enumerate(w.chunks[j][:w.used[j]]):
                        copy = nc.scalar.activation(w.buffers[name][:, t, to:to + n], c.ps[:, t, at:at + n], func)
                        copy.then_inc(copied if x == w.used[j] - 1 else part_copied, 1)
                    if "act" in beside:
                        beside["act"](act, TT * j + t)
                split(j + 2)
            act.wait_ge(copied, TT * n_chunks)
            if parts > 0:
                act.wait_ge(part_copied, parts)

        @block.vector
        def _(dve):
            if norm is not None:
                norm.apply(dve)
            if "dve" in beside:
                beside["dve"](dve)
    ctx.__exit__()


def ffn_weights(w_gate, w_up, w_down):
    gate, up, down = (w.rearrange("(k p) n -> p k n", p=P) for w in (w_gate, w_up, w_down))

    def pair(i, b):
        return [(ALL, (gate, up)[b % 2][:, :, bass.ds(i * (2 * P) + b // 2 * P, P)])]

    parts = [KD, KF // 3, KF // 3]

    def part(i, b):
        at = sum(parts[:b])
        return [(ALL, down[:, at:at + parts[b], bass.ds(i * P, P)])]
    return Weights(KF // 2, 4, pair), Weights(KD, len(parts), part, parts, parts=len(parts))


def ffn(c, gain, weights, ahead=None):
    w_gate_up, w_down = weights
    with c.stage() as ctx:
        a = c.halves(ctx, "a", [P, KF, T])
        with c.stage() as inner:
            c.h = c.halves(inner, "h", [P, KD, T])
            project_swiglu(c, w_gate_up, gain, a, ahead=w_down)
        project_add(c, w_down, c.xT, a, ahead=ahead)


def store_normed(c, gain, out):
    nc = c.nc
    with c.stage() as ctx:
        normed = ctx.sbuf("normed", [P, KD, T])
        with c.stage() as inner:
            norm = Norm(c, inner, gain, normed)
            with nc.Block() as block:
                block.sync(norm.load)
                block.scalar(lambda act: (norm.square(act), norm.root(act)))
                block.tensor(norm.sum)
                block.vector(norm.apply)
        rows = ctx.sbuf("rows", [P, TT, D])
        transposed, copied, stored = ctx.sem("transposed"), ctx.sem("copied"), ctx.sem("stored")
        out_rows = out[0].rearrange("(t p) d -> p t d", p=P)
        with nc.Block() as block:

            @block.tensor
            def _(pe):
                for t in range(TT):
                    for h in range(2):
                        for k in range(4):
                            tr = nc.tensor.transpose(c.ps[:, 2 * t + h, k * P:(k + 1) * P], normed[:, 4 * h + k, t * P:(t + 1) * P], c.ident[:, :])
                        tr.then_inc(transposed, 1)

            @block.scalar
            def _(act):
                for t in range(TT):
                    for h in range(2):
                        act.wait_ge(transposed, 2 * t + h + 1)
                        nc.scalar.activation(rows[:, t, h * T:(h + 1) * T], c.ps[:, 2 * t + h, :], ACT.Copy).then_inc(copied, 1)

            @block.sync
            def _(sp):
                for t in range(TT):
                    sp.wait_ge(copied, 2 * t + 2)
                    sp.dma_start(out_rows[:, t, :], rows[:, t, :]).then_inc(stored, 16)
                sp.wait_ge(stored, 16 * TT)


def attention(c, turns, units, scale, staging, sinks, lag=3):
    nc = c.nc
    steps = [(u, t) for u in range(len(units)) for t in range(TT)]
    n_steps, n_units, n_sinks = len(steps), len(units), len(sinks)
    s_banks, p_bufs = (0, 1, 2), 4
    pt_bank = 3
    act_tiles, dve_tiles = (1, 3), (0, 2)
    movers = len(act_tiles)
    slots = sorted(staging)
    last_user = {s: max(u for u in range(n_units) if s in units[u]["slots"]) for s in slots}
    width = [P * (t + 1) for t in range(TT)]
    with c.stage() as ctx:
        probs = ctx.sbuf("probs", [P, p_bufs, T])
        probsT = ctx.sbuf("probsT", [P, 2, TT, T])
        stat = ctx.sbuf("stat", [P, 3, p_bufs])
        top, total, inverse = stat[:, 0, :], stat[:, 1, :], stat[:, 2, :]
        scored, topped, exped, summed, normed = (ctx.sem(x) for x in ("scored", "topped", "exped", "inverted", "normed"))
        p_used, pt_act, pt_dve, pv_done, o_read = (ctx.sem(x) for x in ("p_used", "pt_act", "pt_dve", "pv_done", "o_read"))
        staged = {s: ctx.sem(f"staged{s}") for s in slots}
        scaled = ctx.sem("scaled")
        copies = {s: len(staging[s](0)) for s in slots}

        def loop(eng, body):
            if turns == 1:
                body(0)
                return
            with eng.Fori(0, turns) as i:
                body(i)

        def moved(eng, i, u, t):
            tiles, sem = (act_tiles, pt_act) if t in act_tiles else (dve_tiles, pt_dve)
            eng.wait_ge(sem, i * (n_units * movers) + (u * movers + tiles.index(t) + 1))

        with nc.Block() as block:

            @block.sync
            def _(sp):
                sp.sem_inc(pv_done, n_units)

                def body(i):
                    for s in sorted(slots, key=lambda s: last_user[s]):
                        hold(sp, pv_done, i * n_units + (last_user[s] + 1), c.sp_tick)
                        for dest, source in staging[s](i):
                            sp.dma_start(dest, source).then_inc(staged[s], 16)
                loop(sp, body)

            @block.tensor
            def _(pe):
                def score(i, s):
                    u, t = steps[s]
                    unit = units[u]
                    if t == 0:
                        for slot in unit["slots"]:
                            pe.wait_ge(staged[slot], i * (16 * copies[slot]) + 16 * copies[slot])
                    if s >= len(s_banks):
                        pe.wait_ge(exped, i * n_steps + (s - len(s_banks) + 1))
                    w, bank = width[t], s_banks[s % len(s_banks)]
                    out, q = c.ps[:, bank, 0:w], slice(t * P, (t + 1) * P)
                    nc.tensor.matmul(out, unit["q"][:, q], unit["k"](i)[:, 0:w], start=True, stop=False)
                    if "q2" in unit:
                        nc.tensor.matmul(out, unit["q2"][:, q], unit["k2"](i)[:, 0:w], start=False, stop=False)
                    if "bias" in unit:
                        nc.tensor.matmul(out, unit["ones"], unit["bias"](i)[:, 0:w], start=False, stop=False)
                    if unit["mask"] is not None:
                        mm = nc.tensor.matmul(out, c.mask_ident[:, :], unit["mask"](t), start=False, stop=True)
                    else:
                        mm = nc.tensor.matmul(c.ps[:, bank, w - P:w], c.mask_ident[:, :], c.mask_causal[:, :], start=False, stop=True)
                    mm.then_inc(scored, 1)

                def transposes(i, s):
                    u, t = steps[s]
                    pe.wait_ge(normed, i * n_steps + (s + 1))
                    moved(pe, i, u, t)
                    for j in range(t + 1):
                        tr = nc.tensor.transpose(c.ps[:, pt_bank + t, j * P:(j + 1) * P], probs[:, s % p_bufs, j * P:(j + 1) * P], c.ident[:, :])
                    tr.then_inc(p_used, 1)
                    if t == 1 and u >= 1:
                        weigh(i, u - 1)

                def weigh(i, u):
                    unit = units[u]
                    for t in (act_tiles[-1], dve_tiles[-1]):
                        moved(pe, i, u + 1, t)
                    if unit["first"]:
                        done = sum(1 for x in sinks if x < u)
                        pe.wait_ge(o_read, i * n_sinks + (done + n_sinks))
                    for j in range(TT):
                        mm = nc.tensor.matmul(unit["out"][:, j * P:T], unit["v"](j), probsT[:, u % 2, j, j * P:T],
                                              start=unit["first"] and j == 0, stop=unit["last"] and j == TT - 1 and "add" not in unit,
                                              skip_group_check=True)
                    if "add" in unit:
                        mm = nc.tensor.matmul(unit["out"], unit["add"], unit["add_to"](i), start=False, stop=unit["last"], skip_group_check=True)
                    mm.then_inc(pv_done, 1)

                pe.sem_inc(o_read, n_sinks)
                pe.sem_inc(pt_act, movers)
                pe.sem_inc(pt_dve, movers)

                def body(i):
                    for s in range(n_steps + lag):
                        if s < n_steps:
                            score(i, s)
                        if s >= lag:
                            transposes(i, s - lag)
                    weigh(i, n_units - 1)
                loop(pe, body)

            def move(eng, i, s, sem, copy):
                u, t = steps[s]
                eng.wait_ge(p_used, i * n_steps + (s + 1))
                if t in (act_tiles[0], dve_tiles[0]):
                    eng.wait_ge(pv_done, i * n_units + (n_units + u - 1))
                copy(probsT[:, u % 2, 0:t + 1, t * P:(t + 1) * P],
                     c.ps[:, pt_bank + t, 0:width[t]].rearrange("p (j q) -> p j q", q=P)).then_inc(sem, 1)

            @block.scalar
            def _(act):
                def read_out(i, u):
                    act.wait_ge(pv_done, i * n_units + (n_units + u + 1))
                    nc.scalar.activation(sinks[u](i), units[u]["sum"], ACT.Copy).then_inc(o_read, 1)

                def body(i):
                    for s in range(n_steps + lag):
                        if s < n_steps:
                            u, t = steps[s]
                            act.wait_ge(topped, i * n_steps + (s + 1))
                            if s >= p_bufs:
                                act.wait_ge(p_used, i * n_steps + (s - p_bufs + 1))
                            nc.scalar.activation(probs[:, s % p_bufs, 0:width[t]], c.ps[:, s_banks[s % len(s_banks)], 0:width[t]], ACT.Exp,
                                                 bias=top[:, s % p_bufs:s % p_bufs + 1], scale=scale,
                                                 accum_out=total[:, s % p_bufs:s % p_bufs + 1]).then_inc(exped, 1)
                        if s >= lag:
                            u, t = steps[s - lag]
                            if t in act_tiles:
                                move(act, i, s - lag, pt_act, lambda d, x: nc.scalar.activation(d, x, ACT.Copy))
                            if t == 2 and u >= 1 and u - 1 in sinks:
                                read_out(i, u - 1)
                    read_out(i, n_units - 1)
                loop(act, body)
                act.wait_ge(o_read, n_sinks * (turns + 1))

            @block.vector
            def _(dve):
                def body(i):
                    def normalise(s):
                        u, t = steps[s]
                        dve.wait_ge(exped, i * n_steps + (s + 1))
                        one = slice(s % p_bufs, s % p_bufs + 1)
                        nc.vector.reciprocal(inverse[:, one], total[:, one]).then_inc(summed, 1)
                        dve.wait_ge(summed, i * n_steps + (s + 1))
                        p = probs[:, s % p_bufs, 0:width[t]]
                        gate = units[u]["gate"](i, t) if units[u].get("gate") else None
                        if gate is None:
                            op = nc.vector.tensor_scalar(p, p, inverse[:, one], None, ALU.mult)
                        else:
                            op = nc.vector.tensor_scalar(p, p, inverse[:, one], gate, ALU.mult, ALU.mult)
                        op.then_inc(normed, 1)

                    for s in range(n_steps + lag):
                        if s < n_steps:
                            u, t = steps[s]
                            dve.wait_ge(scored, i * n_steps + (s + 1))
                            one = top[:, s % p_bufs:s % p_bufs + 1]
                            top_op = nc.vector.tensor_reduce(one, c.ps[:, s_banks[s % len(s_banks)], 0:width[t]], AX.X, ALU.max, negate=True)
                            if scale == 1.0:
                                top_op.then_inc(topped, 1)
                            else:
                                top_op.then_inc(scaled, 1)
                                dve.wait_ge(scaled, i * n_steps + (s + 1))
                                nc.vector.tensor_scalar(one, one, scale, None, ALU.mult).then_inc(topped, 1)
                        if 1 <= s <= n_steps:
                            normalise(s - 1)
                        if s >= lag and steps[s - lag][1] in dve_tiles:
                            move(dve, i, s - lag, pt_dve, nc.vector.tensor_copy)
                loop(dve, body)


def head_norm_beside_rows(c, w, buf, gains, ahead):
    nc = c.nc
    tiles, ring = buf.shape[1], 4
    with c.stage() as ctx:
        squares = ctx.sbuf("squares", [P, ring, T])
        rstd = ctx.sbuf("rstd", [P, ring, T])
        squared, summed, inverted, rooted, normed = (ctx.sem(n) for n in ("squared", "summed", "inverted", "rooted", "normed"))
        units = TT * len(w.chunks)
        per = -(-tiles // units)
        of = lambda n: range(n * per, min((n + 1) * per, tiles)) if n >= 0 else ()

        def square(act, n):
            if n >= ring:
                act.wait_ge(summed, n - ring + 1)
            nc.scalar.activation(squares[:, n % ring, :], buf[:, n, :], ACT.Square).then_inc(squared, 1)

        def pe_part(pe, unit):
            for n in of(unit):
                pe.wait_ge(squared, n + 1)
                if n >= ring:
                    pe.wait_ge(rooted, n - ring + 1)
                nc.tensor.matmul(c.ps[:, 4 + n % 4, :], c.ones[:, :], squares[:, n % ring, :], start=True, stop=True).then_inc(summed, 1)

        def act_first(act):
            for n in range(ring):
                square(act, n)

        def act_part(act, unit):
            for n in of(unit):
                act.wait_ge(summed, n + 1)
                if n >= ring:
                    act.wait_ge(normed, n - ring + 1)
                nc.scalar.activation(rstd[:, n % ring, :], c.ps[:, 4 + n % 4, :], ACT.Sqrt, bias=c.eps[:, 0:1], scale=1.0 / P).then_inc(rooted, 1)
                if n + ring < tiles:
                    square(act, n + ring)

        def dve_part(dve):
            def apply(n):
                dve.wait_ge(inverted, n + 1)
                nc.vector.scalar_tensor_tensor(buf[:, n, :], buf[:, n, :], gains[:, n:n + 1], rstd[:, n % ring, :], ALU.mult, ALU.mult).then_inc(normed, 1)

            for n in range(tiles):
                dve.wait_ge(rooted, n + 1)
                nc.vector.reciprocal(rstd[:, n % ring, :], rstd[:, n % ring, :]).then_inc(inverted, 1)
                if n >= 1:
                    apply(n - 1)
            apply(tiles - 1)
            dve.wait_ge(normed, tiles)
        project_rows(c, w, {"pe": pe_part, "act_first": act_first, "act": act_part, "dve": dve_part}, ahead)


def fox_attention(c, w_rows, f_bias, q_gain, k_gain, qkT, ahead):
    nc = c.nc
    with c.stage() as ctx:
        v = ctx.sbuf("v", [P, TT, FOX_H * P])
        f = ctx.sbuf("f", [P, TT, FOX_H])
        gains = ctx.sbuf("gains", [P, 2 * FOX_H])
        pair = ctx.sbuf("pair", [P, 2])
        bias = ctx.sbuf("bias", [P, FOX_H])
        minus_tri = ctx.sbuf("minus_tri", [P, T])
        cum = ctx.sbuf("cum", [FOX_H, T])
        cum_rows = ctx.sbuf("cum_rows", [1, FOX_H, T])
        g_in, g_set = ctx.sem("gains_in"), ctx.sem("gains_set")
        with nc.Block() as block:

            @block.sync
            def _(sp):
                sp.dma_start(pair[:, 0:1], q_gain.rearrange("(p a) -> p a", a=1)).then_inc(g_in, 16)
                sp.dma_start(pair[:, 1:2], k_gain.rearrange("(p a) -> p a", a=1)).then_inc(g_in, 16)
                sp.dma_start(bias[:, :], f_bias.partition_broadcast(P)).then_inc(g_in, 16)
                sp.dma_start(minus_tri[:, :], c.ins["c_minus_tri"]).then_inc(g_in, 16)
                sp.dma_start(c.xT[:, :, :], c.x_dram).then_inc(c.x_back, 16)
                sp.wait_ge(g_in, 64)

            @block.vector
            def _(dve):
                dve.wait_ge(g_in, 64)
                nc.vector.tensor_scalar(gains[:, 0:FOX_H], pair[:, 0:1].to_broadcast([P, FOX_H]), float(P) ** -0.5, None, ALU.mult).then_inc(g_set, 1)
                nc.vector.tensor_copy(gains[:, FOX_H:], pair[:, 1:2].to_broadcast([P, FOX_H])).then_inc(g_set, 1)
                dve.wait_ge(g_set, 2)
        w_rows.buffers = dict(v=v, f=f)
        head_norm_beside_rows(c, w_rows, qkT, gains, ahead)
        forget_sums(c, f, bias, minus_tri, cum, cum_rows)

        def head(s):
            return dict(q=qkT[:, s, :], k=lambda i: qkT[:, s + FOX_H, :], v=lambda j: v[:, j, s * P:(s + 1) * P], mask=None, slots=[],
                        ones=c.ones[0:1, :], bias=lambda i: cum_rows[:, s, :], out=c.ps[:, 7, :], sum=c.ps[:, 7, :], first=True, last=True)
        attention(c, 1, [head(s) for s in range(FOX_H)], 1.0, {}, {s: (lambda i, s=s: qkT[:, s, :]) for s in range(FOX_H)})


def forget_sums(c, f, bias, minus_tri, cum, cum_rows):
    nc = c.nc
    with c.stage() as ctx:
        z, e, low = (ctx.sbuf(n, [P, TT, FOX_H]) for n in ("z", "e", "low"))
        zed, exped, logged, ready, summed, copied, moved = (ctx.sem(n) for n in ("zed", "exped", "logged", "ready", "summed", "copied", "moved"))
        with nc.Block() as block:

            @block.vector
            def _(dve):
                step = Chain(dve, c.dve_step)
                step(nc.vector.tensor_tensor(z[:, :, :], f[:, :, :], bias[:, :].unsqueeze(1).to_broadcast([P, TT, FOX_H]), ALU.add))
                nc.vector.tensor_scalar(low[:, :, :], z[:, :, :], 0.0, None, ALU.min).then_inc(zed, 1)
                dve.wait_ge(logged, 1)
                nc.vector.tensor_tensor(z[:, :, :], low[:, :, :], e[:, :, :], ALU.subtract).then_inc(ready, 1)
                dve.wait_ge(ready, 1)

            @block.scalar
            def _(act):
                act.wait_ge(zed, 1)
                nc.scalar.activation(e[:, :, :], z[:, :, :], ACT.Abs).then_inc(exped, 1)
                act.wait_ge(exped, 1)
                nc.scalar.activation(e[:, :, :], e[:, :, :], ACT.Exp, scale=-1.0).then_inc(exped, 1)
                act.wait_ge(exped, 2)
                nc.scalar.activation(e[:, :, :], e[:, :, :], ACT.Ln, bias=1.0).then_inc(logged, 1)
                act.wait_ge(summed, 1)
                nc.scalar.activation(cum[:, :], c.ps[0:FOX_H, 0, :], ACT.Copy).then_inc(copied, 1)

            @block.tensor
            def _(pe):
                pe.wait_ge(ready, 1)
                for t in range(TT):
                    mm = nc.tensor.matmul(c.ps[0:FOX_H, 0, t * P:T], z[:, t, :], minus_tri[:, 0:T - t * P],
                                          start=(t == 0), stop=(t == TT - 1), skip_group_check=True)
                mm.then_inc(summed, 1)

            @block.sync
            def _(sp):
                sp.wait_ge(copied, 1)
                sp.dma_start(cum_rows[0:1, :, :], cum[:, :]).then_inc(moved, 16)
                sp.wait_ge(moved, 16)


def ssm(c, A, w_u, w_qk, ahead, qkT, ygT):
    nc = c.nc
    with c.stage() as ctx:
        uT = ygT
        PM = [P, PAIRS]
        bT = [ctx.sbuf(n, [P, PAIRS, P]) for n in ("bT_re", "bT_im")]
        powers = ctx.sbuf("powers", [P, 9, 3, PAIRS])
        skip = ctx.sbuf("skip", [P, SSM_T])
        cT = [c.xT[:, 4 * x:4 * x + 4, :].rearrange("p k (j n) -> p (k j) n", n=P) for x in range(2)]
        with c.stage() as inner:
            before, after = ssm_parameters(c, A, inner, PM, bT, cT, powers, skip, qkT)
            project_copy(c, w_u, uT, w_qk, before, after, Norm(c, inner, A["mix_norm_g"][0], c.h))
        S = [ctx.sbuf(n, [P, PAIRS, T]) for n in ("s_re", "s_im")]
        scan(c, uT, bT, cT, powers, skip, S, ygT, w_qk, ahead, qkT)


def ssm_parameters(c, A, ctx, PM, bT, cT, powers, skip, room):
    nc = c.nc
    names = ("ar", "ai", "dt", "mag", "th", "turn", "cos", "sin", "lre", "lim", "nr", "den", "cre", "cim", "t0", "t1", "half_pi")
    m = {n: ctx.sbuf(n, PM) for n in names}
    b_in, tmp = ([ctx.sbuf(f"{n}{x}", [P, PAIRS, SSM_H]) for x in range(2)] for n in ("b_in", "tmp"))
    b_wide, c_wide = ([room[:, 4 * x:4 * x + 4, :].rearrange("p k (j n) -> p (k j) n", n=P) for x in pair] for pair in ((0, 1), (2, 3)))
    param_in, zeroed, c_in = ctx.sem("param_in"), ctx.sem("zeroed"), ctx.sem("c_in")
    mag_set, angle, trig, b_made, tiles_out, turned, moved = (ctx.sem(n) for n in ("mag_set", "angle", "trig", "b_made", "tiles_out", "turned", "moved"))
    by_state = lambda a: a.rearrange("(j two) s -> (two s) j", two=2)
    dt2 = A["ssm_log_step"][0].rearrange("(j two) -> two j", two=2)

    def load(sp):
        sp.dma_start(m["ar"][:, :], by_state(A["ssm_a_re"][0]), allow_slow_non_contiguous=True).then_inc(param_in, 16)
        sp.dma_start(m["ai"][:, :], by_state(A["ssm_a_im"][0]), allow_slow_non_contiguous=True).then_inc(param_in, 16)
        for two in range(2):
            sp.dma_start(m["dt"][two * SSM_S:(two + 1) * SSM_S, :], dt2[two].partition_broadcast(SSM_S), allow_slow_non_contiguous=True).then_inc(param_in, 16)
        sp.dma_start(skip[:, :], A["ssm_d"][0].rearrange("(t p) -> p t", p=P), allow_slow_non_contiguous=True).then_inc(param_in, 16)
        for x, name in enumerate(("ssm_b_re", "ssm_b_im")):
            sp.dma_start(b_in[x][:, :, :], A[name][0].rearrange("(j two) s h -> (two s) j h", two=2)).then_inc(param_in, 16)
        sp.dma_start(c.x_dram, c.xT[:, :, :]).then_inc(c.x_saved, 16)
        sp.wait_ge(zeroed, 5)
        for x, name in enumerate(("ssm_c_re", "ssm_c_im")):
            view = A[name][0].rearrange("(t g) h s -> g h t s", g=8)
            for g in range(8):
                at = g % 2 * SSM_S
                sp.dma_start(c_wide[x][g * SSM_H:(g + 1) * SSM_H, g // 2::4, at:at + SSM_S], view[g]).then_inc(c_in, 16)

    def trigonometry(act):
        act.wait_ge(param_in, 16 * 7)
        nc.scalar.activation(m["dt"][:, :], m["dt"][:, :], ACT.Exp).then_inc(mag_set, 1)
        act.wait_ge(angle, 1)
        nc.scalar.activation(m["mag"][:, :], m["mag"][:, :], ACT.Exp).then_inc(trig, 1)
        act.wait_ge(angle, 2)
        act.wait_ge(zeroed, 5)
        nc.scalar.activation(m["sin"][:, :], m["th"][:, :], ACT.Sin).then_inc(trig, 1)
        nc.scalar.activation(m["turn"][:, :], m["th"][:, :], ACT.Abs).then_inc(trig, 1)
        act.wait_ge(trig, 3)
        nc.scalar.activation(m["cos"][:, :], m["turn"][:, :], ACT.Sin, bias=m["half_pi"][:, 0:1], scale=-1.0).then_inc(trig, 1)

    def blocks(dve):
        v = nc.vector
        step = Chain(dve, c.dve_step)
        tt = lambda o, a, b, op: step(v.tensor_tensor(m[o][:, :], m[a][:, :], m[b][:, :], op))
        for buf in (*b_wide, *c_wide):
            v.memset(buf, 0.0).then_inc(zeroed, 1)
        v.memset(m["half_pi"][:, :], math.pi / 2).then_inc(zeroed, 1)
        dve.wait_ge(zeroed, 5)
        dve.wait_ge(param_in, 16 * 7)
        dve.wait_ge(mag_set, 1)
        step(v.tensor_tensor(m["th"][:, :], m["ai"][:, :], m["dt"][:, :], ALU.mult))
        v.tensor_tensor(m["mag"][:, :], m["ar"][:, :], m["dt"][:, :], ALU.mult).then_inc(angle, 1)
        step(v.tensor_scalar(m["turn"][:, :], m["th"][:, :], 1.0 / (2 * math.pi), 12582912.0, ALU.mult, ALU.add))
        step(v.tensor_scalar(m["turn"][:, :], m["turn"][:, :], 12582912.0, None, ALU.subtract))
        for part in (6.28125, 0.0019350051879882812, 3.019915981956753e-07):
            step(v.scalar_tensor_tensor(m["th"][:, :], m["turn"][:, :], -part, m["th"][:, :], ALU.mult, ALU.add))
        v.tensor_scalar(m["th"][:, :], m["th"][:, :], 3.1415925, -3.1415925, ALU.min, ALU.max).then_inc(angle, 1)
        dve.wait_ge(trig, 4)
        tt("lre", "mag", "cos", ALU.mult)
        tt("lim", "mag", "sin", ALU.mult)
        step(v.tensor_scalar(m["nr"][:, :], m["lre"][:, :], 1.0, None, ALU.subtract))
        tt("den", "ar", "ar", ALU.mult)
        tt("t0", "ai", "ai", ALU.mult)
        tt("den", "den", "t0", ALU.add)
        step(v.reciprocal(m["den"][:, :], m["den"][:, :]))
        tt("t0", "nr", "ar", ALU.mult)
        tt("t1", "lim", "ai", ALU.mult)
        tt("t0", "t0", "t1", ALU.add)
        tt("cre", "t0", "den", ALU.mult)
        tt("t0", "lim", "ar", ALU.mult)
        tt("t1", "nr", "ai", ALU.mult)
        tt("t0", "t0", "t1", ALU.subtract)
        tt("cim", "t0", "den", ALU.mult)
        spread = lambda n: m[n][:, :].unsqueeze(2).to_broadcast([P, PAIRS, SSM_H])
        for x, (first, second, op) in enumerate(((("cre", 0), ("cim", 1), ALU.subtract), (("cre", 1), ("cim", 0), ALU.add))):
            step(v.tensor_tensor(tmp[0][:, :, :], spread(first[0]), b_in[first[1]][:, :, :], ALU.mult))
            step(v.tensor_tensor(tmp[1][:, :, :], spread(second[0]), b_in[second[1]][:, :, :], ALU.mult))
            for two in range(2):
                rows = slice(two * SSM_S, (two + 1) * SSM_S)
                for q in range(4):
                    at = (2 * q + two) * SSM_H
                    step(v.tensor_tensor(b_wide[x][rows, q::4, at:at + SSM_H], tmp[0][rows, q::4, :], tmp[1][rows, q::4, :], op))
            dve.sem_inc(b_made, 1)
        for lv in range(9):
            re, im, neg = (powers[:, lv, z, :] for z in range(3))
            if lv == 0:
                step(v.tensor_copy(re, m["lre"][:, :]))
                step(v.tensor_copy(im, m["lim"][:, :]))
            else:
                r0, i0, n0 = (powers[:, lv - 1, z, :] for z in range(3))
                step(v.tensor_tensor(m["t0"][:, :], i0, i0, ALU.mult))
                step(v.tensor_tensor(m["t1"][:, :], r0, r0, ALU.mult))
                step(v.tensor_tensor(re, m["t1"][:, :], m["t0"][:, :], ALU.subtract))
                step(v.tensor_tensor(m["t0"][:, :], r0, i0, ALU.mult))
                step(v.tensor_scalar(im, m["t0"][:, :], 2.0, None, ALU.mult))
            step(v.tensor_scalar(neg, im, -1.0, None, ALU.mult))

    def turn(pe):
        pe.wait_ge(tiles_out, 1)
        for n in range(16):
            x, q = n // 4, n % 4
            if n < 8:
                pe.wait_ge(b_made, x + 1)
            else:
                pe.wait_ge(c_in, 16 * 16)
                pe.wait_ge(moved, n - 7)
            for y in range(4):
                tr = nc.tensor.transpose(c.ps[:, n % 8, y * P:(y + 1) * P], (*b_wide, *c_wide)[x][:, 4 * q + y, :], c.ident[:, :])
            tr.then_inc(turned, 1)

    def move(act):
        act.sem_inc(tiles_out, 1)
        act.wait_ge(c.x_saved, 16)
        for n in range(16):
            x, q = n // 4, n % 4
            act.wait_ge(turned, n + 1)
            nc.scalar.activation((*bT, *cT)[x][:, 4 * q:4 * q + 4, :], c.ps[:, n % 8, :], ACT.Copy, scale=-1.0 if x == 3 else 1.0).then_inc(moved, 1)
        act.wait_ge(moved, 16)
    return {"sp": load, "act": trigonometry, "dve": blocks}, {"pe": turn, "act": move}


def scan(c, uT, bT, cT, powers, skip, S, ygT, w_qk, ahead, qkT):
    nc = c.nc
    LEVELS = 9
    TOGETHER = 2
    BIG = 3
    with c.stage() as ctx:
        n_small = T >> (BIG + 1)
        small = [bT[x // 2][:, :, 0:n_small] if x % 2 else c.ps[:, 4 + x, :].rearrange("p (j n) -> p j n", j=PAIRS) for x in range(4)]
        filled, moved, swept, ready, y_done, y_sum, y_out = (
            ctx.sem(n) for n in ("filled", "moved", "swept", "ready", "y_done", "y_sum", "y_out"))
        def fill(pe):
            for j in range(PAIRS):
                for x in range(2):
                    n = 2 * j + x
                    if n >= 4:
                        pe.wait_ge(moved, n - 3)
                    nc.tensor.matmul(c.ps[:, 4 + n % 4, :], bT[x][:, j, :], uT[:, j // 4, :], start=True, stop=True).then_inc(filled, 1)

        def outputs(pe):
            for t in range(SSM_T):
                for q in range(4):
                    j = 4 * t + q
                    pe.wait_ge(ready, j + 1)
                    for x in range(2):
                        mm = nc.tensor.matmul(c.ps[:, 4 + t, :], cT[x][:, j, :], S[x][:, j, :], start=(q == 0 and x == 0), stop=(q == 3 and x == 1))
                mm.then_inc(y_done, 1)

        def move(act):
            for j in range(PAIRS):
                for x in range(2):
                    act.wait_ge(filled, 2 * j + x + 1)
                    nc.scalar.activation(S[x][:, j, :], c.ps[:, 4 + (2 * j + x) % 4, :], ACT.Copy).then_inc(moved, 1)

        def gelus(act):
            for t in range(SSM_T):
                act.wait_ge(y_sum, t + 1)
                nc.scalar.activation(ygT[:, t, :], ygT[:, t, :], ACT.Gelu_apprx_tanh).then_inc(y_out, 1)
            act.wait_ge(y_out, SSM_T)

        def sweeps(dve):
            v = nc.vector
            done = [0]

            def after(ins, n=1):
                done[0] += 1
                ins.then_inc(swept, 1)

            def views(level, down):
                d = 1 << level
                if down:
                    return slice(3 * d - 1, T, 2 * d), slice(2 * d - 1, T - d, 2 * d)
                return slice(2 * d - 1, T, 2 * d), slice(d - 1, T, 2 * d)

            def pair_steps(first, level, down):
                to, of = views(level, down)
                pairs = range(first, first + TOGETHER)
                since = 2 * TOGETHER - 2
                for j in pairs:
                    re = powers[:, level, 0, j:j + 1]
                    if done[0] > since:
                        dve.wait_ge(swept, done[0] - since)
                    for s in S:
                        after(v.scalar_tensor_tensor(s[:, j, to], s[:, j, of], re, s[:, j, to], ALU.mult, ALU.add))
                for j in pairs:
                    im, neg = powers[:, level, 1, j:j + 1], powers[:, level, 2, j:j + 1]
                    Sr, Si = S[0][:, j, :], S[1][:, j, :]
                    dve.wait_ge(swept, done[0] - since)
                    after(v.scalar_tensor_tensor(Sr[:, to], Si[:, of], neg, Sr[:, to], ALU.mult, ALU.add))
                    after(v.scalar_tensor_tensor(Si[:, to], Sr[:, of], im, Si[:, to], ALU.mult, ALU.add))

            def all_step(level, down):
                to, of = views(level, down)
                n = len(range(*to.indices(T)))
                a = [s[:, :, 0:n] for s in small]
                lam = [powers[:, level, z, :].unsqueeze(2).to_broadcast([P, PAIRS, n]) for z in range(3)]
                Sr, Si = S[0], S[1]
                after(v.tensor_tensor(a[0], Sr[:, :, of], lam[0], ALU.mult))
                after(v.tensor_tensor(a[1], Si[:, :, of], lam[2], ALU.mult))
                after(v.tensor_tensor(a[2], Si[:, :, of], lam[0], ALU.mult))
                after(v.tensor_tensor(a[3], Sr[:, :, of], lam[1], ALU.mult))
                dve.wait_ge(swept, done[0])
                after(v.tensor_tensor(a[0], a[0], a[1], ALU.add))
                after(v.tensor_tensor(a[2], a[2], a[3], ALU.add))
                dve.wait_ge(swept, done[0])
                after(v.tensor_tensor(Sr[:, :, to], Sr[:, :, to], a[0], ALU.add))
                after(v.tensor_tensor(Si[:, :, to], Si[:, :, to], a[2], ALU.add))
                dve.wait_ge(swept, done[0])

            for first in range(0, PAIRS, TOGETHER):
                dve.wait_ge(moved, 2 * (first + TOGETHER))
                for level in range(BIG):
                    pair_steps(first, level, False)
            dve.wait_ge(swept, done[0])
            for level in range(BIG, LEVELS):
                all_step(level, False)
            for level in range(LEVELS - 2, BIG - 1, -1):
                all_step(level, True)
            for first in range(0, PAIRS, TOGETHER):
                for level in range(BIG - 1, -1, -1):
                    pair_steps(first, level, True)
                dve.wait_ge(swept, done[0])
                dve.sem_inc(ready, TOGETHER)
            for t in range(SSM_T):
                dve.wait_ge(y_done, t + 1)
                v.scalar_tensor_tensor(ygT[:, t, :], uT[:, t, :], skip[:, t:t + 1], c.ps[:, 4 + t, :], ALU.mult, ALU.add).then_inc(y_sum, 1)
            dve.wait_ge(y_sum, SSM_T)

        project_copy(c, w_qk, qkT, ahead, before={"pe": fill, "act": move}, after={"pe": outputs, "act": gelus, "dve": sweeps})


def merge(c, A, ygT, attT, weights, ahead):
    nc = c.nc
    w_merge, w_out = weights
    with c.stage() as ctx:
        mixed = ctx.sbuf("mixed", [P, KD, T])
        sig = ctx.sbuf("sig", [P, 3, T])
        part = ctx.sbuf("part", [P, 2, T])
        yg = c.halves(ctx, "yg", [P, SSM_T, T])
        mixed_done, parted, yg_split, yg_low = (ctx.sem(n) for n in ("mixed_done", "parted", "yg_split", "yg_low"))

        def yg_high_half(act):
            for k in range(SSM_T):
                high_half(nc, yg.high[:, k, :], ygT[:, k, :]).then_inc(yg_split, 1)

        def start(pe):
            pe.sem_inc(mixed_done, 1)
            pe.wait_ge(yg_low, SSM_T)

        def act(eng, i, wait_tile, bank_free, split):
            for b in range(3):
                wait_tile(b)
                if b == 0:
                    eng.wait_ge(mixed_done, i + 1)
                nc.scalar.activation(sig[:, b, :], c.ps[:, b, :], ACT.Sigmoid).then_inc(bank_free, 1)
                split(b)
            split(3)

        def dve(eng, i, wait_tile, bank_free):
            eng.wait_ge(bank_free, i * 4 + (4 + 2))
            nc.vector.tensor_tensor(part[:, 0, :], sig[:, 1, :], tile_of(attT, i, 1, 0), ALU.mult).then_inc(parted, 1)
            eng.wait_ge(bank_free, i * 4 + (4 + 3))
            wait_tile(3)
            nc.vector.tensor_tensor(part[:, 1, :], sig[:, 2, :], c.ps[:, 3, :], ALU.mult).then_inc(bank_free, 1)
            eng.wait_ge(bank_free, i * 4 + (4 + 4))
            nc.vector.tensor_tensor(part[:, 1, :], part[:, 1, :], sig[:, 0, :], ALU.mult).then_inc(parted, 1)
            eng.wait_ge(parted, i * 2 + 2)
            nc.vector.tensor_tensor(tile_of(mixed, i, 1, 0), part[:, 0, :], part[:, 1, :], ALU.add).then_inc(mixed_done, 1)

        def yg_low_half(dve):
            for k in range(SSM_T):
                dve.wait_ge(yg_split, k + 1)
                low_half(nc.vector, yg.low[:, k, :], ygT[:, k, :], yg.high[:, k, :]).then_inc(yg_low, 1)
        project(c, w_merge, {"act": act, "dve": dve}, [c.h, c.h, yg, yg], w_out, before={"pe": start, "act": yg_high_half, "dve": yg_low_half},
                after={"dve": lambda eng: eng.wait_ge(mixed_done, KD + 1)})
        project_add(c, w_out, c.xT, c.h, mixed, ahead, {"dve": lambda dve: dve.wait_ge(c.x_back, 16)})


def merge_weights(w_in, w_glu):
    col_g = SSM_W + 3 * FOX_H * P + FOX_H
    wide, glu = w_in.rearrange("(k p) n -> p k n", p=P), w_glu.rearrange("(k p) n -> p k n", p=P)
    kinds = ((wide, col_g), (wide, col_g + D), (glu, D), (glu, 0))

    def source(i, b):
        view, col = kinds[b]
        return [(ALL, view[:, :, bass.ds(i * P + col, P)])]
    return Weights(KD, 4, source, [KD, KD, SSM_T, SSM_T])


def first_mix(c, A, ahead):
    w_in = A["w_in"][0]
    w_u, w_qk = columns(w_in, 1, SSM_T), columns(w_in, FOX_H, 2, SSM_W)
    at = SSM_W + 2 * FOX_H * P
    w_rows = RowWeights(w_in, [(at, FOX_H * P, "v", ACT.Copy), (at + FOX_H * P, FOX_H, "f", ACT.Copy)])
    w_merge, w_out = merge_weights(w_in, A["ssm_w_glu"][0]), columns(A["w_out"][0], 2, 4)
    with c.stage() as ctx:
        c.h = c.halves(ctx, "h", [P, KD, T])
        ygT = ctx.sbuf("ygT", [P, SSM_T, T])
        qkT = ctx.sbuf("qkT", [P, 2 * FOX_H, T])
        ssm(c, A, w_u, w_qk, w_rows, qkT, ygT)
        fox_attention(c, w_rows, A["fox_forget_bias"][0], A["q_norm_g"][0], A["k_norm_g"][0], qkT, w_merge)
        merge(c, A, ygT, qkT, (w_merge, w_out), ahead)


DENSE = TT - 1
TD = DENSE * P
CHUNKS = PEER_K
TB = 32
BLOCKS = TD // TB
QUAD = 4
RING = 4


def peer(c, A, w_query):
    with c.stage() as ctx:
        route = Route(c, ctx)
        h_row = ctx.sbuf("h_row", [P, D])
        ring = ctx.sbuf("ring", [P, RING, 2 * D])
        c.h = c.halves(ctx, "h", [P, KD, T])
        peer_scores(c, w_query, A["ffn_norm_g"][0], A["peer_sub_keys"][0], route, ring[:, 0:2, :].rearrange("p s (k t) -> p (s k) t", t=T))
        peer_gates(c, route, ring, h_row)
        peer_experts(c, A["peer_uT"], A["peer_uv"], route, h_row, ring)
        add_rows(c, ring)


def add_rows(c, rows):
    nc = c.nc
    with c.stage() as ctx:
        turned, added = ctx.sem("turned"), ctx.sem("added")
        with nc.Block() as block:

            @block.tensor
            def _(pe):
                for k in range(KD):
                    for t in range(TT):
                        tr = nc.tensor.transpose(c.ps[:, k, t * P:(t + 1) * P], rows[:, t, k * P:(k + 1) * P], c.ident[:, :])
                    tr.then_inc(turned, 1)

            @block.vector
            def _(dve):
                for k in range(KD):
                    dve.wait_ge(turned, k + 1)
                    nc.vector.tensor_tensor(c.xT[:, k, :], c.xT[:, k, :], c.ps[:, k, :], ALU.add).then_inc(added, 1)
                dve.wait_ge(added, KD)


HC = 2 * PEER_H


def peer_scores(c, w_query, gain, sub_keys, route, room):
    nc = c.nc
    per_turn = w_query.per_turn
    with c.stage() as ctx:
        query = ctx.sbuf("query", [P, per_turn, T])
        scores = ctx.sbuf("scores", [P, per_turn, TT, PEER_K])
        keys = ctx.sbuf("keys", [P, HC, P])
        keysT = ctx.sbuf("keysT", [P, HC, P])
        keys_in, turned, moved, copied, scored, scores_out, searched = (
            ctx.sem(n) for n in ("keys_in", "turned", "moved", "copied", "scored", "scores_out", "searched"))
        top = ctx.sbuf("turn_top", [P, TT, per_turn, TOPK])
        top_at = ctx.sbuf("turn_top_at", [P, TT, per_turn, TOPK], U32)
        quarters = HC // 4

        def load_keys(sp):
            sp.dma_start(keys[:, :, :], sub_keys.rearrange("h c k d -> k (h c) d")).then_inc(keys_in, 16)

        def turn_keys(pe):
            pe.wait_ge(keys_in, 16)
            for n in range(quarters):
                for y in range(4):
                    tr = nc.tensor.transpose(c.ps[:, 4 + n, y * P:(y + 1) * P], keys[:, 4 * n + y, :], c.ident[:, :])
                tr.then_inc(turned, 1)

        def move_keys(act):
            for n in range(quarters):
                act.wait_ge(turned, n + 1)
                nc.scalar.activation(keysT[:, 4 * n:4 * n + 4, :], c.ps[:, 4 + n, :], ACT.Copy).then_inc(moved, 1)
            act.wait_ge(moved, quarters)
            act.sem_inc(scored, per_turn)
            act.sem_inc(searched, per_turn)

        def score(pe, i, b, bank_free):
            pe.wait_ge(copied, i * per_turn + (b + 1))
            pe.sem_inc(bank_free, 1)
            for t in range(TT):
                mm = nc.tensor.matmul(c.ps[:, 4 + b, t * P:(t + 1) * P], query[:, b, t * P:(t + 1) * P], tile_of(keysT, i, per_turn, b), start=True, stop=True)
            mm.then_inc(scored, 1)

        def copy(act, i, wait_tile, bank_free, split):
            def copy_scores(b):
                act.wait_ge(scored, i * per_turn + (b + 1 + per_turn))
                act.wait_ge(searched, i * per_turn + (b + 1))
                nc.scalar.activation(scores[:, b, :, :], c.ps[:, 4 + b, :], ACT.Copy).then_inc(scores_out, 1)

            for b in range(per_turn):
                wait_tile(b)
                act.wait_ge(scored, i * per_turn + (b + 1))
                nc.scalar.activation(query[:, b, :], c.ps[:, b, :], ACT.Copy).then_inc(copied, 1)
                split(b)
                if b >= 1:
                    copy_scores(b - 1)
            copy_scores(per_turn - 1)

        def search(dve, i, wait_tile, bank_free):
            step = Chain(dve, c.dve_step, i, per_turn * 5 * TT + 2, c.dve_tick)
            for b in range(per_turn):
                hold(dve, scores_out, i * per_turn + (b + 1), c.dve_tick)
                route.top16(step, TT, top[:, :, b, :], top_at[:, :, b, :], scores[:, b, :, :])
                dve.sem_inc(searched, 1)
            for all_turns, turn in ((route.top, top), (route.top_at, top_at)):
                step.mark(nc.vector.tensor_copy(all_turns[:, :, bass.ds(i * per_turn, per_turn), :], turn[:, :, :, :]))
            step.wait()
            if not isinstance(i, int):
                ends.append(step)

        ends = []
        project(c, w_query, {"act": copy, "pe": score, "dve": search}, before={"sp": load_keys, "pe": turn_keys, "act": move_keys}, norm=Norm(c, ctx, gain, c.h, squares=room))
        ends[0].ends(w_query.turns)


class Route:

    def __init__(self, c, ctx):
        self.c = c
        self.gates_all = c.nc.dram_tensor("peer_gates", (BLOCKS, P, PEER_K * TB), F32).ap()
        self.top = ctx.sbuf("top", [P, TT, HC, TOPK])
        self.top_at = ctx.sbuf("top_at", [P, TT, HC, TOPK], U32)
        self.idx = ctx.sbuf("idx", [P, SLOTS], U32)
        self.gates = ctx.sbuf("gates", [P, SLOTS])
        flat = ctx.sbuf("work", [P, SLOTS * TOPK])
        self.sums = flat[:, :].rearrange("p (h s) -> p h s", h=PEER_H)
        self.hit = flat[:, :].rearrange("p (s k) -> p s k", k=TOPK)
        self.top_atf = ctx.sbuf("top_atf", [P, PEER_H, 2, TOPK])
        self.best = ctx.sbuf("best", [P, PEER_H, TOPK])
        self.best_at = ctx.sbuf("best_at", [P, PEER_H, TOPK], U32)
        self.half_at = ctx.sbuf("half_at", [P, 2, SLOTS], U32)
        self.half_f = ctx.sbuf("half_f", [P, 2, SLOTS])
        self.key_no = ctx.sbuf("key_no", [P, 2, SLOTS])
        self.iota = ctx.sbuf("iota", [P, TOPK])
        self.total = ctx.sbuf("total", [P, PEER_H])
        self.less, self.exped, self.routed = (ctx.sem(n) for n in ("less", "exped", "routed"))

    STEPS = 1 + 5 * PEER_H + 1 + 3 + 1 + 2 * 3 + 1 + 3

    def top16(self, step, n, values, at, source):
        v = self.c.nc.vector
        for half in (slice(0, 8), slice(8, 16)):
            for r in range(n):
                step.mark(v.max(values[:, r, half], source[:, r, :]))
            step.wait()
            for r in range(n):
                step.mark(v.max_index(at[:, r, half], values[:, r, half], source[:, r, :]))
            step.wait()
            if half.start == 0:
                for r in range(n):
                    step.mark(v.match_replace(source[:, r, :], values[:, r, half], source[:, r, :], LOWEST))
                step.wait()

    def of_tile(self, buf, t):
        return buf[:, bass.ds(t, 1), :, :].rearrange("p t (h c) k -> p (t h) c k", c=2)

    def pairs(self, step, t):
        v = self.c.nc.vector
        pair = self.of_tile(self.top, t)
        sums = self.sums.rearrange("p h (i j) -> p h i j", j=TOPK)
        wide = [P, PEER_H, TOPK, TOPK]
        step(v.tensor_tensor(sums, pair[:, :, 0, :].unsqueeze(3).to_broadcast(wide), pair[:, :, 1, :].unsqueeze(2).to_broadcast(wide), ALU.add))
        self.top16(step, PEER_H, self.best, self.best_at, self.sums)
        step(v.tensor_copy(self.total[:, :], self.best[:, :, 0]))
        v.tensor_tensor(self.best[:, :, :], self.best[:, :, :], self.total[:, :].unsqueeze(2).to_broadcast([P, PEER_H, TOPK]), ALU.subtract).then_inc(self.less, 1)

    def exp(self, act, t):
        act.wait_ge(self.less, t + 1)
        self.c.nc.scalar.activation(self.best[:, :, :], self.best[:, :, :], ACT.Exp).then_inc(self.exped, 1)

    def experts(self, step, dve, t, between=None):
        v = self.c.nc.vector
        wide = [P, PEER_H, TOPK, TOPK]
        flat = self.best_at[:, :, :].rearrange("p h s -> p (h s)")
        step.mark(v.tensor_copy(self.top_atf[:, :, :, :], self.of_tile(self.top_at, t)))
        step.mark(v.tensor_scalar(self.half_at[:, 0, :], flat, 4, None, ALU.logical_shift_right))
        step.mark(v.tensor_scalar(self.half_at[:, 1, :], flat, TOPK - 1, None, ALU.bitwise_and))
        step.wait()
        step(v.tensor_copy(self.half_f[:, :, :], self.half_at[:, :, :]))
        hit = self.hit
        for x in range(2):
            step(v.tensor_tensor(hit, self.half_f[:, x, :].unsqueeze(2).to_broadcast([P, SLOTS, TOPK]),
                                 self.iota[:, :].unsqueeze(1).to_broadcast([P, SLOTS, TOPK]), ALU.is_equal))
            hits = hit.rearrange("p (h s) k -> p h s k", h=PEER_H)
            step(v.tensor_tensor(hits, hits, self.top_atf[:, :, x, :].unsqueeze(2).to_broadcast(wide), ALU.mult))
            step(v.tensor_reduce(self.key_no[:, x, :], hit, AX.X, ALU.add))
            if between is not None:
                between(x)
        step(v.scalar_tensor_tensor(self.idx[:, :], self.key_no[:, 0, :], float(PEER_K), self.key_no[:, 1, :], ALU.mult, ALU.add))
        dve.wait_ge(self.exped, t + 1)
        step(v.tensor_reduce(self.total[:, :], self.best[:, :, :], AX.X, ALU.add))
        step(v.reciprocal(self.total[:, :], self.total[:, :]))
        gate = self.gates[:, :].rearrange("p (h s) -> p h s", h=PEER_H)
        step(v.tensor_tensor(gate, self.best[:, :, :], self.total[:, :].unsqueeze(2).to_broadcast([P, PEER_H, TOPK]), ALU.mult))
        dve.sem_inc(self.routed, 1)


def peer_gates(c, route, ring, h_row):
    nc = c.nc
    quads = P // QUAD
    per_block = TB // QUAD
    mine = lambda q: q % 4 == 3
    theirs = sum(not mine(q) for q in range(quads))
    AHEAD = 4
    sections = (12, 20, 28, quads)
    with c.stage() as ctx:
        keys = ctx.sbuf("keys", [P, PEER_K])
        slots = ctx.sbuf("slots", [P, 3, P])
        firsts = ctx.sbuf("firsts", [P, P, PEER_K])
        seconds = ctx.sbuf("seconds", [P, AHEAD * QUAD, PEER_K])
        spread = ring[:, :, :].rearrange("p s n -> p (s n)").rearrange("p (x i t) -> p x i t", x=2, t=TB)
        tables_in, turned, moved, first_made, first_mine, gated, second_made, summed, copied = (
            ctx.sem(n) for n in ("tables_in", "turned", "moved", "first_made", "first_mine", "gated", "second_made", "summed", "copied"))
        stored = [ctx.sem(f"stored{x}") for x in range(2)]
        row_turned, row_copied = ctx.sem("row_turned"), ctx.sem("row_copied")
        row_banks = (5, 6)
        with nc.Block() as block:

            @block.sync
            def _(sp):
                sp.dma_start(route.iota[:, :], c.ins["c_iota"]).then_inc(tables_in, 16)
                sp.dma_start(keys[:, :], c.ins["c_keys"]).then_inc(tables_in, 16)
                for x in range(2):
                    sp.sem_inc(stored[x], 16)
                with sp.Fori(0, DENSE) as n:
                    for b in range(P // TB):
                        hold(sp, copied, n * quads + (4 + (b + 1) * per_block), c.sp_tick)
                        sp.dma_start(route.gates_all[bass.ds(n * (P // TB) + b, 1), :, :].rearrange("a p n -> p (a n)"),
                                     spread[:, b % 2, :, :].rearrange("p i t -> p (i t)")).then_inc(stored[b % 2], 16)
                for x in range(2):
                    sp.wait_ge(stored[x], 16 + 16 * (BLOCKS // 2))

            @block.gpsimd
            def _(pool):
                pool.wait_ge(tables_in, 32)
                with pool.Fori(0, DENSE) as n:
                    hold(pool, moved, n + 1, c.pool_tick)
                    for q in range(quads):
                        if not mine(q):
                            for k in range(q * QUAD, (q + 1) * QUAD):
                                mark = nc.gpsimd.tensor_scalar(firsts[:, k, :], keys[:, :], slots[:, 0, k:k + 1], None, ALU.is_equal)
                            mark.then_inc(first_made, 1)

            @block.tensor
            def _(pe):
                pe.sem_inc(summed, AHEAD)
                pe.sem_inc(copied, 4)
                for x, bank in enumerate(row_banks):
                    for y in range(4):
                        for half in c.h:
                            mm = nc.tensor.matmul(c.ps[:, bank, y * P:(y + 1) * P], half[:, 4 * x + y, T - P:T], c.ident[:, :],
                                                  start=half is c.h.high, stop=half is c.h.low)
                    mm.then_inc(row_turned, 1)
                with pe.Fori(0, DENSE) as n:
                    pe.wait_ge(route.routed, n + 1)
                    pe.wait_ge(copied, n * quads + 4)
                    for x, table in enumerate((route.key_no[:, 0, :], route.key_no[:, 1, :], route.gates[:, :])):
                        tr = nc.tensor.transpose(c.ps[:, 7, x * P:(x + 1) * P], table, c.ident[:, :])
                    tr.then_inc(turned, 1)
                    for q in range(quads):
                        pe.wait_ge(gated, n * quads + (q + 1))
                        pe.wait_ge(second_made, n * quads + (q + 1))
                        pe.wait_ge(copied, n * quads + (q + 1))
                        for y in range(QUAD):
                            mm = nc.tensor.matmul(c.ps[:, q % 4, y * P:(y + 1) * P], seconds[:, q % AHEAD * QUAD + y, :], firsts[:, q * QUAD + y, :],
                                                  start=True, stop=True)
                        mm.then_inc(summed, 1)

            @block.scalar
            def _(act):
                for x, bank in enumerate(row_banks):
                    act.wait_ge(row_turned, x + 1)
                    nc.scalar.activation(h_row[:, x * T:(x + 1) * T], c.ps[:, bank, :], ACT.Copy).then_inc(row_copied, 1)
                act.wait_ge(row_copied, 2)
                route.exp(act, 0)
                with act.Fori(0, DENSE) as n:
                    act.wait_ge(turned, n + 1)
                    nc.scalar.activation(slots[:, :, :], c.ps[:, 7, 0:3 * P], ACT.Copy).then_inc(moved, 1)

                    def gate(q):
                        if mine(q):
                            act.wait_ge(first_mine, n * (quads - theirs) + (q // 4 + 1))
                        else:
                            act.wait_ge(first_made, n * theirs + (q - q // 4 + 1))
                        for k in range(q * QUAD, (q + 1) * QUAD):
                            put = nc.scalar.activation(firsts[:, k, :], firsts[:, k, :], ACT.Copy, scale=slots[:, 2, k:k + 1])
                        put.then_inc(gated, 1)

                    def copy(q):
                        block_no = q // per_block
                        act.wait_ge(summed, n * quads + (q + 1 + AHEAD))
                        if q % per_block == 0:
                            act.wait_ge(stored[block_no % 2], n * (16 * (P // TB // 2)) + 16 * (block_no // 2 + 1))
                        at = q % per_block * QUAD
                        nc.scalar.activation(spread[:, block_no % 2, :, at:at + QUAD].rearrange("p i t -> p t i"),
                                             c.ps[:, q % 4, :].rearrange("p (t i) -> p t i", t=QUAD), ACT.Copy).then_inc(copied, 1)

                    for q in range(quads + 2):
                        if q == sections[0]:
                            route.exp(act, n + 1)
                        if q < quads:
                            gate(q)
                        if q >= 2:
                            copy(q - 2)

            @block.vector
            def _(dve):
                dve.wait_ge(tables_in, 32)
                step = Chain(dve, c.dve_step)
                route.pairs(step, 0)
                dve.wait_ge(route.less, 1)
                route.experts(step, dve, 0)
                with dve.Fori(0, DENSE) as n:
                    step = Chain(dve, c.dve_step, n, Route.STEPS, c.dve_tick)

                    def mark(first, last):
                        spread_over = [P, QUAD, PEER_K]
                        for q in range(first, last):
                            tokens = slice(q * QUAD, (q + 1) * QUAD)
                            numbers = keys[:, :].unsqueeze(1).to_broadcast(spread_over)
                            if mine(q):
                                nc.vector.tensor_tensor(firsts[:, tokens, :], slots[:, 0, tokens].unsqueeze(2).to_broadcast(spread_over), numbers, ALU.is_equal
                                                        ).then_inc(first_mine, 1)
                            dve.wait_ge(summed, n * quads + (q + 1))
                            at = q % AHEAD * QUAD
                            nc.vector.tensor_tensor(seconds[:, at:at + QUAD, :], slots[:, 1, tokens].unsqueeze(2).to_broadcast(spread_over), numbers, ALU.is_equal
                                                    ).then_inc(second_made, 1)

                    route.pairs(step, n + 1)
                    hold(dve, turned, n + 1, c.dve_tick)
                    hold(dve, moved, n + 1, c.dve_tick)
                    mark(0, sections[0])
                    route.experts(step, dve, n + 1, lambda x: mark(sections[x], sections[x + 1]))
                    mark(sections[2], sections[3])
                    step.ends(DENSE)


def peer_experts(c, uT, uv, route, h_row, ring):
    nc = c.nc
    PER = 2 * QUAD
    TURNS = CHUNKS // PER
    HIDDEN = 2
    RAW = 4
    with c.stage() as ctx:
        u_halves, v_halves = (c.halves(ctx, n, [P, 2, D]) for n in "uv")
        hidden = ctx.sbuf("hidden", [P, HIDDEN, TD])
        weighed = c.halves(ctx, "weighed", [P, HIDDEN, TD])
        gates = ctx.sbuf("gates", [P, 2, BLOCKS, QUAD * TB])
        sums = ctx.sbuf("sums", [P, 2, D])
        idx_now = ctx.sbuf("idx_now", [P, 2, QUAD], U32)
        dots, acts, weights = (ctx.sbuf(n, [P, RING]) for n in ("dots", "acts", "weights"))
        u_raw, v_raw = c.w_ring, ctx.sbuf("v_raw", [P, RAW, D])
        u_in, v_in = ([ctx.sem(f"{n}_in{x}") for x in range(RAW)] for n in "uv")
        gates_in = [ctx.sem(f"gates_in{x}") for x in range(2)]
        u_high, u_low, v_high, v_low = (ctx.sem(n) for n in ("u_high", "u_low", "v_high", "v_low"))
        scored, gelued, gated, w_high, w_low, summed = (ctx.sem(n) for n in ("scored", "gelued", "gated", "w_high", "w_low", "summed"))
        gathered = [ctx.sem(f"gathered{s}") for s in range(RING)]
        idx_set, dotted, acted, scaled, used, zeroed, opened, out_read, last_sum = (
            ctx.sem(n) for n in ("idx_set", "dotted", "acted", "scaled", "used", "zeroed", "opened", "out_read", "last_sum"))

        def turns(eng, body):
            with eng.Fori(0, TURNS - 1) as r:
                for b in range(PER):
                    body(r, b, lambda k: True)
            for b in range(PER):
                body(TURNS - 1, b, lambda k: b + k < PER)

        with nc.Block() as block:

            @block.sync
            def _(sp):
                sp.sem_inc(u_low, RAW)
                sp.sem_inc(v_low, RAW)
                sp.sem_inc(gated, PER)
                with sp.Fori(0, TURNS) as r:
                    for b in range(PER):
                        x = b % RAW
                        chunk = bass.ds(r * PER + b, 1)
                        hold(sp, u_low, r * PER + (b + 1), c.sp_tick)
                        sp.dma_start(u_raw[:, x, :], uT[chunk, :, :].rearrange("a p n -> p (a n)")).then_inc(u_in[x], 16)
                        if b % QUAD == 0:
                            hold(sp, gated, r * PER + (b + QUAD), c.sp_tick)
                            sp.dma_start(gates[:, b // QUAD, :, :], route.gates_all[:, :, bass.ds(r * (PER * TB) + b * TB, QUAD * TB)].rearrange("b p n -> p b n")
                                         ).then_inc(gates_in[b // QUAD], 16)
                        hold(sp, v_low, r * PER + (b + 1), c.sp_tick)
                        sp.dma_start(v_raw[:, x, :], uv[bass.ds(r * (PER * P) + b * P, P), D:2 * D]).then_inc(v_in[x], 16)

            @block.gpsimd
            def _(pool):
                pool.sem_inc(used, 2)

                def gather(slot, index):
                    nc.gpsimd.indirect_dma_start(ring[:, slot, :], None, uv, bass.IndirectOffsetOnAxis(ap=index, axis=0)).then_inc(gathered[slot], 16)

                def u_rest(r, b):
                    x = b % 2
                    pool.wait_ge(u_high, r * PER + (b + 1))
                    low_half(nc.gpsimd, u_halves.low[:, x, :], u_raw[:, b % RAW, :], u_halves.high[:, x, :]).then_inc(u_low, 1)

                for n in range(RING - 1):
                    gather(n, route.idx[:, n:n + 1])
                u_rest(0, 0)
                u_rest(0, 1)

                def step(r, b, more):
                    if more(2):
                        u_rest(r, b + 2)
                    x = b % 2
                    pool.wait_ge(v_high, r * PER + (b + 1))
                    low_half(nc.gpsimd, v_halves.low[:, x, :], v_raw[:, b % RAW, :], v_halves.high[:, x, :]).then_inc(v_low, 1)
                    if more(RING - 1):
                        hold(pool, used, r * PER + (b + 2), c.pool_tick)
                        half, y = b // QUAD, b % QUAD
                        if y == 0:
                            n = sum(more(RING - 1 + k) for k in range(QUAD))
                            nc.gpsimd.tensor_copy(idx_now[:, half, 0:n], route.idx[:, bass.ds(r * PER + (b + RING - 1), n)]).then_inc(idx_set, 1)
                            hold(pool, idx_set, r * 2 + (half + 1), c.pool_tick)
                        gather((b + RING - 1) % RING, idx_now[:, half, y:y + 1])
                turns(pool, step)

            @block.tensor
            def _(pe):
                pe.sem_inc(scored, 2)
                pe.sem_inc(gelued, 2)
                pe.sem_inc(w_low, HIDDEN)
                pe.sem_inc(summed, HIDDEN)
                pe.wait_ge(zeroed, 1)
                for bank in range(2 * DENSE):
                    mm = nc.tensor.matmul(c.ps[:, bank, :], sums[:, 0, 0:P], sums[:, 0, 0:T], start=True, stop=True)
                mm.then_inc(opened, 1)

                def score(r, b):
                    x = b % 2
                    pe.wait_ge(u_low, r * PER + (b + 1 + RAW))
                    pe.wait_ge(gelued, r * PER + (b + 1))
                    for k in range(KD):
                        rows_k = slice(k * P, (k + 1) * P)
                        mm = product(nc, c.ps[:, 6 + x, 0:TD], u_halves.high[:, x, rows_k], u_halves.low[:, x, rows_k],
                                     c.h.high[:, k, 0:TD], c.h.low[:, k, 0:TD], start=(k == 0), stop=(k == KD - 1))
                    mm.then_inc(scored, 1)

                score(0, 0)
                score(0, 1)

                def step(r, b, more):
                    x, y = b % 2, b % HIDDEN
                    pe.wait_ge(w_low, r * PER + (b + 1 + HIDDEN))
                    pe.wait_ge(v_low, r * PER + (b + 1 + RAW))
                    for t in range(DENSE):
                        tokens = slice(t * P, (t + 1) * P)
                        for half in range(2):
                            cols = slice(half * T, (half + 1) * T)
                            mm = product(nc, c.ps[:, 2 * t + half, :], weighed.high[:, y, tokens], weighed.low[:, y, tokens],
                                         v_halves.high[:, x, cols], v_halves.low[:, x, cols], start=False, stop=True, skip_group_check=True)
                    mm.then_inc(summed, 1)
                    if more(2):
                        score(r, b + 2)
                turns(pe, step)

            @block.scalar
            def _(act):
                def u_split(r, b):
                    x = b % 2
                    act.wait_ge(u_in[b % RAW], r * (16 * (PER // RAW)) + (b // RAW + 1) * 16)
                    act.wait_ge(scored, r * PER + (b + 1))
                    high_half(nc, u_halves.high[:, x, :], u_raw[:, b % RAW, :]).then_inc(u_high, 1)

                u_split(0, 0)
                u_split(0, 1)

                def step(r, b, more):
                    x, y = b % 2, b % HIDDEN
                    act.wait_ge(scored, r * PER + (b + 3))
                    act.wait_ge(w_low, r * PER + (b + 1))
                    nc.scalar.activation(hidden[:, y, :], c.ps[:, 6 + x, 0:TD], ACT.Gelu_apprx_tanh).then_inc(gelued, 1)
                    if more(2):
                        u_split(r, b + 2)
                    act.wait_ge(gated, r * PER + (b + 1 + PER))
                    act.wait_ge(summed, r * PER + (b + 1))
                    high_half(nc, weighed.high[:, y, :], hidden[:, y, :]).then_inc(w_high, 1)
                    s = b % RING
                    act.wait_ge(dotted, r * PER + (b + 1))
                    nc.scalar.activation(acts[:, s:s + 1], dots[:, s:s + 1], ACT.Gelu_apprx_tanh).then_inc(acted, 1)
                    act.wait_ge(v_in[b % RAW], r * (16 * (PER // RAW)) + (b // RAW + 1) * 16)
                    act.wait_ge(summed, r * PER + (b + 1))
                    high_half(nc, v_halves.high[:, x, :], v_raw[:, b % RAW, :]).then_inc(v_high, 1)
                turns(act, step)
                act.wait_ge(summed, CHUNKS + HIDDEN)
                act.wait_ge(used, CHUNKS + 2)
                for t in range(DENSE):
                    nc.scalar.activation(ring[:, t, 0:D], c.ps[:, 2 * t:2 * t + 2, :].rearrange("p b n -> p (b n)"), ACT.Copy).then_inc(out_read, 1)
                act.wait_ge(out_read, DENSE)

            @block.vector
            def _(dve):
                v = nc.vector
                v.memset(sums[:, :, :], 0.0).then_inc(zeroed, 1)
                dve.wait_ge(zeroed, 1)
                dve.wait_ge(opened, 1)

                def step(r, b, more):
                    quad, y, s = b // QUAD, b % HIDDEN, b % RING
                    dve.wait_ge(gelued, r * PER + (b + 3))
                    dve.wait_ge(gates_in[quad], r * 16 + 16)
                    of = hidden[:, y, :].rearrange("p (b t) -> p b t", t=TB)
                    at = b % QUAD * TB
                    v.tensor_tensor(of, of, gates[:, quad, :, at:at + TB], ALU.mult).then_inc(gated, 1)
                    dve.wait_ge(gathered[s], r * (16 * (PER // RING)) + 16 * (b // RING + 1))
                    v.tensor_tensor_reduce(out=ring[:, s, 0:D], in0=ring[:, s, 0:D], in1=h_row[:, :], scale=1.0, scalar=0.0,
                                           op0=ALU.mult, op1=ALU.add, accum_out=dots[:, s:s + 1]).then_inc(dotted, 1)
                    dve.wait_ge(w_high, r * PER + (b + 1))
                    low_half(v, weighed.low[:, y, :], hidden[:, y, :], weighed.high[:, y, :]).then_inc(w_low, 1)
                    dve.wait_ge(acted, r * PER + (b + 1))
                    v.tensor_tensor(weights[:, s:s + 1], acts[:, s:s + 1], route.gates[:, bass.ds(r * PER + b, 1)], ALU.mult).then_inc(scaled, 1)
                    dve.wait_ge(scaled, r * PER + (b + 1))
                    dve.wait_ge(used, r * PER + (b + 1))
                    half = sums[:, b % 2, :]
                    v.scalar_tensor_tensor(half, ring[:, s, D:2 * D], weights[:, s:s + 1], half, ALU.mult, ALU.add).then_inc(used, 1)
                turns(dve, step)
                dve.wait_ge(used, CHUNKS + 2)
                v.tensor_tensor(ring[:, TT - 1, 0:D], sums[:, 0, :], sums[:, 1, :], ALU.add).then_inc(last_sum, 1)
                dve.wait_ge(last_sum, 1)


def tile_norm(c, ctx, buf, first, tiles, gain, factor, work):
    nc = c.nc
    gains = ctx.sbuf("gains", [P, 1])
    gain_in, squared, summed, inverted, rooted, normed = (ctx.sem(n) for n in ("gain_in", "squared", "summed", "inverted", "rooted", "normed"))

    def sp_part(sp):
        sp.dma_start(gains[:, :], gain.rearrange("(p a) -> p a", a=1)).then_inc(gain_in, 16)

    def act_first(act):
        for b in range(tiles):
            nc.scalar.activation(work[:, b, :], buf[:, first + b, :], ACT.Square).then_inc(squared, 1)

    def act_part(act):
        for b in range(tiles):
            act.wait_ge(summed, b + 1)
            nc.scalar.activation(work[:, b, :], c.ps[:, 4 + b, :], ACT.Sqrt, bias=c.eps[:, 0:1], scale=1.0 / P).then_inc(rooted, 1)
        act.wait_ge(rooted, tiles)

    def pe_part(pe):
        for b in range(tiles):
            pe.wait_ge(squared, b + 1)
            nc.tensor.matmul(c.ps[:, 4 + b, :], c.ones[:, :], work[:, b, :], start=True, stop=True).then_inc(summed, 1)

    def dve_part(dve):
        step = Chain(dve, c.dve_step)
        dve.wait_ge(gain_in, 16)
        step(nc.vector.tensor_scalar(gains[:, :], gains[:, :], factor, None, ALU.mult))
        for b in range(tiles):
            dve.wait_ge(rooted, b + 1)
            nc.vector.reciprocal(work[:, b, :], work[:, b, :]).then_inc(inverted, 1)
        for b in range(tiles):
            dve.wait_ge(inverted, b + 1)
            tile = buf[:, first + b, :]
            nc.vector.scalar_tensor_tensor(tile, tile, gains[:, 0:1], work[:, b, :], ALU.mult, ALU.mult).then_inc(normed, 1)
        dve.wait_ge(normed, tiles)
    return {"sp": sp_part, "act_first": act_first, "act": act_part, "pe": pe_part, "dve": dve_part}


def rope_tables(c, ctx, dims):
    nc = c.nc
    tables = {dim: (ctx.sbuf("swap", [P, P]), ctx.sbuf("cos", [P, T]), ctx.sbuf("sin", [P, T])) for dim in dims}
    tables_in = ctx.sem("tables_in")
    with nc.Block() as block:

        @block.sync
        def _(sp):
            for dim in dims:
                for table, name in zip(tables[dim], ("swap", "cos", "sin")):
                    sp.dma_start(table[:, :], c.ins[f"c_{name}{dim}"]).then_inc(tables_in, 16)
            sp.wait_ge(tables_in, 48 * len(dims))
    return tables


def repeated(w, col, n):
    view = w.rearrange("(k p) n -> p k n", p=P)
    return [((slice(None), slice(None), slice(r * n, (r + 1) * n)), view[:, :, col:col + n]) for r in range(P // n)]


LAM_INIT = 0.8 - 0.6
A_SCALE = (64 + 32) ** -0.5
EV = dict(nope=0, rope=512, ckv=768, krope=896, iq=928, ik=1440, iw=1504, qb=1512, kb=2024, vb=2536)


def even_weights(A):
    w_in = A["ev_w_in"][0]
    rope = columns(w_in, 1, 2, EV["rope"])

    def shared(i, b):
        return (repeated(w_in, EV["ik"], 64), repeated(w_in, EV["krope"], 32), rope.source(0, 0), rope.source(0, 1))[b]
    return dict(qk=columns(w_in, 2, 4, EV["qb"]), iq=columns(w_in, 1, 4, EV["iq"]), shared=Weights(1, 4, shared), nope=columns(w_in, 1, 4, EV["nope"]),
                out=columns(A["ev_w_out"][0], 2, 4))


def even_mix(c, A, w, ahead):
    w_in = A["ev_w_in"][0]
    with c.stage() as ctx:
        c.h = c.halves(ctx, "h", [P, KD, T])
        oT = ctx.sbuf("oT", [P, KD, T])
        rows = [ctx.sbuf(n, [P, TT, w]) for n, w in (("ckv", P), ("iw", DSA_H), ("vb", T))]
        w_rows = RowWeights(w_in, [(EV["vb"], T, 2, ACT.Copy), (EV["ckv"], P, 0, ACT.Copy), (EV["iw"], DSA_H, 1, ACT.Copy)], rows)
        with c.stage() as norming:
            project_rows(c, w_rows, ahead=w["qk"], norm=Norm(c, norming, A["norm_mix"][0], c.h))
        tables = rope_tables(c, ctx, (64, 32))
        differential(c, A, w, tables[64], rows[2], oT)
        selected(c, A, w, tables, rows[0], rows[1], rows[2], oT)
        project_add(c, w["out"], c.xT, c.h, oT, ahead)


def differential(c, A, w, rope64, vb, oT):
    nc = c.nc
    with c.stage() as ctx:
        qkT = ctx.sbuf("qkT", [P, 2 * DIFF_H, T])
        lam = ctx.sbuf("lam", [P, 4, 64])
        both = ctx.sbuf("both", [P, 2, 64])
        dots = ctx.sbuf("dots", [P, 2])
        minus = ctx.sbuf("minus", [P, 1])
        lam_in, dotted, exped = ctx.sem("lam_in"), ctx.sem("dotted"), ctx.sem("exped")

        def load_lambda(sp):
            sp.dma_start(lam[:, :, :], A["ev_lambda"][0].partition_broadcast(P)).then_inc(lam_in, 16)

        def minus_lambda(dve):
            step = Chain(dve, c.dve_step)
            dve.wait_ge(lam_in, 16)
            step(nc.vector.tensor_tensor(both[:, :, :], lam[:, 0::2, :], lam[:, 1::2, :], ALU.mult))
            nc.vector.tensor_reduce(dots[:, :], both[:, :, :], AX.X, ALU.add).then_inc(dotted, 1)
            dve.wait_ge(exped, 1)
            step(nc.vector.scalar_tensor_tensor(minus[:, :], dots[:, 1:2], -LAM_INIT, dots[:, 0:1], ALU.add, ALU.subtract))

        def exp_lambda(act):
            act.wait_ge(dotted, 1)
            nc.scalar.activation(dots[:, :], dots[:, :], ACT.Exp).then_inc(exped, 1)
        project_rope(c, w["qk"], [rope64] * 4, [1.0] * 4, lambda i, b: tile_of(qkT, i, 4, b), w["iq"],
                     {"sp": load_lambda, "dve": minus_lambda, "act": exp_lambda})

        def head_map(s, m):
            half = slice(64 * m, 64 * m + 64)
            return dict(q=qkT[half, s, :], k=lambda i: qkT[half, s + DIFF_H, :], v=lambda j: vb[:, j, s * P:(s + 1) * P], mask=None, slots=[],
                        gate=(lambda i, t: minus[:, 0:1]) if m else None, out=c.ps[:, 7, :], sum=c.ps[:, 7, :], first=m == 0, last=m == 1)
        attention(c, 1, [head_map(s, m) for s in range(DIFF_H) for m in range(2)], 64 ** -0.5, {},
                  {2 * s + 1: (lambda i, s=s: oT[:, s + 4, :]) for s in range(DIFF_H)})


def selected(c, A, w, tables, ckv, iw, score, oT):
    nc = c.nc
    with c.stage() as ctx:
        add_mask = ctx.sbuf("add_mask", [P, TT, T], BF16)
        keysT = ctx.sbuf("keysT", [P, T])
        krT = ctx.sbuf("krT", [P, 4, T])
        qrT = ctx.sbuf("qrT", [P, 2, T])
        q_lat = ctx.sbuf("q_lat", [P, DSA_H, T])
        w_uv = ctx.sbuf("w_uv", [P, DSA_H, 64])
        with c.stage() as inner:
            shared = inner.sbuf("shared", [P, 2, T])
            w_uk = inner.sbuf("w_uk", [P, 4, P])
            head_rows = inner.sbuf("head_rows", [P, 4])
            best = inner.sbuf("best", [P, TT, 8])
            left = {1: score[:, 0, 0:2 * P]}
            up_in, masked = inner.sem("up_in"), inner.sem("masked")
            with c.stage() as scoring:
                iqT = scoring.sbuf("iqT", [P, DSA_H // 2, T])
                project_rope(c, w["iq"], [tables[64]] * 4, [1.0] * 4, lambda i, b: iqT[:, b, :], w["shared"],
                             before=tile_norm(c, scoring, oT, 4, DIFF_H, A["ev_subln"][0], 1.0 - LAM_INIT, score))
                latents_before, latents_after = latents(c, scoring, A["ev_kv_gain"][0], ckv, keysT)
                project_rope(c, w["shared"], [tables[64], tables[32], tables[32], tables[32]], [1.0, 1.0, A_SCALE, A_SCALE],
                             lambda i, b: shared[:, b, :] if b < 2 else qrT[:, b - 2, :], w["nope"],
                             latents_before, latents_after)
                index_scores(c, iqT, shared[:, 0, :], iw, score, best, left)
            qnT = inner.sbuf("qnT", [P, 4, T])
            left.update({t: inner.sbuf(f"left{t}", [P, P * (t + 1)])[:, :] for t in range(2, TT)})
            made, copied, queries_made = inner.sem("made"), inner.sem("copied"), inner.sem("queries_made")

            def load_up(sp):
                sp.dma_start(w_uk[:, :, :], A["ev_w_uk"][0].rearrange("(j two) d c -> (two d) j c", two=2)).then_inc(up_in, 16)
                sp.dma_start(head_rows[:, :], c.ins["c_head_rows"]).then_inc(up_in, 16)
                sp.dma_start(w_uv[:, :, :], A["ev_w_uv"][0].rearrange("h c d -> c h d")).then_inc(up_in, 16)

            def up(pe):
                pe.wait_ge(up_in, 48)
                pe.wait_ge(queries_made, 1)
                for h in range(DSA_H):
                    r = slice(64 * (h % 2), 64 * (h % 2) + 64)
                    nc.tensor.matmul(c.ps[:, h, :], w_uk[r, h // 2, :], qnT[r, h // 2, :], start=True, stop=True).then_inc(made, 1)

            def scale_up(act):
                act.sem_inc(queries_made, 1)
                for h in range(DSA_H):
                    act.wait_ge(made, h + 1)
                    nc.scalar.activation(q_lat[:, h, :], c.ps[:, h, :], ACT.Copy, scale=A_SCALE).then_inc(copied, 1)
                act.wait_ge(copied, DSA_H)

            def choose(dve):
                dve.wait_ge(up_in, 48)
                for h in range(4):
                    nc.vector.tensor_scalar(krT[:, h, :], shared[:, 1, :], head_rows[:, h:h + 1], None, ALU.mult).then_inc(masked, 1)
                choose_keys(c, dve, score, best, left, add_mask)
                dve.wait_ge(masked, 4)
            project_copy(c, w["nope"], qnT, w["out"], before={"sp": load_up, "dve": choose}, after={"pe": up, "act": scale_up})
        outT = ctx.sbuf("outT", [P, DSA_H, T])

        def head(s):
            return dict(q=q_lat[:, s, :], k=lambda i: keysT, q2=qrT[:, s // 4, :], k2=lambda i: krT[:, s % 4, :], v=lambda j: ckv[:, j, :], slots=[],
                        mask=lambda t: add_mask[:, t, 0:P * (t + 1)], out=c.ps[:, 7, :], sum=c.ps[:, 7, :], first=True, last=True)
        attention(c, 1, [head(s) for s in range(DSA_H)], 1.0, {}, {s: (lambda i, s=s: outT[:, s, :]) for s in range(DSA_H)})
        with c.stage() as inner:
            made, copied = inner.sem("made"), inner.sem("copied")
            with nc.Block() as block:

                @block.tensor
                def _(pe):
                    for h in range(DSA_H):
                        r = slice(64 * (h % 2), 64 * (h % 2) + 64)
                        nc.tensor.matmul(c.ps[r, h // 2, :], w_uv[:, h, :], outT[:, h, :], start=True, stop=True).then_inc(made, 1)

                @block.scalar
                def _(act):
                    for j in range(DSA_H // 2):
                        act.wait_ge(made, 2 * j + 2)
                        nc.scalar.activation(oT[:, j, :], c.ps[:, j, :], ACT.Copy).then_inc(copied, 1)
                    act.wait_ge(copied, DSA_H // 2)


def latents(c, ctx, gain, ckv, keysT):
    nc = c.nc
    gains = ctx.sbuf("gains", [P, P])
    squares = ctx.sbuf("squares", [P, TT, P])
    rstd = ctx.sbuf("rstd", [P, TT])
    gain_in, squared, averaged, inverted, rooted, normed, banks_read, turned, copied = (
        ctx.sem(n) for n in ("gain_in", "squared", "averaged", "inverted", "rooted", "normed", "banks_read", "turned", "copied"))

    def sp_part(sp):
        sp.dma_start(gains[:, :], gain.partition_broadcast(P)).then_inc(gain_in, 16)

    def act_first(act):
        for t in range(TT):
            nc.scalar.activation(squares[:, t, :], ckv[:, t, :], ACT.Square, accum_out=rstd[:, t:t + 1]).then_inc(squared, 1)

    def act_part(act):
        act.wait_ge(inverted, 1)
        nc.scalar.activation(rstd[:, :], rstd[:, :], ACT.Sqrt).then_inc(rooted, 1)

    def dve_part(dve):
        dve.wait_ge(squared, TT)
        nc.vector.tensor_scalar(rstd[:, :], rstd[:, :], 1.0 / P, EPS, ALU.mult, ALU.add).then_inc(averaged, 1)
        dve.wait_ge(averaged, 1)
        nc.vector.reciprocal(rstd[:, :], rstd[:, :]).then_inc(inverted, 1)
        dve.wait_ge(rooted, 1)
        dve.wait_ge(gain_in, 16)
        for t in range(TT):
            nc.vector.scalar_tensor_tensor(ckv[:, t, :], ckv[:, t, :], rstd[:, t:t + 1], gains[:, :], ALU.mult, ALU.mult).then_inc(normed, 1)

    def turn(pe):
        pe.wait_ge(normed, TT)
        pe.wait_ge(banks_read, 1)
        for t in range(TT):
            tr = nc.tensor.transpose(c.ps[:, 0, t * P:(t + 1) * P], ckv[:, t, :], c.ident[:, :])
        tr.then_inc(turned, 1)

    def copy(act):
        act.sem_inc(banks_read, 1)
        act.wait_ge(turned, 1)
        nc.scalar.activation(keysT[:, :], c.ps[:, 0, :], ACT.Copy).then_inc(copied, 1)
        act.wait_ge(copied, 1)
    return {"sp": sp_part, "act_first": act_first, "act": act_part, "dve": dve_part}, {"pe": turn, "act": copy}


def index_scores(c, iqT, ikT, iw, score, best, left):
    assert DSA_SEL // 8 == 2 * DSA_H
    nc = c.nc
    IH = DSA_H
    width = [P * (t + 1) for t in range(TT)]
    with c.stage() as ctx:
        relus = ctx.sbuf("relus", [P, 4, T])
        weights = ctx.sbuf("weights", [P, TT, IH])
        made, rectified, summed = ctx.sem("made"), ctx.sem("rectified"), ctx.sem("summed")
        steps = [(t, h) for t in range(1, TT) for h in range(IH)]
        with nc.Block() as block:

            @block.tensor
            def _(pe):
                for n, (t, h) in enumerate(steps):
                    if n >= 4:
                        pe.wait_ge(rectified, n - 3)
                    r = slice(64 * (h % 2), 64 * (h % 2) + 64)
                    nc.tensor.matmul(c.ps[:, n % 4, 0:width[t]], iqT[r, h // 2, t * P:(t + 1) * P], ikT[r, 0:width[t]],
                                     start=True, stop=True).then_inc(made, 1)

            @block.scalar
            def _(act):
                for n, (t, h) in enumerate(steps):
                    act.wait_ge(made, n + 1)
                    if n >= 4:
                        act.wait_ge(summed, n - 3)
                    nc.scalar.activation(relus[:, n % 4, 0:width[t]], c.ps[:, n % 4, 0:width[t]], ACT.Relu, scale=64 ** -0.5).then_inc(rectified, 1)

            @block.vector
            def _(dve):
                v = nc.vector
                step = Chain(dve, c.dve_step)
                step(v.tensor_scalar(weights[:, :, :], iw[:, :, :], float(IH) ** -0.5, None, ALU.mult))
                for n, (t, h) in enumerate(steps):
                    dve.wait_ge(rectified, n + 1)
                    s, factor = score[:, t, 0:width[t]], weights[:, t, h:h + 1]
                    if h == 0:
                        v.tensor_scalar(s, relus[:, n % 4, 0:width[t]], factor, None, ALU.mult).then_inc(summed, 1)
                    else:
                        dve.wait_ge(summed, n)
                        v.scalar_tensor_tensor(s, relus[:, n % 4, 0:width[t]], factor, s, ALU.mult, ALU.add).then_inc(summed, 1)
                    if h == IH - 1:
                        dve.wait_ge(summed, n + 1)
                        last = score[:, t, t * P:(t + 1) * P]
                        step(v.tensor_tensor(last, last, c.causal[:, :], ALU.add))
                    if t >= 2:
                        take_best(c, step, score, best, left, [1], n - IH)


def take_best(c, step, score, best, left, tiles, n):
    v = c.nc.vector
    of = [(t, best[:, t, :], left[t], left[t] if n else score[:, t, 0:P * (t + 1)]) for t in tiles]
    for t, eight, after, before in of:
        step.mark(v.max(eight, before))
    step.wait()
    for t, eight, after, before in of:
        step.mark(v.match_replace(after, eight, before, LOWEST))
    step.wait()


def choose_keys(c, dve, score, best, left, add_mask):
    v = c.nc.vector
    step = Chain(dve, c.dve_step)
    for n in range(DSA_SEL // 8):
        take_best(c, step, score, best, left, range(2, TT), n)
    for t in range(1, TT):
        step.mark(v.tensor_tensor(left[t], left[t], score[:, t, 0:P * (t + 1)], ALU.is_equal))
    step.wait()
    for t in range(1, TT):
        step.mark(v.tensor_scalar(add_mask[:, t, 0:P * (t + 1)], left[t], NEG, None, ALU.mult))
    step.mark(v.tensor_copy(add_mask[:, 0, 0:P], c.mask_causal[:, :]))
    step.wait()


OD = dict(q=0, kc=1024, vc=1280, ks=1536, vs=1792, kw=2048, vw=2304, gates=2560)
GW = NSA_G * NSA_D


def odd_weights(A):
    w_in, w_out = A["od_w_in"][0], A["od_w_out"][0]
    view = w_in.rearrange("(k p) n -> p k n", p=P)

    def q_tile(i, j):
        return [((slice(None), slice(None), slice(64 * b, 64 * b + 64)),
                 view[:, :, bass.ds(i * 512 + (b * 256 + j * 64), 64)]) for b in range(2)]

    def k_tile(i, b):
        return [(ALL, view[:, :, bass.ds(i * 512 + (OD["kc"] + b * P), P)])]

    def out_tile(i, m):
        return [((slice(64 * b, 64 * b + 64), slice(4 * g, 4 * g + 4), slice(None)),
                 w_out[g * 512 + b * 256:g * 512 + b * 256 + 256, :].rearrange("(j d) n -> d j n", d=64)[:, :, bass.ds(i * 512 + m * P, P)])
                for b in range(2) for g in range(2)]
    return dict(q=Weights(2, 4, q_tile), k=Weights(3, 2, k_tile), vc=columns(w_in, 1, 2, OD["vc"]), out=Weights(2, 4, out_tile))


def odd_mix(c, A, w, ahead):
    nc = c.nc
    w_in = A["od_w_in"][0]
    with c.stage() as ctx:
        c.h = c.halves(ctx, "h", [P, KD, T])
        oT = ctx.sbuf("oT", [P, KD, T])
        with c.stage() as ctx:
            qT = ctx.sbuf("qT", [P, KD, T])
            kT = ctx.sbuf("kT", [P, 6, T])
            vs, vw = (ctx.sbuf(n, [P, TT, GW]) for n in ("vs", "vw"))
            gates = ctx.sbuf("gates", [P, TT, 3 * NSA_H])
            order = ctx.sbuf("order", [P, TT, 3, NSA_H])
            pcT = ctx.sbuf("pcT", [P, 4, T])
            vcr = ctx.sbuf("vcr", [P, 2, NSA_D])
            with c.stage() as inner:
                w_rows = RowWeights(w_in, [(OD["vs"], GW, "vs", ACT.Copy), (OD["vw"], GW, "vw", ACT.Copy), (OD["gates"], 3 * NSA_H, "gates", ACT.Sigmoid)],
                                    dict(vs=vs, vw=vw, gates=gates))
                with c.stage() as norming:
                    project_rows(c, w_rows, ahead=w["q"], norm=Norm(c, norming, A["norm_mix"][1], c.h))
                tables = [rope_tables(c, inner, (64,))[64]] * 4
                project_rope(c, w["q"], tables, [NSA_D ** -0.5] * 4, lambda i, b: tile_of(qT, i, 4, b), w["k"],
                             {"dve": lambda dve: reorder_gates(c, dve, gates, order)})
                project_rope(c, w["k"], tables, [1.0] * 4, lambda i, b: tile_of(kT, i, 2, b), w["vc"])
            compressed(c, A, w, qT, kT, order, pcT, vcr)
            nsa_attention(c, qT, kT, vs, vw, order, pcT, vcr, oT)
        project_add(c, w["out"], c.xT, c.h, oT, ahead)


def reorder_gates(c, dve, gates, order):
    step = Chain(dve, c.dve_step)
    for t in range(TT):
        for kind in range(3):
            for i in range(2):
                step.mark(c.nc.vector.tensor_copy(order[:, t, kind, 8 * i:8 * i + 8].rearrange("p (j b) -> p j b", b=2),
                                                  gates[:, t, 24 * i + kind:24 * i + 24:3].rearrange("p (b j) -> p j b", b=2)))
    step.wait()


def compressed(c, A, w, qT, kT, order, pcT, vcr):
    nc = c.nc
    NP = CMP_N + 1
    PAIRS_L = CMP_LEN // 2
    with c.stage() as ctx:
        w1 = ctx.sbuf("w1", [P, 2, PAIRS_L, P])
        w2 = ctx.sbuf("w2", [P, 2, NSA_D])
        pe_rows = ctx.sbuf("pe_rows", [PAIRS_L, 2, P])
        masks = ctx.sbuf("masks", [P, 2, TT, NP])
        cmp_in = ctx.sem("cmp_in")

        def load(sp):
            for z in range(2):
                sp.dma_start(w1[:, z, :, :], A["od_cmp_w1"][0, z].rearrange("(m f) e -> f m e", f=P)).then_inc(cmp_in, 16)
                sp.dma_start(pe_rows[:, z, :], A["od_cmp_pe"][0, z].rearrange("(m two) d -> m (two d)", two=2)).then_inc(cmp_in, 16)
            sp.dma_start(w2[:, :, :], A["od_cmp_w2"][0].rearrange("z e d -> e z d")).then_inc(cmp_in, 16)
            sp.dma_start(masks[:, 0, :, :], c.ins["c_cmp_add"]).then_inc(cmp_in, 16)
            sp.dma_start(masks[:, 1, :, :], c.ins["c_cmp_seen"]).then_inc(cmp_in, 16)
        n_in = 16 * 7
        vcT = ctx.sbuf("vcT", [P, 2, T])
        project_copy(c, w["vc"], vcT, w["out"], {"sp": load})
        tokens = ctx.sbuf("tokens", [P, 2, 2, 2, T])
        peT = ctx.sbuf("peT", [P, 2, PAIRS_L])
        pe_bias = ctx.sbuf("pe_bias", [P, 2])
        hidden = ctx.sbuf("hidden", [P, 2, 2, 2, NP])
        spread = ctx.sbuf("spread", [P, 2, 2, 2, NP])
        kcT = ctx.sbuf("kcT", [P, 2, NP])
        s = ctx.sbuf("s", [P, TT, NSA_H, NP])
        stat = ctx.sbuf("stat", [P, 2, TT, NSA_H])
        padded, made, biased, hid, spread_done, kv_made, kv_done, pe_turned, pe_moved = (
            ctx.sem(n) for n in ("padded", "made", "biased", "hid", "spread_done", "kv_made", "kv_done", "pe_turned", "pe_moved"))
        scored, less, exped, weighed, turned, copied = (ctx.sem(n) for n in ("scored", "less", "exped", "weighed", "turned", "copied"))
        tokens_in = [ctx.sem(f"tokens_in{z}") for z in range(2)]
        source = (kT, vcT)
        half = lambda b: slice(64 * b, 64 * b + 64)
        with nc.Block() as block:

            @block.sync
            def _(sp):
                for z in range(2):
                    for b in range(2):
                        for after in range(2):
                            sp.dma_start(tokens[half(after), z, b, :, 0:T - after], source[z][half(b), 0:2, after:T]).then_inc(tokens_in[z], 16)

            @block.gpsimd
            def _(pool):
                nc.gpsimd.memset(hidden[:, :, :, :, :], 0.0).then_inc(padded, 1)

            @block.tensor
            def _(pe):
                pe.wait_ge(cmp_in, n_in)
                for z in range(2):
                    tr = nc.tensor.transpose(c.ps[:, 1, z * PAIRS_L:(z + 1) * PAIRS_L], pe_rows[:, z, :], c.ident[0:PAIRS_L, 0:PAIRS_L])
                tr.then_inc(pe_turned, 1)
                pe.wait_ge(pe_moved, 1)
                for z in range(2):
                    for m in range(PAIRS_L):
                        mm = nc.tensor.matmul(c.ps[:, 2 * z, 0:1], w1[:, z, m, :], peT[:, z, m:m + 1], start=(m == 0), stop=(m == PAIRS_L - 1))
                    mm.then_inc(made, 1)
                    pe.wait_ge(tokens_in[z], 16 * 4)
                    for m in range(PAIRS_L):
                        block_tokens = tokens[:, z, :, :, 2 * m:2 * m + CMP_STRIDE * (CMP_N - 1) + 1:CMP_STRIDE]
                        mm = nc.tensor.matmul(c.ps[:, 4 + 2 * z, 0:4 * CMP_N].rearrange("p (b i n) -> p b i n", b=2, i=2), w1[:, z, m, :], block_tokens,
                                              start=(m == 0), stop=(m == PAIRS_L - 1))
                    mm.then_inc(made, 1)
                pe.wait_ge(hid, 4)
                for b in range(2):
                    mm = nc.tensor.matmul(c.ps[half(b), 0, 0:2 * NP], w2[:, 0, :], hidden[:, 0, b, :, :].rearrange("p i n -> p (i n)"), start=True, stop=True)
                mm.then_inc(kv_made, 1)
                pe.wait_ge(spread_done, 2)
                for i in range(2):
                    mm = nc.tensor.matmul(c.ps[:, 1, i * NSA_D:(i + 1) * NSA_D], spread[:, i, :, :, :].rearrange("p a b n -> p (a b n)"), w2[:, 1, :],
                                          start=True, stop=True)
                mm.then_inc(kv_made, 1)
                pe.wait_ge(kv_done, 2)
                for t in range(TT):
                    for h in range(NSA_H):
                        i, j, b = h // 8, (h // 2) % 4, h % 2
                        mm = nc.tensor.matmul(c.ps[:, 2 * t + b, (h // 2) * NP:(h // 2 + 1) * NP], qT[half(b), 4 * i + j, t * P:(t + 1) * P], kcT[half(b), i, :],
                                              start=True, stop=True)
                    mm.then_inc(scored, 1)
                for t in range(TT):
                    pe.wait_ge(weighed, t + 1)
                    for m in range(4):
                        tr = nc.tensor.transpose(c.ps[:, t, m * P:(m + 1) * P], s[:, t, 4 * m:4 * m + 4, :].rearrange("p h n -> p (h n)"), c.ident[:, :])
                    tr.then_inc(turned, 1)

            @block.scalar
            def _(act):
                act.wait_ge(pe_turned, 1)
                nc.scalar.activation(peT[:, :, :], c.ps[:, 1, 0:2 * PAIRS_L].rearrange("p (z m) -> p z m", z=2), ACT.Copy).then_inc(pe_moved, 1)
                act.wait_ge(padded, 1)
                for z in range(2):
                    act.wait_ge(made, 2 * z + 1)
                    nc.scalar.activation(pe_bias[:, z:z + 1], c.ps[:, 2 * z, 0:1], ACT.Copy).then_inc(biased, 1)
                    act.wait_ge(biased, z + 1)
                    for b in range(2):
                        act.wait_ge(made, 2 * z + 2)
                        nc.scalar.activation(hidden[:, z, b, :, 0:CMP_N], c.ps[:, 4 + 2 * z, 2 * b * CMP_N:2 * (b + 1) * CMP_N].rearrange("p (i n) -> p i n", i=2),
                                             ACT.Gelu_apprx_tanh, bias=pe_bias[:, z:z + 1]).then_inc(hid, 1)
                act.wait_ge(kv_made, 1)
                nc.scalar.activation(kcT[:, :, :], c.ps[:, 0, 0:2 * NP].rearrange("p (i n) -> p i n", i=2), ACT.Copy).then_inc(kv_done, 1)
                act.wait_ge(kv_made, 2)
                nc.scalar.activation(vcr[:, :, :], c.ps[:, 1, 0:P].rearrange("p (i d) -> p i d", i=2), ACT.Copy).then_inc(kv_done, 1)
                for t in range(TT):
                    act.wait_ge(less, t + 1)
                    nc.scalar.activation(s[:, t, :, :], s[:, t, :, :], ACT.Exp).then_inc(exped, 1)
                for t in range(TT):
                    act.wait_ge(turned, t + 1)
                    nc.scalar.activation(pcT[:, :, t * P:(t + 1) * P], c.ps[:, t, :].rearrange("p (m q) -> p m q", m=4), ACT.Copy).then_inc(copied, 1)
                act.wait_ge(copied, TT)

            @block.vector
            def _(dve):
                v = nc.vector
                step = Chain(dve, c.dve_step)
                dve.wait_ge(hid, 4)
                for a in range(2):
                    v.tensor_copy(spread[:, :, a, :, :], hidden[:, 1, :, :, :].rearrange("p b i n -> p i b n")).then_inc(spread_done, 1)
                full = [P, NSA_H, NP]
                for t in range(TT):
                    dve.wait_ge(scored, t + 1)
                    st, top, den = s[:, t, :, :], stat[:, 0, t, :], stat[:, 1, t, :]
                    for b in range(2):
                        step.mark(v.tensor_tensor(s[:, t, b::2, :], c.ps[:, 2 * t + b, 0:NSA_H // 2 * NP].rearrange("p (h n) -> p h n", n=NP),
                                                  masks[:, 0, t, :].unsqueeze(1).to_broadcast([P, NSA_H // 2, NP]), ALU.add))
                    step.wait()
                    step(v.tensor_reduce(top, st, AX.X, ALU.max))
                    v.tensor_tensor(st, st, top.unsqueeze(2).to_broadcast(full), ALU.subtract).then_inc(less, 1)
                for t in range(TT):
                    dve.wait_ge(exped, t + 1)
                    st, zero, den = s[:, t, :, :], stat[:, 0, t, :], stat[:, 1, t, :]
                    step(v.tensor_tensor(st, st, masks[:, 1, t, :].unsqueeze(1).to_broadcast(full), ALU.mult))
                    step(v.tensor_reduce(den, st, AX.X, ALU.add))
                    step(v.tensor_scalar(zero, den, 0.0, None, ALU.is_equal))
                    step(v.tensor_tensor(den, den, zero, ALU.add))
                    step(v.reciprocal(den, den))
                    step(v.tensor_tensor(den, den, order[:, t, 0, :], ALU.mult))
                    v.tensor_tensor(st, st, den.unsqueeze(2).to_broadcast(full), ALU.mult).then_inc(weighed, 1)


def nsa_attention(c, qT, kT, vs, vw, order, pcT, vcr, oT):
    TILES = NSA_HPG
    with c.stage() as ctx:
        q = [ctx.sbuf(f"q{j}", [P, T]) for j in range(TILES)]
        k = [ctx.sbuf(n, [P, T]) for n in ("k_sel", "k_win")]
        v = [ctx.sbuf(n, [P, TT, P]) for n in ("v_sel", "v_win")]
        pc = [ctx.sbuf(f"pc{m}", [P, T]) for m in range(TILES // 2)]
        vc = ctx.sbuf("vc", [P, NSA_D])

        def values(i):
            return [(vc[:, :], vcr[:, i, :])]
        staging = {f"q{j}": (lambda i, j=j: [(q[j][:, :], tile_of(qT, i, TILES, j))]) for j in range(TILES)}
        staging.update({f"pc{m}": (lambda i, m=m: [(pc[m][:, :], tile_of(pcT, i, 2, m))] + (values(i) if m == 0 else [])) for m in range(2)})
        for kind, buf in enumerate((vs, vw)):
            staging[f"kv{kind}"] = lambda i, kind=kind, buf=buf: [(k[kind][:, :], kT[:, i + (2 + 2 * kind), :]),
                                                                  (v[kind][:, :, :], buf[:, :, bass.ds(i * P, P)])]

        def head(j, b, kind):
            half = slice(64 * b, 64 * b + 64)
            unit = dict(q=q[j][half, :], k=lambda i: k[kind][half, :], v=lambda x: v[kind][:, x, half], mask=None,
                        slots=[f"q{j}", f"kv{kind}"] + ["pc0", f"pc{j // 2}"][:1 + j // 2] * (kind == 0),
                        gate=lambda i, t: order[:, t, 1 + kind, bass.ds(i * (2 * TILES) + (2 * j + b), 1)],
                        out=c.ps[half, 7, :], sum=c.ps[:, 7, :], first=kind == 0, last=kind == 1)
            if kind == 0:
                rows = slice(32 * (2 * (j % 2) + b), 32 * (2 * (j % 2) + b) + 32)
                unit["add"], unit["add_to"] = vc[rows, :], lambda i: pc[j // 2][rows, :]
            return unit
        attention(c, KD // TILES, [head(j, b, kind) for j in range(TILES) for b in range(2) for kind in range(2)], 1.0, staging,
                  {4 * j + 3: (lambda i, j=j: tile_of(oT, i, TILES, j)) for j in range(TILES)})


FIRST = ("mix_norm_g w_in ssm_a_re ssm_a_im ssm_log_step ssm_b_re ssm_b_im ssm_c_re ssm_c_im ssm_d ssm_w_glu "
         "fox_forget_bias q_norm_g k_norm_g w_out ffn_norm_g peer_w_query peer_sub_keys").split()
SECOND = ("norm_mix norm_ffn norm_final ev_w_in ev_kv_gain ev_w_uk ev_w_uv ev_lambda ev_subln ev_w_out "
          "od_w_in od_cmp_pe od_cmp_w1 od_cmp_w2 od_w_out ffn_w_gate ffn_w_up ffn_w_down").split()


def constants():
    row, token = np.arange(P), np.arange(T)
    made = {
        "c_ident": np.eye(P),
        "c_causal": np.where(row[None] <= row[:, None], 0.0, NEG),
        "c_minus_tri": np.where(row[:, None] <= token[None], -1.0, 0.0),
        "c_iota": np.tile(np.arange(TOPK), (P, 1)),
        "c_keys": np.tile(np.arange(PEER_K), (P, 1)),
        "c_head_rows": row[:, None] // 32 == np.arange(4)[None],
    }
    for dim in (32, 64):
        rates = (10000.0 ** (-np.arange(0, dim, 2) / dim)).astype(np.float32)
        angles = (token.astype(np.float32)[:, None] * rates[None]).T
        made[f"c_cos{dim}"] = np.tile(np.cos(angles), (P // dim * 2, 1))
        made[f"c_sin{dim}"] = np.tile(np.sin(angles), (P // dim * 2, 1))
        swap = np.zeros((P, P))
        for r in range(P):
            second = r % dim >= dim // 2
            swap[r - dim // 2 if second else r + dim // 2, r] = 1.0 if second else -1.0
        made[f"c_swap{dim}"] = swap
    block = np.arange(CMP_N + 1)
    query = np.arange(TT)[None, :, None] * P + row[:, None, None]
    seen = (block * CMP_STRIDE + CMP_LEN - 1 <= query) & (block < CMP_N)
    made["c_cmp_add"], made["c_cmp_seen"] = np.where(seen, 0.0, NEG), seen
    return {name: table.astype(np.float32) for name, table in made.items()}


def build(nc, ins, out):
    with ExitStack() as ctx:
        c = Core(nc, ctx, ins)
        w_query = columns(ins["peer_w_query"][0], PEER_H // 2, 4)
        w_even, w_odd = even_weights(ins), odd_weights(ins)
        w_ffn = [ffn_weights(ins["ffn_w_gate"][n], ins["ffn_w_up"][n], ins["ffn_w_down"][n]) for n in range(2)]
        load_consts(c)
        first_mix(c, ins, w_query)
        peer(c, ins, w_query)
        even_mix(c, ins, w_even, w_ffn[0][0])
        ffn(c, ins["norm_ffn"][0], w_ffn[0])
        odd_mix(c, ins, w_odd, w_ffn[1][0])
        ffn(c, ins["norm_ffn"][1], w_ffn[1])
        store_normed(c, ins["norm_final"], out)


def kernel(**inputs):
    import concourse.bacc as bacc
    from concourse.bass_utils import run_bass_kernel_spmd

    arrays = {"x": inputs["x"]}
    arrays.update({name: inputs[name] for name in FIRST})
    arrays.update({name: inputs[name + "_2"] for name in SECOND})
    arrays["peer_uv"] = np.concatenate([np.asarray(inputs["peer_u"])[0], np.asarray(inputs["peer_v"])[0]], axis=1)
    arrays["peer_uT"] = np.asarray(inputs["peer_u"])[0].reshape(CHUNKS, P, KD, P).transpose(0, 3, 2, 1).reshape(CHUNKS, P, D)
    arrays.update(constants())
    arrays = {name: np.ascontiguousarray(a) for name, a in arrays.items()}
    nc = bacc.Bacc("TRN2", target_bir_lowering=False, num_devices=1)
    ins = {name: nc.dram_tensor(f"in_{name}_dram", a.shape, mybir.dt.from_np(a.dtype), kind="ExternalInput").ap() for name, a in arrays.items()}
    out = nc.dram_tensor("out_0_dram", (1, T, D), F32, kind="ExternalOutput").ap()
    build(nc, ins, out)
    result = run_bass_kernel_spmd(nc, [{f"in_{name}_dram": a for name, a in arrays.items()}], core_ids=[0])
    return result.results[0]["out_0_dram"]
```
